# Optimizing a Trainium2 kernel written in Bass

```python
import math
import jax, jax.numpy as jnp
from jax import lax
import numpy as np

D_MODEL = 1024
BATCH = 1
SEQ = 1024
DEPTH = 1
DEC_BATCH = 8
DEC_SEQ = 1
PAST_LEN = 8192
PAGE_SIZE = 128

D_MIX = 2 * D_MODEL
SSD_WIDTH = D_MIX // 2
SSD_HEADDIM = 64
SSD_HEADS = SSD_WIDTH // SSD_HEADDIM
SSD_GROUPS = 2
SSD_STATE = 128
CONV_WIDTH = 4
CONV_DIM = SSD_WIDTH + 2 * SSD_GROUPS * SSD_STATE
SSD_CHUNK = 128
GLA_WIDTH = D_MIX - SSD_WIDTH
GLA_HEADS = 4
GLA_DV = GLA_WIDTH // GLA_HEADS
GLA_DK = GLA_DV // 2
GLA_KEY_WIDTH = GLA_HEADS * GLA_DK
GLA_GATE_RANK = 16
GLA_GATE_TAU = 16.0
GLA_CHUNK = 64
IN_SIZES = (SSD_WIDTH, CONV_DIM, SSD_HEADS, GLA_KEY_WIDTH, GLA_KEY_WIDTH, GLA_WIDTH, GLA_WIDTH, GLA_GATE_RANK)
D_IN_PROJ = sum(IN_SIZES)
PEER_HEADS = 8
PEER_NKEYS = 128
PEER_EXPERTS = PEER_NKEYS * PEER_NKEYS
PEER_TOPK = 16
PEER_DQ = 256
PEER_TOKEN_BLOCK = 128
N_MOD = 6
EPS = 1e-6

kernel_name = 'hymba_ssd_gla_peer_adaln_step'

def _rms_f32(x):
    return x * lax.rsqrt(jnp.mean(x * x, axis=-1, keepdims=True) + EPS)

def rmsnorm(x, w):
    return _rms_f32(x.astype(jnp.float32)).astype(x.dtype) * w

def _chunk_len(L, c):
    q = min(c, L)
    return q if L % q == 0 else L

def causal_conv(xbc, buf, w, b):
    xp = jnp.concatenate([buf.astype(xbc.dtype), xbc], axis=1)
    out = lax.conv_general_dilated(xp, w.astype(xbc.dtype)[:, None, :], window_strides=(1,), padding='VALID',
                                   dimension_numbers=('NWC', 'WIO', 'NWC'), feature_group_count=xbc.shape[-1])
    return out + b, xp[:, -(CONV_WIDTH - 1):]

def ssd_scan(x, dt, A, B, C, h0):
    b, L, H, P = x.shape
    G, N = B.shape[2], B.shape[3]
    r = H // G
    Q = _chunk_len(L, SSD_CHUNK)
    nc = L // Q
    xc = x.reshape(b, nc, Q, G, r, P).transpose(1, 0, 2, 3, 4, 5)
    dtc = dt.reshape(b, nc, Q, G, r).transpose(1, 0, 2, 3, 4)
    Bc = B.reshape(b, nc, Q, G, N).transpose(1, 0, 2, 3, 4)
    Cc = C.reshape(b, nc, Q, G, N).transpose(1, 0, 2, 3, 4)
    Ar = A.reshape(G, r)
    causal = jnp.tril(jnp.ones((Q, Q), bool))[None, :, :, None, None]

    def step(h, inp):
        xq, dtq, Bq, Cq = inp
        cum = jnp.cumsum(dtq * Ar, axis=1)
        seg = cum[:, :, None] - cum[:, None, :]
        decay = jnp.exp(jnp.where(causal, seg, -jnp.inf))
        cb = jnp.einsum('btgn,bsgn->btsg', Cq, Bq)
        xdt = xq * dtq[..., None]
        y_intra = jnp.einsum('btsg,btsgr,bsgrp->btgrp', cb, decay, xdt)
        y_inter = jnp.einsum('btgn,bgrpn->btgrp', Cq, h) * jnp.exp(cum)[..., None]
        to_end = jnp.exp(cum[:, -1:] - cum)
        h_new = h * jnp.exp(cum[:, -1])[..., None, None] + jnp.einsum('bsgn,bsgr,bsgrp->bgrpn', Bq, to_end, xdt)
        return h_new, y_intra + y_inter

    hT, ys = lax.scan(step, h0.reshape(b, G, r, P, N), (xc, dtc, Bc, Cc))
    y = ys.transpose(1, 0, 2, 3, 4, 5).reshape(b, L, H, P)
    return y, hT.reshape(b, H, P, N)

def gla_scan(q, k, v, log_a, S0):
    b, L, H, dk = q.shape
    dv = v.shape[-1]
    Q = _chunk_len(L, GLA_CHUNK)
    nc = L // Q
    resh = lambda t: t.reshape(b, nc, Q, H, t.shape[-1]).transpose(1, 0, 2, 3, 4)
    causal = jnp.tril(jnp.ones((Q, Q), bool))[None, :, :, None, None]

    def step(S, inp):
        qq, kk, vv, la = inp
        cum = jnp.cumsum(la, axis=1)
        seg = cum[:, :, None] - cum[:, None, :]
        w = jnp.exp(jnp.where(causal, seg, -jnp.inf))
        att = jnp.einsum('bthd,bshd,btshd->bths', qq, kk, w)
        o_intra = jnp.einsum('bths,bshv->bthv', att, vv)
        o_inter = jnp.einsum('bthd,bhdv->bthv', qq * jnp.exp(cum), S)
        k_end = kk * jnp.exp(cum[:, -1:] - cum)
        S_new = S * jnp.exp(cum[:, -1])[..., None] + jnp.einsum('bshd,bshv->bhdv', k_end, vv)
        return S_new, o_intra + o_inter

    ST, os_ = lax.scan(step, S0, (resh(q), resh(k), resh(v), resh(log_a)))
    return os_.transpose(1, 0, 2, 3, 4).reshape(b, L, H, dv), ST

def mixer(h, conv_buf, ssm_state, gla_state, w_in, w_conv, b_conv, dt_bias, a_log, d_skip, ssd_norm,
          w_gate_up, b_gate, gla_norm, w_out):
    f32 = jnp.float32
    b, L, _ = h.shape
    proj = h @ w_in
    z, xbc, dt_raw, q, k, v, g_out, gate_lr = jnp.split(proj, list(np.cumsum(IN_SIZES)[:-1]), axis=-1)
    xbc, new_buf = causal_conv(xbc, conv_buf, w_conv, b_conv)
    xbc = jax.nn.silu(xbc).astype(f32)
    xs, Bm, Cm = jnp.split(xbc, [SSD_WIDTH, SSD_WIDTH + SSD_GROUPS * SSD_STATE], axis=-1)
    xs = xs.reshape(b, L, SSD_HEADS, SSD_HEADDIM)
    dt = jax.nn.softplus(dt_raw.astype(f32) + dt_bias.astype(f32))
    A = -jnp.exp(a_log.astype(f32))
    y, ssm_new = ssd_scan(xs, dt, A, Bm.reshape(b, L, SSD_GROUPS, SSD_STATE),
                          Cm.reshape(b, L, SSD_GROUPS, SSD_STATE), ssm_state.astype(f32))
    y = (y + d_skip.astype(f32)[:, None] * xs).reshape(b, L, SSD_WIDTH) * jax.nn.silu(z.astype(f32))
    y = _rms_f32(y.reshape(b, L, SSD_GROUPS, SSD_WIDTH // SSD_GROUPS)).reshape(b, L, SSD_WIDTH) * ssd_norm.astype(f32)
    log_a = jax.nn.log_sigmoid((gate_lr @ w_gate_up + b_gate).astype(f32)) / GLA_GATE_TAU
    qh = q.astype(f32).reshape(b, L, GLA_HEADS, GLA_DK) * (GLA_DK ** -0.5)
    kh = k.astype(f32).reshape(b, L, GLA_HEADS, GLA_DK)
    vh = v.astype(f32).reshape(b, L, GLA_HEADS, GLA_DV)
    o, gla_new = gla_scan(qh, kh, vh, log_a.reshape(b, L, GLA_HEADS, GLA_DK), gla_state.astype(f32))
    o = (_rms_f32(o) * gla_norm.astype(f32)).reshape(b, L, GLA_WIDTH) * jax.nn.silu(g_out.astype(f32))
    out = jnp.concatenate([y, o], axis=-1).astype(h.dtype) @ w_out
    return out, new_buf, ssm_new, gla_new

def peer(h, w_query, sub_keys1, sub_keys2, expert_down, expert_up):
    f32 = jnp.float32
    b, L, D = h.shape
    T = b * L
    pad = (-T) % PEER_TOKEN_BLOCK
    blocks = jnp.pad(h.reshape(T, D), ((0, pad), (0, 0))).reshape(-1, PEER_TOKEN_BLOCK, D)

    def block_fn(xb):
        qd = (xb @ w_query).astype(f32).reshape(-1, PEER_HEADS, 2, PEER_DQ // 2)
        s1 = jnp.einsum('thd,hkd->thk', qd[:, :, 0], sub_keys1.astype(f32))
        s2 = jnp.einsum('thd,hkd->thk', qd[:, :, 1], sub_keys2.astype(f32))
        v1, i1 = lax.top_k(s1, PEER_TOPK)
        v2, i2 = lax.top_k(s2, PEER_TOPK)
        n = xb.shape[0]
        cand = (v1[..., :, None] + v2[..., None, :]).reshape(n, PEER_HEADS, PEER_TOPK * PEER_TOPK)
        cand_idx = (i1[..., :, None] * PEER_NKEYS + i2[..., None, :]).reshape(n, PEER_HEADS, PEER_TOPK * PEER_TOPK)
        top_s, pos = lax.top_k(cand, PEER_TOPK)
        idx = jnp.take_along_axis(cand_idx, pos, axis=-1)
        g = jax.nn.softmax(top_s, axis=-1)
        u = expert_down[idx]
        act = jax.nn.gelu(jnp.einsum('thkd,td->thk', u, xb).astype(f32), approximate=False)
        return jnp.einsum('thk,thkd->td', (g * act).astype(xb.dtype), expert_up[idx])

    out = lax.map(block_fn, blocks).reshape(-1, D)[:T]
    return out.reshape(b, L, D)

def trunk(x, c, conv0, ssm0, gla0, w_mod, b_mod, norm_mix, norm_ffn, w_in, w_conv, b_conv, dt_bias, a_log,
          d_skip, ssd_norm, w_gate_up, b_gate, gla_norm, w_out, w_query, sub_keys1, sub_keys2, expert_down,
          expert_up, norm_final):
    convs, ssms, glas = [], [], []
    for l in range(DEPTH):
        mod = (jax.nn.silu(c) @ w_mod[l] + b_mod[l]).reshape(-1, N_MOD, 1, D_MODEL)
        sh1, sc1, g1, sh2, sc2, g2 = (mod[:, i] for i in range(N_MOD))
        h = rmsnorm(x, norm_mix[l]) * (1 + sc1) + sh1
        y, cb, sb, gb = mixer(h, conv0[l], ssm0[l], gla0[l], w_in[l], w_conv[l], b_conv[l], dt_bias[l], a_log[l],
                              d_skip[l], ssd_norm[l], w_gate_up[l], b_gate[l], gla_norm[l], w_out[l])
        x = x + g1 * y
        h = rmsnorm(x, norm_ffn[l]) * (1 + sc2) + sh2
        x = x + g2 * peer(h, w_query[l], sub_keys1[l], sub_keys2[l], expert_down[l], expert_up[l])
        convs.append(cb)
        ssms.append(sb)
        glas.append(gb)
    return rmsnorm(x, norm_final), jnp.stack(convs), jnp.stack(ssms), jnp.stack(glas)

def setup_inputs(seed: int = 0) -> dict:
    key = jax.random.key(seed)
    ks = jax.random.split(key, 32)
    nrm = lambda k, s, sc: jax.random.normal(k, s, jnp.float32) * sc
    Dp = DEPTH
    dt0 = jnp.exp(jax.random.uniform(ks[10], (Dp, SSD_HEADS), jnp.float32, math.log(1e-3), math.log(1e-1)))
    return {
        'x_prompt': nrm(ks[0], (BATCH, SEQ, D_MODEL), 1.0),
        'x_sample': nrm(ks[1], (DEC_BATCH, DEC_SEQ, D_MODEL), 1.0),
        'state_conv': nrm(ks[2], (Dp, DEC_BATCH, CONV_WIDTH - 1, CONV_DIM), 1.0),
        'state_ssm': nrm(ks[3], (Dp, DEC_BATCH, SSD_HEADS, SSD_HEADDIM, SSD_STATE), 0.1),
        'state_gla': nrm(ks[4], (Dp, DEC_BATCH, GLA_HEADS, GLA_DK, GLA_DV), 0.1),
        'c_prompt': nrm(ks[5], (BATCH, D_MODEL), 1.0),
        'c_sample': nrm(ks[6], (DEC_BATCH, D_MODEL), 1.0),
        'w_mod': nrm(ks[7], (Dp, D_MODEL, N_MOD * D_MODEL), 0.5 * D_MODEL ** -0.5),
        'b_mod': nrm(ks[8], (Dp, N_MOD * D_MODEL), 0.02),
        'norm_mix': 1.0 + nrm(ks[9], (Dp, D_MODEL), 0.1),
        'norm_ffn': 1.0 + nrm(ks[11], (Dp, D_MODEL), 0.1),
        'w_in': nrm(ks[12], (Dp, D_MODEL, D_IN_PROJ), D_MODEL ** -0.5),
        'w_conv': nrm(ks[13], (Dp, CONV_WIDTH, CONV_DIM), CONV_WIDTH ** -0.5),
        'b_conv': nrm(ks[14], (Dp, CONV_DIM), 0.02),
        'dt_bias': dt0 + jnp.log(-jnp.expm1(-dt0)),
        'a_log': jnp.log(jax.random.uniform(ks[15], (Dp, SSD_HEADS), jnp.float32, 1.0, 16.0)),
        'd_skip': 1.0 + nrm(ks[16], (Dp, SSD_HEADS), 0.1),
        'ssd_norm': 1.0 + nrm(ks[17], (Dp, SSD_WIDTH), 0.1),
        'w_gate_up': nrm(ks[18], (Dp, GLA_GATE_RANK, GLA_KEY_WIDTH), GLA_GATE_RANK ** -0.5),
        'b_gate': nrm(ks[19], (Dp, GLA_KEY_WIDTH), 0.02),
        'gla_norm': 1.0 + nrm(ks[20], (Dp, GLA_DV), 0.1),
        'w_out': nrm(ks[21], (Dp, D_MIX, D_MODEL), D_MIX ** -0.5),
        'w_query': nrm(ks[22], (Dp, D_MODEL, PEER_HEADS * PEER_DQ), D_MODEL ** -0.5),
        'sub_keys1': nrm(ks[23], (Dp, PEER_HEADS, PEER_NKEYS, PEER_DQ // 2), (PEER_DQ // 2) ** -0.5),
        'sub_keys2': nrm(ks[24], (Dp, PEER_HEADS, PEER_NKEYS, PEER_DQ // 2), (PEER_DQ // 2) ** -0.5),
        'expert_down': nrm(ks[25], (Dp, PEER_EXPERTS, D_MODEL), D_MODEL ** -0.5),
        'expert_up': nrm(ks[26], (Dp, PEER_EXPERTS, D_MODEL), 0.5),
        'norm_final': 1.0 + nrm(ks[27], (D_MODEL,), 0.1),
    }

def reference(x_prompt, x_sample, state_conv, state_ssm, state_gla, c_prompt, c_sample, w_mod, b_mod, norm_mix,
              norm_ffn, w_in, w_conv, b_conv, dt_bias, a_log, d_skip, ssd_norm, w_gate_up, b_gate, gla_norm, w_out,
              w_query, sub_keys1, sub_keys2, expert_down, expert_up, norm_final):
    weights = (w_mod, b_mod, norm_mix, norm_ffn, w_in, w_conv, b_conv, dt_bias, a_log, d_skip, ssd_norm,
               w_gate_up, b_gate, gla_norm, w_out, w_query, sub_keys1, sub_keys2, expert_down, expert_up, norm_final)
    bp = x_prompt.shape[0]
    conv0 = jnp.zeros((DEPTH, bp, CONV_WIDTH - 1, CONV_DIM), x_prompt.dtype)
    ssm0 = jnp.zeros((DEPTH, bp, SSD_HEADS, SSD_HEADDIM, SSD_STATE), jnp.float32)
    gla0 = jnp.zeros((DEPTH, bp, GLA_HEADS, GLA_DK, GLA_DV), jnp.float32)
    y_prompt, conv_p, ssm_p, gla_p = trunk(x_prompt, c_prompt, conv0, ssm0, gla0, *weights)
    y_sample, conv_s, ssm_s, gla_s = trunk(x_sample, c_sample, state_conv, state_ssm, state_gla, *weights)
    return (y_prompt, y_sample, conv_p, ssm_p, gla_p, conv_s, ssm_s, gla_s)


_drawn_inputs = setup_inputs


def setup_inputs(seed=0):
    import zlib

    import numpy as np

    out = dict(_drawn_inputs(seed))
    spreads = {}
    factors = {'d_skip': 25.304, 'b_gate': 6.157, 'gla_norm': 3.184}
    for name, (base, spread) in spreads.items():
        noise = np.random.default_rng([zlib.crc32(name.encode()), seed]).standard_normal(out[name].shape)
        drawn = base * np.exp(spread * noise) if base else spread * noise
        out[name] = __import__('jax').numpy.asarray(drawn.astype(out[name].dtype))
    for name, factor in factors.items():
        out[name] = (out[name] * factor).astype(out[name].dtype)
    return out
```

```python
from contextlib import ExitStack

import concourse.bass as bass
from concourse import mybir

F32 = mybir.dt.float32
U32 = mybir.dt.uint32
ACT = mybir.ActivationFunctionType
ALU = mybir.AluOpType
AXX = mybir.AxisListType.X

P = 128
D = 1024
KD = D // P
SEQ = 1024
NT = SEQ // P
NS = 8
ROWS = SEQ + NS
TILED = (NT + 1) * P
THIRD = ROWS // 3
MODS = 6 * D
NXBC = 12
NQK = 8
HS = 16
HP = 64
GH = 4
GV = 256
HALF = 64
PH = 8
TOPK = 16
SLOTS = PH * TOPK
RING = 8
GROUP = 4
EPS = 1e-6
LOWEST = -3.0e38


def bcast(ap, shape):
    return ap.to_broadcast(shape)


def wait_apart(eng, sem, value):
    eng.wait_ge(sem, value)
    eng.nop(nofuse=True)


class Chain:

    def __init__(self, eng, sem, base=0):
        self.eng, self.sem, self.base, self.n = eng, sem, base, 0

    def step(self, ins):
        ins.then_inc(self.sem, 1)
        self.n += 1
        self.eng.wait_ge(self.sem, self.base + self.n)

    def step_apart(self, ins):
        ins.then_inc(self.sem, 1)
        self.n += 1
        wait_apart(self.eng, self.sem, self.base + self.n)

    def mark(self, ins):
        ins.then_inc(self.sem, 1)
        self.n += 1

    def join(self):
        self.eng.wait_ge(self.sem, self.base + self.n)


class Prog:

    def __init__(self, nc, stack, io):
        self.nc, self.io = nc, io
        self.stack = stack
        d = lambda name, shape: nc.dram_tensor(name, shape, F32, kind="Internal").ap()
        self.mod_d = d("mod_d", (NS + 1, MODS))
        self.proj_d = d("proj_d", (ROWS, 3, D))
        self.xbc_d = d("xbc_d", (NXBC, P, ROWS))
        self.qk_d = d("qk_d", (NQK, P, ROWS))
        self.cum_d = d("cum_d", (GH, P, ROWS))
        self.x1_d = d("x1_d", (ROWS, D))
        self.h2_d = d("h2_d", (TILED, D))
        s = lambda name, shape: stack.enter_context(nc.sbuf_tensor(name, shape, F32))
        self.ident = s("ident", [P, P])
        self.tri = s("tri", [P, P])
        self.later = s("later", [P, P])
        self.blk = s("blk", [P, P])
        self.ones = s("ones", [P, P])
        self.sel8 = s("sel8", [NS, NS, P])
        self.eye8 = s("eye8", [P, NS, NS])
        self.iota16 = s("iota16", [P, TOPK])
        self.eps = s("eps", [P, 1])
        self.dt = s("dt", [P, NT + 1, HS])
        self.dta = s("dta", [P, NT + 1, HS])
        self.ecum = s("ecum", [P, NT, HS])
        self.etoend = s("etoend", [P, NT, HS])
        self.etot = s("etot", [P, NT, HS])
        self.edta = s("edta", [NS, HS])
        self.ps = stack.enter_context(nc.psum_tensor("ps", [P, 8 * 512], F32))

    def sem(self, name):
        handle = self.nc.alloc_semaphore(name=name)
        self.sems.append(handle)
        return handle

    def phase(self, emit, *args):
        self.sems = []
        emit(self, *args)
        self.nc.clear_and_free_semaphores(self.sems)
        self.nc.all_engine_barrier()

    def bank(self, n, rows=P, cols=512, at=0):
        return self.ps[0:rows, n * 512 + at:n * 512 + at + cols]


def modulation(g):
    nc, io = g.nc, g.io
    NB = MODS // 512
    with ExitStack() as st:
        sb = lambda n, s: st.enter_context(nc.sbuf_tensor(n, s, F32))
        sem = lambda n: g.sem(n)
        c_sb = sb("c_sb", [NS + 1, D])
        sc_sb = sb("sc_sb", [NS + 1, D])
        cT = sb("cT", [P, KD, NS + 1])
        w = sb("w_mod_sb", [P, 2, KD, 512])
        bm = sb("bm", [NS + 1, MODS])
        mod = sb("mod", [NS + 1, MODS])
        c_in, bm_in = sem("m_c_in"), sem("m_bm_in")
        w_in = [sem("m_w_in0"), sem("m_w_in1")]
        consts0, consts = sem("m_consts0"), sem("m_consts")
        silu_done, cT_ps, cT_done = sem("m_silu_done"), sem("m_cT_ps"), sem("m_cT_done")
        prod, summed, stored = sem("m_prod"), sem("m_summed"), sem("m_stored")
        block = st.enter_context(nc.Block())

        @block.sync
        def _(sp):
            sp.dma_start(c_sb[:], io["c_all"]).then_inc(c_in, 16)
            sp.dma_start(bm[:], io["b_mod"].partition_broadcast(NS + 1)).then_inc(bm_in, 16)
            for b in range(2):
                sp.dma_start(w[:, b], io["w_mod"][b]).then_inc(w_in[b], 16)
            with sp.Fori(0, NB // 2 - 1) as i:
                for b in range(2):
                    sp.wait_ge(prod, i * 2 + b + 1)
                    sp.dma_start(w[:, b], io["w_mod"][bass.ds(i * 2 + b + 2, 1)].squeeze(0)).then_inc(w_in[b], 16)
            sp.wait_ge(summed, NB)
            sp.dma_start(g.mod_d, mod[:]).then_inc(stored, 16)
            sp.wait_ge(stored, 16)

        @block.gpsimd
        def _(pool):
            for t, v in ((g.ident, 0.0), (g.tri, 1.0), (g.later, 1.0), (g.ones, 1.0),
                         (g.sel8, 1.0), (g.eye8, 1.0), (g.eps, EPS)):
                nc.gpsimd.memset(t[:], v).then_inc(consts0, 1)
            nc.gpsimd.iota(g.iota16[:], [[1, TOPK]], base=0, channel_multiplier=0,
                           allow_small_or_imprecise_dtypes=True).then_inc(consts0, 1)
            pool.wait_ge(consts0, 8)
            sel = nc.gpsimd.affine_select
            sel(out=g.ident[:], in_=g.ident[:], compare_op=ALU.not_equal, fill=1.0, base=0,
                pattern=[[-1, P]], channel_multiplier=1).then_inc(consts, 1)
            sel(out=g.tri[:], in_=g.tri[:], compare_op=ALU.is_ge, fill=0.0, base=0,
                pattern=[[1, P]], channel_multiplier=-1).then_inc(consts, 1)
            sel(out=g.later[:], in_=g.later[:], compare_op=ALU.is_gt, fill=0.0, base=0,
                pattern=[[-1, P]], channel_multiplier=1).then_inc(consts, 1)
            sel(out=g.sel8[:], in_=g.sel8[:], compare_op=ALU.is_equal, fill=0.0, base=0,
                pattern=[[-1, NS], [0, P]], channel_multiplier=1).then_inc(consts, 1)
            sel(out=g.eye8[:], in_=g.eye8[:], compare_op=ALU.is_equal, fill=0.0, base=0,
                pattern=[[-1, NS], [1, NS]], channel_multiplier=0).then_inc(consts, 1)
            pool.wait_ge(consts, 5)
            nc.gpsimd.tensor_copy(g.blk[:], g.tri[:]).then_inc(consts, 1)
            pool.wait_ge(consts, 6)
            nc.gpsimd.memset(g.blk[0:HALF, HALF:P], 0.0).then_inc(consts, 1)
            pool.wait_ge(consts, 7)

        @block.scalar
        def _(act):
            act.wait_ge(c_in, 16)
            nc.scalar.activation(sc_sb[:], c_sb[:], ACT.Silu).then_inc(silu_done, 1)
            act.wait_ge(cT_ps, 1)
            nc.scalar.activation(cT[:].rearrange("p k r -> p (k r)"), g.bank(0, cols=KD * (NS + 1)),
                                 ACT.Copy).then_inc(cT_done, 1)

        @block.tensor
        def _(pe):
            pe.wait_ge(silu_done, 1)
            pe.wait_ge(consts, 1)
            for k in range(KD):
                last = nc.tensor.transpose(g.bank(0, cols=NS + 1, at=k * (NS + 1)),
                                           sc_sb[:, k * P:(k + 1) * P], g.ident[0:NS + 1, 0:NS + 1])
            last.then_inc(cT_ps, 1)
            pe.wait_ge(cT_done, 1)
            with pe.Fori(0, NB // 2) as i:
                for b in range(2):
                    pe.wait_ge(w_in[b], i * 16 + 16)
                    for k in range(KD):
                        last = nc.tensor.matmul(g.bank(2 + b, rows=NS + 1), cT[:, k, :], w[:, b, k, :],
                                                start=(k == 0), stop=(k == KD - 1))
                    last.then_inc(prod, 1)
                pe.wait_ge(summed, i * 2 + 2)

        @block.vector
        def _(dve):
            dve.wait_ge(bm_in, 16)
            with dve.Fori(0, NB // 2) as i:
                for b in range(2):
                    dve.wait_ge(prod, i * 2 + b + 1)
                    cols = bass.ds((i * 2 + b) * 512, 512)
                    nc.vector.tensor_tensor(mod[:, cols], g.bank(2 + b, rows=NS + 1), bm[:, cols],
                                            ALU.add).then_inc(summed, 1)


def norm_in(g, hT):
    nc, io = g.nc, g.io
    with ExitStack() as st:
        sb = lambda n, s: st.enter_context(nc.sbuf_tensor(n, s, F32))
        sem = lambda n: g.sem(n)
        x = sb("n_x", [P, D])
        sq = sb("n_sq", [P, D])
        h = sb("n_h", [P, D])
        ms, lr, r = sb("n_ms", [P, 1]), sb("n_lr", [P, 1]), sb("n_r", [P, 1])
        scale = [sb("n_scale_s", [P, D]), sb("n_scale_p", [P, D])]
        shift = [sb("n_shift_s", [P, D]), sb("n_shift_p", [P, D])]
        norm = sb("n_norm", [P, D])
        mods_in, x_in, scales = sem("n_mods_in"), sem("n_x_in"), sem("n_scales")
        act_ch, rstd, normed, hchain = sem("n_act_ch"), sem("n_rstd"), sem("n_normed"), sem("n_hchain")
        flipped, kept = sem("n_flipped"), sem("n_kept")
        block = st.enter_context(nc.Block())

        @block.sync
        def _(sp):
            sp.dma_start(norm[:], io["norm_mix"].partition_broadcast(P)).then_inc(mods_in, 16)
            sp.dma_start(shift[0][0:NS, :], g.mod_d[0:NS, 0:D]).then_inc(mods_in, 16)
            sp.dma_start(scale[0][0:NS, :], g.mod_d[0:NS, D:2 * D]).then_inc(mods_in, 16)
            sp.dma_start(shift[1][:], g.mod_d[NS, 0:D].partition_broadcast(P)).then_inc(mods_in, 16)
            sp.dma_start(scale[1][:], g.mod_d[NS, D:2 * D].partition_broadcast(P)).then_inc(mods_in, 16)
            sp.dma_start(x[0:NS, :], io["x_sample"]).then_inc(x_in, 16)
            with sp.Fori(0, NT) as i:
                sp.wait_ge(normed, i + 1)
                sp.dma_start(x[:], io["x_prompt"][bass.ds(i * P, P), :]).then_inc(x_in, 16)

        def rows(kind):
            return NS if kind == 0 else P

        @block.scalar
        def _(act):
            def tile(kind, n):
                rs = rows(kind)
                act.wait_ge(x_in, n * 16 + 16)
                ch = Chain(act, act_ch, n * 2)
                ch.step(nc.scalar.activation(sq[0:rs, :], x[0:rs, :], ACT.Square, accum_out=ms[0:rs, :]))
                ch.step(nc.scalar.activation(lr[0:rs, :], ms[0:rs, :], ACT.Ln, scale=1.0 / D, bias=g.eps[0:rs, :]))
                nc.scalar.activation(r[0:rs, :], lr[0:rs, :], ACT.Exp, scale=-0.5).then_inc(rstd, 1)
                act.wait_ge(flipped, n + 1)
                cols = slice(SEQ, ROWS) if kind == 0 else bass.ds((n - 1) * P, P)
                src = g.ps[:, 0:KD * P].rearrange("p (k r) -> p k r", r=P)[:, :, 0:rs]
                nc.scalar.activation(hT[:, :, cols], src, ACT.Copy).then_inc(kept, 1)

            tile(0, 0)
            with act.Fori(1, NT + 1) as i:
                tile(1, i)
            act.wait_ge(kept, NT + 1)

        @block.vector
        def _(dve):
            dve.wait_ge(mods_in, 80)
            for kind, rs in ((0, NS), (1, P)):
                s = scale[kind][0:rs, :]
                nc.vector.scalar_tensor_tensor(out=s, in0=s, scalar=1.0, in1=norm[0:rs, :],
                                               op0=ALU.add, op1=ALU.mult).then_inc(scales, 1)
            dve.wait_ge(scales, 2)

            def tile(kind, n):
                rs = rows(kind)
                dve.wait_ge(rstd, n + 1)
                if not (kind == 0):
                    dve.wait_ge(flipped, n)
                nc.vector.scalar_tensor_tensor(out=h[0:rs, :], in0=x[0:rs, :], scalar=r[0:rs, :],
                                               in1=scale[kind][0:rs, :], op0=ALU.mult,
                                               op1=ALU.mult).then_inc(hchain, 1)
                dve.wait_ge(hchain, n + 1)
                nc.vector.tensor_tensor(h[0:rs, :], h[0:rs, :], shift[kind][0:rs, :], ALU.add).then_inc(normed, 1)

            tile(0, 0)
            with dve.Fori(1, NT + 1) as i:
                tile(1, i)

        @block.tensor
        def _(pe):
            def tile(kind, n):
                rs = rows(kind)
                pe.wait_ge(normed, n + 1)
                if not (kind == 0):
                    pe.wait_ge(kept, n)
                for k in range(KD):
                    last = nc.tensor.transpose(g.ps[:, k * P:k * P + rs], h[0:rs, k * P:(k + 1) * P],
                                               g.ident[0:rs, 0:rs])
                last.then_inc(flipped, 1)

            tile(0, 0)
            with pe.Fori(1, NT + 1) as i:
                tile(1, i)


def projections(g, hT):
    nc, io = g.nc, g.io
    with ExitStack() as st:
        sb = lambda n, s: st.enter_context(nc.sbuf_tensor(n, s, F32))
        sem = lambda n: g.sem(n)
        NPAR = 4 + 1 + 3 * NS
        w = [sb(f"p_w{b}", [P, KD, P]) for b in range(2)]
        par = [sb(f"p_par{b}", [P, NPAR]) for b in range(2)]
        raw = [sb(f"p_raw{b}", [P, 3 + ROWS]) for b in range(2)]
        acc = [sb(f"p_acc{b}", [P, ROWS]) for b in range(2)]
        res = [sb(f"p_res{b}", [P, ROWS]) for b in range(2)]
        w_in, par_in = [sem("p_w_in0"), sem("p_w_in1")], [sem("p_par_in0"), sem("p_par_in1")]
        cleared, chan, evac = sem("p_cleared"), sem("p_chan"), sem("p_evac")
        convd, cchain, silud, cstored = sem("p_convd"), sem("p_cchain"), sem("p_silud"), sem("p_cstored")
        bstored = [sem("p_bstored0"), sem("p_bstored1")]
        NC = NXBC + NQK
        STEPS = 7

        with nc.Block() as block:
            @block.sync
            def _(sp):
                for b in range(2):
                    sp.dma_start(w[b][:], io["w_chan"][b]).then_inc(w_in[b], 16)
                with sp.Fori(0, NC // 2 - 1) as i:
                    for b in range(2):
                        sp.wait_ge(chan, i * 2 + b + 1)
                        sp.dma_start(w[b][:], io["w_chan"][bass.ds(i * 2 + b + 2, 1)].squeeze(0)).then_inc(w_in[b], 16)

            @block.gpsimd
            def _(pool):
                for b in range(2):
                    pool.dma_start(par[b][:], io["conv_par"][b]).then_inc(par_in[b], 16)

                def store(i, more):
                    for b in range(2):
                        c = i * 2 + b
                        one = lambda t: t[bass.ds(c, 1)].squeeze(0)
                        wait_apart(pool, silud, c + 1)
                        pool.dma_start(one(g.xbc_d), res[b][:]).then_inc(bstored[b], 16)
                        pool.dma_start(one(io["conv_p"]), raw[b][:, SEQ:SEQ + 3]).then_inc(bstored[b], 16)
                        pool.dma_start(one(io["conv_s"])[:, 0:2 * NS], par[b][:, 5 + NS:5 + 3 * NS]).then_inc(bstored[b], 16)
                        pool.dma_start(one(io["conv_s"])[:, 2 * NS:3 * NS], raw[b][:, SEQ + 3:ROWS + 3]).then_inc(bstored[b], 16)
                        if more:
                            wait_apart(pool, bstored[b], i * 64 + 64)
                            pool.dma_start(par[b][:], io["conv_par"][bass.ds(c + 2, 1)].squeeze(0)).then_inc(par_in[b], 16)

                with pool.Fori(0, NXBC // 2 - 1) as i:
                    store(i, True)
                store(NXBC // 2 - 1, False)
                with pool.Fori(0, NQK // 2) as i:
                    for b in range(2):
                        wait_apart(pool, evac, i * 2 + b + NXBC + 1)
                        pool.dma_start(g.qk_d[bass.ds(i * 2 + b, 1)].squeeze(0), raw[b][:, 3:3 + ROWS]).then_inc(bstored[b], 16)
                        wait_apart(pool, bstored[b], i * 16 + 16 + 64 * (NXBC // 2))

            @block.tensor
            def _(pe):
                def chunk(b, c, wait):
                    pe.wait_ge(w_in[b], wait)
                    for j in range(3):
                        for k in range(KD):
                            last = nc.tensor.matmul(g.bank(3 * b + j, cols=THIRD), w[b][:, k, :],
                                                    hT[:, k, j * THIRD:(j + 1) * THIRD],
                                                    start=(k == 0), stop=(k == KD - 1))
                    last.then_inc(chan, 1)

                chunk(0, 0, 16)
                chunk(1, 1, 16)
                with pe.Fori(1, NC // 2) as i:
                    for b in range(2):
                        pe.wait_ge(evac, i * 2 + b - 1)
                        chunk(b, i * 2 + b, i * 16 + 16)

            @block.scalar
            def _(act):
                def evacuate(b, c):
                    act.wait_ge(chan, c + 1)
                    src = g.ps[:, 3 * b * 512:(3 * b + 3) * 512].rearrange("p (j c) -> p j c", c=512)[:, :, 0:THIRD]
                    nc.scalar.activation(raw[b][:, 3:3 + ROWS].rearrange("p (j c) -> p j c", c=THIRD), src,
                                         ACT.Copy).then_inc(evac, 1)

                def silu(b, c):
                    act.wait_ge(convd, c + 1)
                    nc.scalar.activation(res[b][:], acc[b][:], ACT.Silu).then_inc(silud, 1)

                act.wait_ge(cleared, 2)
                evacuate(0, 0)
                evacuate(1, 1)
                silu(0, 0)
                silu(1, 1)
                with act.Fori(1, NXBC // 2) as i:
                    for b in range(2):
                        act.wait_ge(bstored[b], i * 64)
                        evacuate(b, i * 2 + b)
                    for b in range(2):
                        silu(b, i * 2 + b)
                with act.Fori(0, NQK // 2) as i:
                    for b in range(2):
                        act.wait_ge(bstored[b], i * 16 + 64 * (NXBC // 2))
                        evacuate(b, i * 2 + b + NXBC)
                act.wait_ge(evac, NC)

            @block.vector
            def _(dve):
                for b in range(2):
                    nc.vector.memset(raw[b][:, 0:3], 0.0).then_inc(cleared, 1)
                with dve.Fori(0, NXBC // 2) as i:
                    for b in range(2):
                        c = i * 2 + b
                        ch = Chain(dve, cchain, c * STEPS)
                        dve.wait_ge(par_in[b], i * 16 + 16)
                        dve.wait_ge(evac, c + 1)
                        tap = lambda j: par[b][:, j:j + 1]
                        late, new = acc[b][:, SEQ:ROWS], raw[b][:, SEQ + 3:ROWS + 3]
                        body = acc[b][:, 0:SEQ]
                        ch.mark(nc.vector.tensor_scalar(body, raw[b][:, 0:SEQ], tap(0), tap(4), ALU.mult, ALU.add))
                        ch.step(nc.vector.tensor_scalar(late, new, tap(3), tap(4), ALU.mult, ALU.add))
                        for j in range(1, 4):
                            old = par[b][:, 5 + (j - 1) * NS:5 + j * NS]
                            mul_add = nc.vector.scalar_tensor_tensor
                            ins = mul_add(out=late, in0=old, scalar=tap(j - 1), in1=late, op0=ALU.mult, op1=ALU.add)
                            ch.mark(ins)
                            ins = mul_add(out=body, in0=raw[b][:, j:j + SEQ], scalar=tap(j), in1=body,
                                          op0=ALU.mult, op1=ALU.add)
                            if j < 3:
                                ch.step(ins)
                            else:
                                ins.then_inc(convd, 1)
                        assert ch.n == STEPS

        wt = [sb(f"p_wt{b}", [P, KD, 512]) for b in range(2)]
        evs = [sb(f"p_ev{s}", [P, 512]) for s in range(6)]
        wdt, wgate = sb("p_wdt", [P, KD, HS]), sb("p_wgate", [P, KD, 16])
        wt_in, wd_in = [sem("p_wt_in0"), sem("p_wt_in1")], sem("p_wd_in")
        tprod, tevac = sem("p_tprod"), sem("p_tevac")
        tstored = [sem(f"p_tstored{s}") for s in range(6)]
        NRT = NT + 1

        with nc.Block() as block:
            @block.sync
            def _(sp):
                for b in range(2):
                    sp.dma_start(wt[b][:], io["w_rows"][b]).then_inc(wt_in[b], 16)
                with sp.Fori(0, 2) as i:
                    for b in range(2):
                        sp.wait_ge(tprod, (i * 2 + b + 1) * NRT)
                        sp.dma_start(wt[b][:], io["w_rows"][bass.ds(i * 2 + b + 2, 1)].squeeze(0)).then_inc(wt_in[b], 16)

            @block.gpsimd
            def _(pool):
                with pool.Fori(0, 3) as i:
                    for b in range(2):
                        for t in range(NRT):
                            n = b * NRT + t
                            rs = P if t < NT else NS
                            wait_apart(pool, tevac, i * (2 * NRT) + n + 1)
                            dst = g.proj_d[t * P:t * P + rs, bass.ds(i, 1), b * 512:(b + 1) * 512].squeeze(1)
                            pool.dma_start(dst, evs[n % 6][0:rs, :]).then_inc(tstored[n % 6], 16)
                for s in range(6):
                    pool.wait_ge(tstored[s], 16 * 3 * (2 * NRT // 6))

            @block.tensor
            def _(pe):
                def block_rows(i, first):
                    for b in range(2):
                        pe.wait_ge(wt_in[b], i * 16 + 16)
                        for t in range(NRT):
                            n = b * NRT + t
                            rs = P if t < NT else NS
                            if n >= 6 or not first:
                                pe.wait_ge(tevac, i * (2 * NRT) + n - 5)
                            for k in range(KD):
                                last = nc.tensor.matmul(g.bank(n % 6, rows=rs), hT[:, k, t * P:t * P + rs],
                                                        wt[b][:, k, :], start=(k == 0), stop=(k == KD - 1))
                            last.then_inc(tprod, 1)

                block_rows(0, True)
                with pe.Fori(1, 3) as i:
                    block_rows(i, False)

            @block.scalar
            def _(act):
                def block_rows(i, first, func):
                    for b in range(2):
                        for t in range(NRT):
                            n = b * NRT + t
                            rs = P if t < NT else NS
                            if n >= 6 or not first:
                                act.wait_ge(tstored[n % 6], i * (16 * (2 * NRT // 6)) + 16 * (n // 6))
                            act.wait_ge(tprod, i * (2 * NRT) + n + 1)
                            nc.scalar.activation(evs[n % 6][0:rs, :], g.bank(n % 6, rows=rs), func).then_inc(tevac, 1)

                block_rows(0, True, ACT.Silu)
                block_rows(1, False, ACT.Silu)
                block_rows(2, False, ACT.Copy)

        dbias, an = sb("p_dbias", [P, HS]), sb("p_an", [P, HS])
        al = sb("p_al", [P, HS])
        dx, dm = sb("p_dx", [P, NT + 1, HS]), sb("p_dm", [P, NT + 1, HS])
        wgu, bg = sb("p_wgu", [16, GH * P]), sb("p_bg", [P, GH])
        gT = sb("p_gT", [16, ROWS])
        xg, ab, cum = sb("p_xg", [P, ROWS]), sb("p_ab", [P, ROWS]), sb("p_cum", [P, ROWS])
        keep, mn = sb("p_keep", [P, ROWS]), sb("p_mn", [P, ROWS])
        small_in, a_neg = sem("p_small_in"), sem("p_a_neg")
        dtps, dch, dabs, dlog, dready = sem("p_dtps"), sem("p_dch"), sem("p_dabs"), sem("p_dlog"), sem("p_dready")
        decps, decs = sem("p_decps"), sem("p_decs")
        gps, gts, gup, gch, gabs, glog = (sem("p_gps"), sem("p_gts"), sem("p_gup"), sem("p_gch"),
                                          sem("p_gabs"), sem("p_glog"))
        ach, cumd, cums, keepd = sem("p_ach"), sem("p_cumd"), sem("p_cums"), sem("p_keepd")

        with nc.Block() as block:
            @block.sync
            def _(sp):
                sp.dma_start(wdt[:], io["w_dt"]).then_inc(small_in, 16)
                sp.dma_start(wgate[:], io["w_gate"]).then_inc(small_in, 16)
                sp.dma_start(dbias[:], io["dt_bias"].partition_broadcast(P)).then_inc(small_in, 16)
                sp.dma_start(al[:], io["a_log"].partition_broadcast(P)).then_inc(small_in, 16)
                sp.dma_start(wgu[:], io["w_gate_up"]).then_inc(small_in, 16)
                sp.dma_start(bg[:], io["b_gate"]).then_inc(small_in, 16)
                for c in range(GH):
                    sp.wait_ge(cumd, c + 1)
                    sp.dma_start(g.cum_d[c], cum[:]).then_inc(cums, 16)
                sp.wait_ge(cums, 16 * GH)

            @block.tensor
            def _(pe):
                pe.wait_ge(small_in, 96)
                for t in range(NRT):
                    rs = P if t < NT else NS
                    for k in range(KD):
                        last = nc.tensor.matmul(g.bank(0, rows=rs, cols=HS, at=t * HS), hT[:, k, t * P:t * P + rs],
                                                wdt[:, k, :], start=(k == 0), stop=(k == KD - 1))
                last.then_inc(dtps, 1)
                for j in range(3):
                    for k in range(KD):
                        last = nc.tensor.matmul(g.bank(1 + j, rows=16, cols=THIRD), wgate[:, k, :],
                                                hT[:, k, j * THIRD:(j + 1) * THIRD], start=(k == 0), stop=(k == KD - 1))
                last.then_inc(gps, 1)
                pe.wait_ge(dready, 2)
                for n, lhs in enumerate((g.tri, g.later, g.ones)):
                    last = nc.tensor.matmul(g.bank(4, cols=P, at=n * P), lhs[:],
                                            g.dta[:, 0:NT, :].rearrange("p t h -> p (t h)"), start=True, stop=True)
                last.then_inc(decps, 1)
                pe.wait_ge(gts, 1)
                for c in range(GH):
                    if c:
                        pe.wait_ge(gabs, c)
                    for j in range(3):
                        last = nc.tensor.matmul(g.bank(5 + j, cols=THIRD), wgu[:, c * P:(c + 1) * P],
                                                gT[:, j * THIRD:(j + 1) * THIRD], start=True, stop=True)
                    last.then_inc(gup, 1)

            @block.vector
            def _(dve):
                V = nc.vector
                V.memset(keep[:], 1.0).then_inc(keepd, 1)
                dve.wait_ge(keepd, 1)
                V.memset(keep[:, 0:SEQ].rearrange("p (t s) -> p t s", s=P)[:, :, 0:1], 0.0).then_inc(keepd, 1)
                V.memset(keep[:, SEQ:ROWS], 0.0).then_inc(keepd, 1)
                ch = Chain(dve, dch)
                dve.wait_ge(dtps, 1)
                dve.wait_ge(small_in, 96)
                parts = ((P, slice(0, NT), NT), (NS, slice(NT, NT + 1), 1))
                for rs, ts, n in parts:
                    src = g.ps[0:rs, ts.start * HS:ts.stop * HS].rearrange("p (t h) -> p t h", h=HS)
                    V.tensor_tensor(dx[0:rs, ts, :], src, bcast(dbias[0:rs, :].unsqueeze(1), [rs, n, HS]),
                                    ALU.add).then_inc(dabs, 1)
                dve.wait_ge(dabs, 2)
                for rs, ts, n in parts:
                    ch.step(V.tensor_scalar(g.dt[0:rs, ts, :], dx[0:rs, ts, :], 0.0, None, ALU.max))
                dve.wait_ge(dlog, 2)
                for rs, ts, n in parts:
                    ch.step(V.tensor_tensor(g.dt[0:rs, ts, :], g.dt[0:rs, ts, :], dm[0:rs, ts, :], ALU.add))
                dve.wait_ge(a_neg, 1)
                for rs, ts, n in parts:
                    V.scalar_tensor_tensor(out=g.dta[0:rs, ts, :], in0=g.dt[0:rs, ts, :], scalar=-1.0,
                                           in1=bcast(an[0:rs, :].unsqueeze(1), [rs, n, HS]),
                                           op0=ALU.mult, op1=ALU.mult).then_inc(dready, 1)
                dve.wait_ge(keepd, 3)
                gc = Chain(dve, gch)
                for c in range(GH):
                    dve.wait_ge(gup, c + 1)
                    if c:
                        dve.wait_ge(glog, c)
                    src = g.ps[:, 5 * 512:8 * 512].rearrange("p (j c) -> p j c", c=512)[:, :, 0:THIRD]
                    V.tensor_scalar(xg[:].rearrange("p (j c) -> p j c", c=THIRD), src, bg[:, c:c + 1], None,
                                    ALU.add).then_inc(gabs, 1)
                    dve.wait_ge(gabs, c + 1)
                    gc.step(V.tensor_scalar(mn[:], xg[:], 0.0, None, ALU.min))
                    dve.wait_ge(glog, c + 1)
                    gc.step(V.tensor_tensor(ab[:], mn[:], ab[:], ALU.subtract))
                    if c:
                        dve.wait_ge(cums, 16 * c)
                    gc.step(V.tensor_tensor_scan(xg[:], keep[:], ab[:], 0.0, ALU.mult, ALU.add))
                    V.tensor_scalar(cum[:], xg[:], 1.0 / 16.0, None, ALU.mult).then_inc(cumd, 1)
                    dve.wait_ge(cumd, c + 1)

            @block.scalar
            def _(act):
                A = nc.scalar.activation
                act.wait_ge(small_in, 96)
                A(an[:], al[:], ACT.Exp).then_inc(a_neg, 1)
                ch = Chain(act, ach)
                for n, (rs, ts) in enumerate(((P, slice(0, NT)), (NS, slice(NT, NT + 1)))):
                    act.wait_ge(dabs, n + 1)
                    ch.step(A(dm[0:rs, ts, :], dx[0:rs, ts, :], ACT.Abs))
                    ch.step(A(dm[0:rs, ts, :], dm[0:rs, ts, :], ACT.Exp, scale=-1.0))
                    A(dm[0:rs, ts, :], dm[0:rs, ts, :], ACT.Ln, bias=1.0).then_inc(dlog, 1)
                act.wait_ge(gps, 1)
                src = g.ps[0:16, 512:4 * 512].rearrange("p (j c) -> p j c", c=512)[:, :, 0:THIRD]
                A(gT[:].rearrange("p (j c) -> p j c", c=THIRD), src, ACT.Copy).then_inc(gts, 1)
                act.wait_ge(decps, 1)
                for n, dst in enumerate((g.ecum, g.etoend, g.etot)):
                    A(dst[:].rearrange("p t h -> p (t h)"), g.bank(4, cols=P, at=n * P), ACT.Exp).then_inc(decs, 1)
                act.wait_ge(dready, 2)
                A(g.edta[:], g.dta[0:NS, NT, :], ACT.Exp).then_inc(decs, 1)
                for c in range(GH):
                    act.wait_ge(gabs, c + 1)
                    if c:
                        act.wait_ge(cumd, c)
                    ch.step(A(ab[:], xg[:], ACT.Abs))
                    ch.step(A(ab[:], ab[:], ACT.Exp, scale=-1.0))
                    A(ab[:], ab[:], ACT.Ln, bias=1.0).then_inc(glog, 1)
                act.wait_ge(decs, 4)


class Output:

    def __init__(self, g, st, pre, rows):
        nc = g.nc
        self.g, self.rows = g, rows
        sb = lambda n, s: st.enter_context(nc.sbuf_tensor(pre + n, s, F32))
        sem = lambda n: g.sem(pre + n)
        self.w = sb("w_out", [P, 2 * KD, D])
        self.cat, self.catT = sb("cat", [P, 2 * D]), sb("catT", [P, 2 * KD, P])
        self.x, self.x1, self.h2 = sb("x", [P, D]), sb("x1", [P, D]), sb("h2", [P, D])
        self.junk = sb("junk", [P, D])
        self.ms, self.r = sb("ms2", [P, 2]), sb("r2", [P, 1])
        self.gate1, self.scale2, self.shift2 = sb("gate1", [P, D]), sb("scale2", [P, D]), sb("shift2", [P, D])
        self.norm = sb("norm_ffn", [P, D])
        self.w_in, self.mods_in, self.scaled = sem("w_out_in"), sem("mods_in"), sem("scaled")
        self.x_in, self.cat_ready = sem("x_in"), sem("cat_ready")
        self.catT_ps, self.catT_kept, self.prod = sem("catT_ps"), sem("catT_kept"), sem("prod")
        self.och, self.x1_ready, self.r2_ready, self.h2_ready = (sem("och"), sem("x1_ready"), sem("r2_ready"),
                                                                 sem("h2_ready"))
        self.ach, self.x1_stored, self.h2_stored = sem("oach"), sem("x1_stored"), sem("h2_stored")

    def load_constants(self, sp):
        g, io, rs = self.g, self.g.io, self.rows
        take = lambda a: (g.mod_d[0:NS, a * D:(a + 1) * D] if rs == NS
                          else g.mod_d[NS, a * D:(a + 1) * D].partition_broadcast(P))
        sp.dma_start(self.norm[0:rs, :], io["norm_ffn"].partition_broadcast(rs)).then_inc(self.mods_in, 16)
        sp.dma_start(self.gate1[0:rs, :], take(2)).then_inc(self.mods_in, 16)
        sp.dma_start(self.shift2[0:rs, :], take(3)).then_inc(self.mods_in, 16)
        sp.dma_start(self.scale2[0:rs, :], take(4)).then_inc(self.mods_in, 16)
        sp.dma_start(self.w[:], io["w_out"]).then_inc(self.w_in, 16)

    def prepare(self, dve):
        rs = self.rows
        dve.wait_ge(self.mods_in, 64)
        s = self.scale2[0:rs, :]
        self.g.nc.vector.scalar_tensor_tensor(out=s, in0=s, scalar=1.0, in1=self.norm[0:rs, :],
                                              op0=ALU.add, op1=ALU.mult).then_inc(self.scaled, 1)
        dve.wait_ge(self.scaled, 1)

    def tensor(self, pe, n):
        g, nc, rs = self.g, self.g.nc, self.rows
        pe.wait_ge(self.cat_ready, n + 1)
        for half in range(2):
            for k in range(KD):
                c = half * KD + k
                last = nc.tensor.transpose(g.ps[:, (3 + 2 * half) * 512 + k * P:][:, 0:rs],
                                           self.cat[0:rs, c * P:(c + 1) * P], g.ident[0:rs, 0:rs])
            last.then_inc(self.catT_ps, 1)
        pe.wait_ge(self.w_in, 16)
        for half in range(2):
            pe.wait_ge(self.catT_kept, n * 2 + half + 1)
            for k in range(half * KD, half * KD + KD):
                for cols in range(2):
                    last = nc.tensor.matmul(g.bank(cols, rows=rs), self.catT[:, k, 0:rs],
                                            self.w[:, k, cols * 512:(cols + 1) * 512],
                                            start=(k == 0), stop=(k == 2 * KD - 1))
        last.then_inc(self.prod, 1)

    def scalar(self, act, n):
        g, A, rs = self.g, self.g.nc.scalar.activation, self.rows
        for half in range(2):
            act.wait_ge(self.catT_ps, n * 2 + half + 1)
            src = g.ps[:, (3 + 2 * half) * 512:][:, 0:KD * P].rearrange("p (k r) -> p k r", r=P)[:, :, 0:rs]
            A(self.catT[:, half * KD:(half + 1) * KD, 0:rs], src, ACT.Copy).then_inc(self.catT_kept, 1)
        act.wait_ge(self.x1_ready, n + 1)
        ch = Chain(act, self.ach, n * 2)
        ch.step(A(self.junk[0:rs, :], self.x1[0:rs, :], ACT.Square, accum_out=self.ms[0:rs, 0:1]))
        ch.step(A(self.ms[0:rs, 1:2], self.ms[0:rs, 0:1], ACT.Ln, scale=1.0 / D, bias=g.eps[0:rs, :]))
        A(self.r[0:rs, :], self.ms[0:rs, 1:2], ACT.Exp, scale=-0.5).then_inc(self.r2_ready, 1)
        act.wait_ge(self.r2_ready, n + 1)

    def vector(self, dve, n, first):
        g, V, rs = self.g, self.g.nc.vector, self.rows
        ch = Chain(dve, self.och, n * 2)
        dve.wait_ge(self.prod, n + 1)
        dve.wait_ge(self.x_in, n * 16 + 16)
        if not first:
            dve.wait_ge(self.x1_stored, n * 16)
            dve.wait_ge(self.h2_stored, n * 16)
        ch.step(V.tensor_tensor(self.x1[0:rs, :], g.ps[0:rs, 0:D], self.gate1[0:rs, :], ALU.mult))
        V.tensor_tensor(self.x1[0:rs, :], self.x1[0:rs, :], self.x[0:rs, :], ALU.add).then_inc(self.x1_ready, 1)
        dve.wait_ge(self.r2_ready, n + 1)
        ch.step(V.scalar_tensor_tensor(out=self.h2[0:rs, :], in0=self.x1[0:rs, :], scalar=self.r[0:rs, :],
                                       in1=self.scale2[0:rs, :], op0=ALU.mult, op1=ALU.mult))
        V.tensor_tensor(self.h2[0:rs, :], self.h2[0:rs, :], self.shift2[0:rs, :], ALU.add).then_inc(self.h2_ready, 1)

    def store(self, eng, n, row):
        g, rs = self.g, self.rows
        rows = bass.ds(row, rs)
        wait_apart(eng, self.x1_ready, n + 1)
        eng.dma_start(g.x1_d[rows, :], self.x1[0:rs, :]).then_inc(self.x1_stored, 16)
        wait_apart(eng, self.h2_ready, n + 1)
        eng.dma_start(g.h2_d[rows, :], self.h2[0:rs, :]).then_inc(self.h2_stored, 16)


def mix_prompt(g):
    nc, io = g.nc, g.io
    R = HS // 2
    QS = float(P) ** -0.5
    with ExitStack() as st:
        sb = lambda n, s: st.enter_context(nc.sbuf_tensor("x_" + n, s, F32))
        sem = lambda n: g.sem("x_" + n)
        out = Output(g, st, "xo_", P)
        xbc, zgv, qk, cum = sb("xbc", [P, NXBC, P]), sb("zgv", [P, 3, D]), sb("qk", [P, NQK, P]), sb("cum", [P, GH, P])
        dec = sb("dec", [P, HS, P])
        xs, xdt, xend = sb("xs", [P, HS, HP]), sb("xdt", [P, HS, HP]), sb("xend", [P, HS, HP])
        b_rows, cb = sb("b_rows", [P, 2, P]), sb("cb", [P, 2, P])
        S, GS = sb("S", [P, HS, HP]), sb("GS", [P, GH, GV])
        yb, yt = sb("yb", [P, HS, HP]), sb("yt", [P, HS, HP])
        d1, ref2, end = sb("d1", [P, GH, P]), sb("ref2", [P, GH, P]), sb("end", [P, GH, P])
        qd, kd, qi, ecg = sb("qd", [P, GH, P]), sb("kd", [P, GH, P]), sb("qi", [P, GH, P]), sb("ecg", [P, GH, P])
        att, keT = sb("att", [P, GH, P]), sb("keT", [P, GH, P])
        dskip, ssdn, glan = sb("dskip", [P, HS]), sb("ssdn", [P, D]), sb("glan", [P, GV])
        msy, ry, mso, ro = sb("msy", [P, 4]), sb("ry", [P, 2]), sb("mso", [P, 8]), sb("ro", [P, GH])
        consts_in, xbc_in, gla_in, zgv_in = sem("consts_in"), sem("xbc_in"), sem("gla_in"), sem("zgv_in")
        seg_in, xs_ps, xs_kept, xdt_ready, xend_ready = (sem("seg_in"), sem("xs_ps"), sem("xs_kept"),
                                                         sem("xdt_ready"), sem("xend_ready"))
        seg_ps, dec_ready, m_ready, y_ps, su_ps = (sem("seg_ps"), sem("dec_ready"), sem("m_ready"), sem("y_ps"),
                                                   sem("su_ps"))
        y_used, y_sum, ry_ready, s_ready, gs_ready = (sem("y_used"), sem("y_sum"), sem("ry_ready"), sem("s_ready"),
                                                      sem("gs_ready"))
        gdiff, gexp, gprod, att_ps, att_ready = (sem("gdiff"), sem("gexp"), sem("gprod"), sem("att_ps"),
                                                 sem("att_ready"))
        ke_ps, ke_kept, o_ps, gs_ps, ro_ready = sem("ke_ps"), sem("ke_kept"), sem("o_ps"), sem("gs_ps"), sem("ro_ready")
        vch, ach, s_out = sem("vch"), sem("ach"), sem("s_out")
        VSTEPS, ASTEPS = 6, 4
        block = st.enter_context(nc.Block())
        head = lambda t, h: t[:, h, :]
        per_head = lambda t, n: bcast(t[:, bass.ds(n, 1), :].squeeze(1).unsqueeze(2), [P, HS, HP])

        @block.sync
        def _(sp):
            sp.dma_start(dskip[:], io["d_skip"].partition_broadcast(P)).then_inc(consts_in, 16)
            sp.dma_start(ssdn[:], io["ssd_norm"].partition_broadcast(P)).then_inc(consts_in, 16)
            sp.dma_start(glan[:], io["gla_norm"].partition_broadcast(P)).then_inc(consts_in, 16)

            def load(n, first):
                rows = bass.ds(n * P, P)
                if not first:
                    sp.wait_ge(y_ps, n)
                sp.dma_start(xbc[:], g.xbc_d[:, :, rows].rearrange("c p t -> p c t")).then_inc(xbc_in, 16)
                if not first:
                    sp.wait_ge(gprod, n)
                sp.dma_start(qk[:], g.qk_d[:, :, rows].rearrange("c p t -> p c t")).then_inc(gla_in, 16)
                sp.dma_start(cum[:], g.cum_d[:, :, rows].rearrange("c p t -> p c t")).then_inc(gla_in, 16)
                if not first:
                    sp.wait_ge(out.cat_ready, n)
                    sp.wait_ge(gs_ps, n)
                sp.dma_start(zgv[:], g.proj_d[rows, :, :]).then_inc(zgv_in, 16)
                if not first:
                    sp.wait_ge(out.x1_ready, n)
                sp.dma_start(out.x[:], io["x_prompt"][rows, :]).then_inc(out.x_in, 16)

            load(0, True)
            out.load_constants(sp)
            with sp.Fori(1, NT) as n:
                load(n, False)
            sp.wait_ge(s_ready, NT + 1)
            sp.dma_start(io["ssm_p"], S[:].rearrange("p h c -> p (h c)")).then_inc(s_out, 16)
            sp.wait_ge(gs_ready, NT + 1)
            sp.dma_start(io["gla_p"], GS[:].rearrange("p h c -> p (h c)")).then_inc(s_out, 16)
            sp.wait_ge(s_out, 32)

        @block.gpsimd
        def _(pool):
            with pool.Fori(0, NT) as n:
                out.store(pool, n, n * P)
            pool.wait_ge(out.x1_stored, 16 * NT)
            pool.wait_ge(out.h2_stored, 16 * NT)

        @block.tensor
        def _(pe):
            mm, tr = nc.tensor.matmul, nc.tensor.transpose

            def tile(n, first):
                pe.wait_ge(xbc_in, n * 16 + 16)
                if not first:
                    pe.wait_ge(out.h2_ready, n)
                for c in range(KD):
                    tr(g.ps[:, c * P:(c + 1) * P], xbc[:, c, :], g.ident[:])
                for c in range(2):
                    tr(g.bank(2, cols=P, at=c * P), xbc[:, KD + c, :], g.ident[:])
                    last = mm(g.bank(2, cols=P, at=(2 + c) * P), xbc[:, KD + c, :], xbc[:, KD + 2 + c, :],
                              start=True, stop=True)
                last.then_inc(xs_ps, 1)
                pe.wait_ge(seg_in, n + 1)
                for half in range(2):
                    for q in range(2):
                        h = half * R + q * 4
                        last = mm(g.bank(3 + 2 * half + q), g.later[:], dec[:, h:h + 4, :], start=True, stop=True)
                    last.then_inc(seg_ps, 1)
                pe.wait_ge(xdt_ready, n + 1)
                for c in range(2):
                    pe.wait_ge(m_ready, n * 2 + c + 1)
                    for r in range(R):
                        h = c * R + r
                        mm(g.ps[:, h * HP:(h + 1) * HP], dec[:, h, :], xdt[:, h, :], start=True, stop=True)
                pe.wait_ge(s_ready, n + 1)
                for c in range(2):
                    last = mm(g.bank(3 + c), xbc[:, KD + 2 + c, :], S[:, c * R:(c + 1) * R, :], start=True, stop=True)
                last.then_inc(y_ps, 1)
                pe.wait_ge(xend_ready, n + 1)
                pe.wait_ge(xs_kept, n + 1)
                for c in range(2):
                    last = mm(g.bank(5 + c), b_rows[:, c, :], xend[:, c * R:(c + 1) * R, :], start=True, stop=True)
                last.then_inc(su_ps, 1)
                pe.wait_ge(gprod, n + 1)
                for h in range(GH):
                    mm(g.bank(7, cols=P, at=h * P), head(kd, h), head(qd, h), start=True, stop=True)
                for h in range(GH):
                    last = mm(g.bank(2, rows=HALF, cols=HALF, at=h * HALF), ref2[:, h, 0:HALF], ref2[:, h, HALF:P],
                              start=True, stop=True)
                last.then_inc(att_ps, 1)
                pe.wait_ge(s_ready, n + 2)
                for h in range(GH):
                    last = tr(g.bank(5, cols=P, at=h * P), head(end, h), g.ident[:])
                last.then_inc(ke_ps, 1)
                pe.wait_ge(att_ready, n + 1)
                pe.wait_ge(y_used, n + 1)
                pe.wait_ge(zgv_in, n * 16 + 16)
                pe.wait_ge(gs_ready, n + 1)
                for h in range(GH):
                    v = zgv[:, 2, h * GV:(h + 1) * GV]
                    mm(g.ps[:, h * GV:(h + 1) * GV], head(att, h), v, start=True, stop=False)
                    last = mm(g.ps[:, h * GV:(h + 1) * GV], head(qi, h), head(GS, h), start=False, stop=True)
                last.then_inc(o_ps, 1)
                pe.wait_ge(ke_kept, n + 1)
                for h in range(GH):
                    last = mm(g.ps[:, 3 * 512 + h * GV:3 * 512 + (h + 1) * GV], head(keT, h),
                              zgv[:, 2, h * GV:(h + 1) * GV], start=True, stop=True)
                last.then_inc(gs_ps, 1)
                pe.wait_ge(gs_ready, n + 2)
                out.tensor(pe, n)

            tile(0, True)
            with pe.Fori(1, NT) as n:
                tile(n, False)

        @block.scalar
        def _(act):
            A = nc.scalar.activation

            def tile(n):
                ch = Chain(act, ach, n * ASTEPS)
                act.wait_ge(xs_ps, n + 1)
                A(xs[:].rearrange("p h c -> p (h c)"), g.ps[:, 0:D], ACT.Copy)
                A(b_rows[:].rearrange("p c n -> p (c n)"), g.bank(2, cols=2 * P), ACT.Copy).then_inc(xs_kept, 1)
                for half in range(2):
                    act.wait_ge(seg_ps, n * 2 + half + 1)
                    A(dec[:, half * R:(half + 1) * R, :].rearrange("p h t -> p (h t)"),
                      g.ps[:, (3 + 2 * half) * 512:(5 + 2 * half) * 512], ACT.Exp).then_inc(dec_ready, 1)
                act.wait_ge(gdiff, n * 4 + 4)
                A(qd[:], d1[:], ACT.Exp)
                A(kd[:], d1[:], ACT.Exp, scale=-1.0)
                A(ref2[:], ref2[:], ACT.Exp)
                A(end[:], end[:], ACT.Exp)
                A(ecg[:], cum[:], ACT.Exp).then_inc(gexp, 1)
                act.wait_ge(y_sum, n + 1)
                for c in range(2):
                    ins = A(yt[:, c * R:(c + 1) * R, :], yb[:, c * R:(c + 1) * R, :], ACT.Square,
                            accum_out=msy[:, c:c + 1])
                ch.step(ins)
                ch.step(A(msy[:, 2:4], msy[:, 0:2], ACT.Ln, scale=2.0 / D, bias=g.eps[:]))
                A(ry[:], msy[:, 2:4], ACT.Exp, scale=-0.5).then_inc(ry_ready, 1)
                act.wait_ge(ry_ready, n + 1)
                act.wait_ge(ke_ps, n + 1)
                A(keT[:].rearrange("p h d -> p (h d)"), g.bank(5), ACT.Copy).then_inc(ke_kept, 1)
                act.wait_ge(o_ps, n + 1)
                for h in range(GH):
                    ins = A(yt[:, h * 4:(h + 1) * 4, :].rearrange("p h c -> p (h c)"), g.ps[:, h * GV:(h + 1) * GV],
                            ACT.Square, accum_out=mso[:, h:h + 1])
                ch.step(ins)
                ch.step(A(mso[:, 4:8], mso[:, 0:4], ACT.Ln, scale=1.0 / GV, bias=g.eps[:]))
                A(ro[:], mso[:, 4:8], ACT.Exp, scale=-0.5).then_inc(ro_ready, 1)
                act.wait_ge(ro_ready, n + 1)
                assert ch.n == ASTEPS
                out.scalar(act, n)

            with act.Fori(0, NT) as n:
                tile(n)

        @block.vector
        def _(dve):
            V, stt = nc.vector, nc.vector.scalar_tensor_tensor
            V.memset(S[:], 0.0).then_inc(s_ready, 1)
            V.memset(GS[:], 0.0).then_inc(gs_ready, 1)
            dve.wait_ge(s_ready, 1)
            dve.wait_ge(gs_ready, 1)
            dve.wait_ge(consts_in, 48)

            def tile(n, first):
                ch = Chain(dve, vch, n * VSTEPS)
                dta = g.dta[:, bass.ds(n, 1), :].squeeze(1)
                V.tensor_tensor(dec[:], bcast(dta.unsqueeze(2), [P, HS, P]), bcast(g.tri[:].unsqueeze(1), [P, HS, P]),
                                ALU.mult).then_inc(seg_in, 1)
                dve.wait_ge(xs_kept, n + 1)
                V.tensor_tensor(xdt[:], xs[:], per_head(g.dt, n), ALU.mult)
                V.tensor_tensor(cb[:], g.bank(2, cols=2 * P, at=2 * P).rearrange("p (c t) -> p c t", c=2),
                                bcast(g.tri[:].unsqueeze(1), [P, 2, P]), ALU.mult).then_inc(xdt_ready, 1)
                dve.wait_ge(xdt_ready, n + 1)
                V.tensor_tensor(xend[:], xdt[:], per_head(g.etoend, n), ALU.mult).then_inc(xend_ready, 1)
                dve.wait_ge(gla_in, n * 32 + 32)
                by_half = lambda t: t[:].rearrange("p h (c t) -> p (h c) t", c=2)
                V.tensor_tensor(by_half(d1), by_half(cum), bcast(by_half(cum)[:, :, HALF // 2:HALF // 2 + 1],
                                                                 [P, 2 * GH, HALF]), ALU.subtract).then_inc(gdiff, 1)
                seam = bcast(cum[:, :, HALF - 1:HALF], [P, GH, HALF])
                V.tensor_tensor(ref2[:, :, 0:HALF], seam, cum[:, :, 0:HALF], ALU.subtract).then_inc(gdiff, 1)
                V.tensor_tensor(ref2[:, :, HALF:P], cum[:, :, HALF:P], seam, ALU.subtract).then_inc(gdiff, 1)
                V.tensor_tensor(end[:], bcast(cum[:, :, P - 1:P], [P, GH, P]), cum[:], ALU.subtract).then_inc(gdiff, 1)
                for c in range(2):
                    dve.wait_ge(dec_ready, n * 2 + c + 1)
                    m = dec[:, c * R:(c + 1) * R, :]
                    V.tensor_tensor(m, m, bcast(cb[:, c:c + 1, :], [P, R, P]), ALU.mult).then_inc(m_ready, 1)
                dve.wait_ge(gexp, n + 1)
                q, k = qk[:, 0:GH, :], qk[:, GH:NQK, :]
                stt(out=qd[:], in0=q, scalar=QS, in1=qd[:], op0=ALU.mult, op1=ALU.mult)
                V.tensor_tensor(kd[:], k, kd[:], ALU.mult)
                stt(out=ref2[:, :, HALF:P], in0=q[:, :, HALF:P], scalar=QS, in1=ref2[:, :, HALF:P],
                    op0=ALU.mult, op1=ALU.mult)
                V.tensor_tensor(ref2[:, :, 0:HALF], k[:, :, 0:HALF], ref2[:, :, 0:HALF], ALU.mult)
                stt(out=qi[:], in0=q, scalar=QS, in1=ecg[:], op0=ALU.mult, op1=ALU.mult)
                V.tensor_tensor(end[:], k, end[:], ALU.mult).then_inc(gprod, 1)
                dve.wait_ge(y_ps, n + 1)
                V.tensor_tensor(yt[:], xs[:], bcast(dskip[:].unsqueeze(2), [P, HS, HP]), ALU.mult)
                ch.step(V.tensor_tensor(yb[:], g.ps[:, 3 * 512:5 * 512].rearrange("p (h c) -> p h c", c=HP),
                                        per_head(g.ecum, n), ALU.mult))
                V.tensor_tensor(yb[:], yb[:], g.ps[:, 0:D].rearrange("p (h c) -> p h c", c=HP), ALU.add).then_inc(y_used, 1)
                dve.wait_ge(y_used, n + 1)
                ch.mark(V.tensor_tensor(S[:], S[:], per_head(g.etot, n), ALU.mult))
                ch.step(V.tensor_tensor(yb[:], yb[:], yt[:], ALU.add))
                dve.wait_ge(zgv_in, n * 16 + 16)
                V.tensor_tensor(yb[:].rearrange("p h c -> p (h c)"), yb[:].rearrange("p h c -> p (h c)"), zgv[:, 0, :],
                                ALU.mult).then_inc(y_sum, 1)
                dve.wait_ge(su_ps, n + 1)
                V.tensor_tensor(S[:], S[:], g.ps[:, 5 * 512:7 * 512].rearrange("p (h c) -> p h c", c=HP),
                                ALU.add).then_inc(s_ready, 1)
                dve.wait_ge(att_ps, n + 1)
                ch.step(V.tensor_tensor(att[:], g.bank(7).rearrange("p (h t) -> p h t", h=GH),
                                        bcast(g.blk[:].unsqueeze(1), [P, GH, P]), ALU.mult))
                V.tensor_copy(att[0:HALF, :, HALF:P], g.bank(2, rows=HALF, cols=GH * HALF).rearrange(
                    "p (h t) -> p h t", h=GH)).then_inc(att_ready, 1)
                dve.wait_ge(ry_ready, n + 1)
                for c in range(2):
                    ins = stt(out=out.cat[:, c * 512:(c + 1) * 512], in0=yb[:, c * R:(c + 1) * R, :].rearrange(
                        "p h c -> p (h c)"), scalar=ry[:, c:c + 1], in1=ssdn[:, c * 512:(c + 1) * 512],
                        op0=ALU.mult, op1=ALU.mult)
                ch.mark(ins)
                dve.wait_ge(ro_ready, n + 1)
                for h in range(GH):
                    ins = stt(out=out.cat[:, D + h * GV:D + (h + 1) * GV], in0=g.ps[:, h * GV:(h + 1) * GV],
                              scalar=ro[:, h:h + 1], in1=glan[:], op0=ALU.mult, op1=ALU.mult)
                ch.step(ins)
                V.tensor_tensor(out.cat[:, D:2 * D], out.cat[:, D:2 * D], zgv[:, 1, :], ALU.mult).then_inc(out.cat_ready, 1)
                dve.wait_ge(gs_ps, n + 1)
                for h in range(GH):
                    ins = stt(out=head(GS, h), in0=head(GS, h), scalar=ecg[:, h, P - 1:P],
                              in1=g.ps[:, 3 * 512 + h * GV:3 * 512 + (h + 1) * GV], op0=ALU.mult, op1=ALU.add)
                ins.then_inc(gs_ready, 1)
                dve.wait_ge(gs_ready, n + 2)
                ch.join()
                assert ch.n == VSTEPS
                out.vector(dve, n, first)

            out.prepare(dve)
            tile(0, True)
            with dve.Fori(1, NT) as n:
                tile(n, False)


def mix_sample(g):
    nc, io = g.nc, g.io
    HC = HS // 2
    QS = float(P) ** -0.5
    with ExitStack() as st:
        sb = lambda n, s: st.enter_context(nc.sbuf_tensor("s_" + n, s, F32))
        sem = lambda n: g.sem("s_" + n)
        out = Output(g, st, "so_", NS)
        xbc, qk, cum, zgv = sb("xbc", [P, NXBC, NS]), sb("qk", [P, NQK, NS]), sb("cum", [P, GH, NS]), sb("zgv", [NS, 3, D])
        S = sb("S", [P, NS, HC, P])
        xr, bc, dtx, da = sb("xr", [NS, D]), sb("bc", [NS, 4 * P]), sb("dtx", [NS, D]), sb("da", [NS, D])
        turned = sb("turned", [P, 2, HC, NS])
        t, yT = sb("t", [P, HC, P]), sb("yT", [P, HC, NS])
        ela, qpad = sb("ela", [P, GH, NS]), sb("qpad", [P, GH, NS, NS])
        dskip, ssdn, glan = sb("dskip", [NS, HS]), sb("ssdn", [NS, D]), sb("glan", [NS, GV])
        y, junk = sb("y", [NS, D]), sb("junk", [NS, D])
        ms, r = sb("ms", [NS, 12]), sb("r", [NS, 6])
        none, none_ready, none_stored = sb("none", [TILED - ROWS, D]), sem("none_ready"), sem("none_stored")
        small_in, xbc_in, S_in, GS_in = sem("small_in"), sem("xbc_in"), sem("S_in"), sem("GS_in")
        rows_ps, rows_kept, pre, turn_ps, turn_kept = (sem("rows_ps"), sem("rows_kept"), sem("pre"), sem("turn_ps"),
                                                       sem("turn_kept"))
        bc_ps, s_new, yT_ps, y_done, yr = sem("bc_ps"), sem("s_new"), sem("yT_ps"), sem("y_done"), sem("yr")
        e_ready, v_ps, g_new, o_ps, o_r = sem("e_ready"), sem("v_ps"), sem("g_new"), sem("o_ps"), sem("o_r")
        vch, ach, s_out, g_out = sem("vch"), sem("ach"), sem("s_out"), sem("g_out")
        block = st.enter_context(nc.Block())

        @block.sync
        def _(sp):
            sp.dma_start(xbc[:], g.xbc_d[:, :, SEQ:ROWS].rearrange("c p t -> p c t")).then_inc(xbc_in, 16)
            sp.dma_start(S[:], io["state_ssm"]).then_inc(S_in, 16)
            sp.dma_start(qk[:], g.qk_d[:, :, SEQ:ROWS].rearrange("c p t -> p c t")).then_inc(small_in, 16)
            sp.dma_start(cum[:], g.cum_d[:, :, SEQ:ROWS].rearrange("c p t -> p c t")).then_inc(small_in, 16)
            sp.dma_start(zgv[:], g.proj_d[SEQ:ROWS, :, :]).then_inc(small_in, 16)
            sp.dma_start(dskip[:], io["d_skip"].partition_broadcast(NS)).then_inc(small_in, 16)
            sp.dma_start(ssdn[:], io["ssd_norm"].partition_broadcast(NS)).then_inc(small_in, 16)
            sp.dma_start(glan[:], io["gla_norm"].partition_broadcast(NS)).then_inc(small_in, 16)
            sp.dma_start(out.x[0:NS, :], io["x_sample"]).then_inc(out.x_in, 16)
            out.load_constants(sp)
            sp.wait_ge(s_new, NS)
            sp.dma_start(io["ssm_s"], S[:]).then_inc(s_out, 16)
            sp.wait_ge(y_done, 1)
            sp.wait_ge(s_out, 16)
            sp.dma_start(S[:].rearrange("p b c n -> p (b c n)"),
                         io["state_gla"].rearrange("p b h v -> p (b h v)")).then_inc(GS_in, 16)
            sp.wait_ge(g_new, NS)
            sp.dma_start(io["gla_s"].rearrange("p b h v -> p (b h v)"),
                         S[:].rearrange("p b c n -> p (b c n)")).then_inc(g_out, 16)
            out.store(sp, 0, SEQ)
            sp.wait_ge(g_out, 16)
            sp.wait_ge(out.x1_stored, 16)
            sp.wait_ge(out.h2_stored, 16)

        @block.gpsimd
        def _(pool):
            nc.gpsimd.memset(none[:], 0.0).then_inc(none_ready, 1)
            pool.wait_ge(none_ready, 1)
            pool.dma_start(g.h2_d[ROWS:TILED, :], none[:]).then_inc(none_stored, 16)
            pool.wait_ge(none_stored, 16)

        GS = S[:].rearrange("p b c n -> p b (c n)").rearrange("p b (h v) -> p b h v", h=GH)

        @block.tensor
        def _(pe):
            mm, tr = nc.tensor.matmul, nc.tensor.transpose
            pe.wait_ge(xbc_in, 16)
            for c in range(NXBC):
                last = tr(g.ps[0:NS, c * P:(c + 1) * P], xbc[:, c, :], g.ident[:])
            last.then_inc(rows_ps, 1)
            pe.wait_ge(pre, 2)
            for n, src in enumerate((dtx, da)):
                for c in range(HC):
                    last = tr(g.bank(3, cols=NS, at=(n * HC + c) * NS), src[:, c * P:(c + 1) * P], g.ident[0:NS, 0:NS])
            last.then_inc(turn_ps, 1)
            for b in range(NS):
                if b >= 2:
                    pe.wait_ge(s_new, b - 1)
                mm(g.bank(4 + b % 2), g.sel8[:, b, :], bc[:], start=True, stop=True).then_inc(bc_ps, 1)
            pe.wait_ge(s_new, NS)
            for c in range(HC):
                last = tr(g.ps[0:NS, c * P:(c + 1) * P], yT[:, c, :], g.ident[:])
            last.then_inc(yT_ps, 1)
            pe.wait_ge(small_in, 96)
            for b in range(NS):
                if b >= 1:
                    pe.wait_ge(g_new, b)
                for half in range(2):
                    last = mm(g.bank(6 + half), g.sel8[:, b, :], zgv[:, 2, half * 512:(half + 1) * 512],
                              start=True, stop=True)
                last.then_inc(v_ps, 1)
            pe.wait_ge(g_new, NS)
            for h in range(GH):
                for b in range(NS):
                    last = mm(g.ps[0:NS, 4 * 512 + h * GV:4 * 512 + (h + 1) * GV], qpad[:, h, b, :], GS[:, b, h, :],
                              start=(b == 0), stop=(b == NS - 1))
            last.then_inc(o_ps, 1)
            out.tensor(pe, 0)

        @block.scalar
        def _(act):
            A = nc.scalar.activation
            ch = Chain(act, ach)
            act.wait_ge(rows_ps, 1)
            A(xr[:], g.ps[0:NS, 0:D], ACT.Copy)
            A(bc[:], g.bank(2, rows=NS), ACT.Copy).then_inc(rows_kept, 1)
            act.wait_ge(turn_ps, 1)
            A(turned[:].rearrange("p a c b -> p (a c b)"), g.bank(3, cols=2 * HC * NS), ACT.Copy).then_inc(turn_kept, 1)
            act.wait_ge(small_in, 96)
            A(ela[:], cum[:], ACT.Exp).then_inc(e_ready, 1)
            act.wait_ge(y_done, 1)
            for c in range(2):
                ins = A(junk[:, c * 512:(c + 1) * 512], y[:, c * 512:(c + 1) * 512], ACT.Square, accum_out=ms[:, c:c + 1])
            ch.step(ins)
            ch.step(A(ms[:, 2:4], ms[:, 0:2], ACT.Ln, scale=2.0 / D, bias=g.eps[0:NS, :]))
            A(r[:, 0:2], ms[:, 2:4], ACT.Exp, scale=-0.5).then_inc(yr, 1)
            act.wait_ge(o_ps, 1)
            for h in range(GH):
                ins = A(junk[:, h * GV:(h + 1) * GV], g.ps[0:NS, 4 * 512 + h * GV:4 * 512 + (h + 1) * GV], ACT.Square,
                        accum_out=ms[:, 4 + h:5 + h])
            ch.step(ins)
            ch.step(A(ms[:, 8:12], ms[:, 4:8], ACT.Ln, scale=1.0 / GV, bias=g.eps[0:NS, :]))
            A(r[:, 2:6], ms[:, 8:12], ACT.Exp, scale=-0.5).then_inc(o_r, 1)
            out.scalar(act, 0)

        @block.vector
        def _(dve):
            V, stt = nc.vector, nc.vector.scalar_tensor_tensor
            ch = Chain(dve, vch)
            heads = lambda ap: ap.rearrange("p (h c) -> p h c", c=HP)
            per_head = lambda ap: bcast(ap.unsqueeze(2), [NS, HS, HP])
            V.tensor_copy(heads(da[:]), per_head(g.edta[:])).then_inc(pre, 1)
            dve.wait_ge(rows_kept, 1)
            V.tensor_tensor(heads(dtx[:]), heads(xr[:]), per_head(g.dt[0:NS, NT, :]), ALU.mult).then_inc(pre, 1)
            dve.wait_ge(turn_kept, 1)
            dve.wait_ge(S_in, 16)
            for b in range(NS):
                s_b = S[:, b]
                ch.mark(V.tensor_tensor(s_b, s_b, bcast(turned[:, 1, :, b:b + 1], [P, HC, P]), ALU.mult))
                dve.wait_ge(bc_ps, b + 1)
                row = lambda n: bcast(g.bank(4 + b % 2, cols=2 * P, at=n * 2 * P).rearrange(
                    "p (g n) -> p g n", g=2).unsqueeze(2), [P, 2, HC // 2, P])
                by_group = lambda ap: ap.rearrange("p (g r) n -> p g r n", g=2)
                ch.step(V.tensor_tensor(by_group(t[:]), row(0), by_group(bcast(turned[:, 0, :, b:b + 1], [P, HC, P])),
                                        ALU.mult))
                ch.step(V.tensor_tensor(s_b, s_b, t[:], ALU.add))
                ch.step(V.tensor_tensor(by_group(t[:]), by_group(s_b), row(1), ALU.mult))
                V.tensor_reduce(yT[:, :, b:b + 1].squeeze(2), t[:], AXX, ALU.add).then_inc(s_new, 1)
                dve.wait_ge(s_new, b + 1)
            dve.wait_ge(small_in, 96)
            dve.wait_ge(yT_ps, 1)
            ch.step(V.tensor_tensor(heads(xr[:]), heads(xr[:]), per_head(dskip[:]), ALU.mult))
            ch.step(V.tensor_tensor(y[:], g.ps[0:NS, 0:D], xr[:], ALU.add))
            V.tensor_tensor(y[:], y[:], zgv[:, 0, :], ALU.mult).then_inc(y_done, 1)
            ch.step(V.tensor_scalar(qk[:, 0:GH, :], qk[:, 0:GH, :], QS, None, ALU.mult))
            ch.mark(V.tensor_tensor(qpad[:], bcast(qk[:, 0:GH, :].unsqueeze(3), [P, GH, NS, NS]),
                                    bcast(g.eye8[:].unsqueeze(1), [P, GH, NS, NS]), ALU.mult))
            dve.wait_ge(GS_in, 16)
            dve.wait_ge(e_ready, 1)
            tv = t[:].rearrange("p c n -> p (c n)").rearrange("p (h v) -> p h v", h=GH)
            for b in range(NS):
                gs_b = GS[:, b]
                ch.mark(V.tensor_tensor(gs_b, gs_b, bcast(ela[:, :, b:b + 1], [P, GH, GV]), ALU.mult))
                dve.wait_ge(v_ps, b + 1)
                ch.step(V.tensor_tensor(tv, g.ps[:, 6 * 512:8 * 512].rearrange("p (h v) -> p h v", h=GH),
                                        bcast(qk[:, GH:NQK, b:b + 1], [P, GH, GV]), ALU.mult))
                V.tensor_tensor(gs_b, gs_b, tv, ALU.add).then_inc(g_new, 1)
                dve.wait_ge(g_new, b + 1)
            out.prepare(dve)
            dve.wait_ge(yr, 1)
            for c in range(2):
                cols = slice(c * 512, (c + 1) * 512)
                stt(out=out.cat[0:NS, cols], in0=y[:, cols], scalar=r[:, c:c + 1], in1=ssdn[:, cols],
                    op0=ALU.mult, op1=ALU.mult)
            dve.wait_ge(o_r, 1)
            for h in range(GH):
                ins = stt(out=out.cat[0:NS, D + h * GV:D + (h + 1) * GV],
                          in0=g.ps[0:NS, 4 * 512 + h * GV:4 * 512 + (h + 1) * GV], scalar=r[:, 2 + h:3 + h],
                          in1=glan[:], op0=ALU.mult, op1=ALU.mult)
            ch.step(ins)
            V.tensor_tensor(out.cat[0:NS, D:2 * D], out.cat[0:NS, D:2 * D], zgv[:, 1, :], ALU.mult).then_inc(out.cat_ready, 1)
            out.vector(dve, 0, True)



class Router:

    VSTEPS = 21

    def __init__(self, g, st):
        nc = g.nc
        self.g = g
        sb = lambda n, s, dt=F32: st.enter_context(nc.sbuf_tensor("r_" + n, s, dt))
        sem = lambda n: g.sem("r_" + n)
        self.wq, self.keys = sb("wq", [P, 4, KD, 512]), sb("keys", [P, 2 * PH, P])
        self.h2 = sb("h2", [P, D])
        self.h2T, self.qT = sb("h2T", [P, KD, P]), sb("qT", [P, 2 * PH, P])
        self.work = sb("work", [P, 2 * PH, P])
        self.v, self.iu, self.inum = (sb("v", [P, 2 * PH, TOPK]), sb("iu", [P, 2 * PH, TOPK], U32),
                                      sb("inum", [P, 2 * PH, TOPK]))
        self.top, self.pos = sb("top", [P, PH, TOPK]), sb("pos", [P, PH, TOPK], U32)
        self.part = sb("part", [P, 2, PH, TOPK], U32)
        self.row = sb("row", [P, 2, PH, TOPK])
        self.total, self.e = sb("total", [P, PH]), sb("e", [P, PH, TOPK])
        self.gate, self.num = sb("gate", [P, SLOTS]), sb("num", [P, SLOTS])
        self.idx = sb("idx", [P, SLOTS], U32)
        self.w_in, self.h2_in = sem("wq_in"), sem("h2_in")
        self.h2T_ps, self.h2T_kept, self.q_ps, self.q_kept = sem("h2T_ps"), sem("h2T_kept"), sem("q_ps"), sem("q_kept")
        self.s_ps, self.s_kept, self.vch = sem("s_ps"), sem("s_kept"), sem("vch")
        self.shifted, self.e_ready, self.chosen, self.numbered, self.gated = (
            sem("shifted"), sem("e_ready"), sem("chosen"), sem("numbered"), sem("gated"))

    def load_constants(self, sp):
        sp.dma_start(self.wq[:], self.g.io["w_query"].rearrange("n p k c -> p n k c")).then_inc(self.w_in, 16)
        sp.dma_start(self.keys[:], self.g.io["sub_keys"]).then_inc(self.w_in, 16)

    def tensor(self, pe, n):
        g, nc = self.g, self.g.nc
        pe.wait_ge(self.h2_in, n * 16 + 16)
        for k in range(KD):
            last = nc.tensor.transpose(g.ps[:, 2 * 512 + k * P:2 * 512 + (k + 1) * P], self.h2[:, k * P:(k + 1) * P],
                                       g.ident[:])
        last.then_inc(self.h2T_ps, 1)
        yield
        pe.wait_ge(self.w_in, 32)
        pe.wait_ge(self.h2T_kept, n + 1)

        def scores(b):
            pe.wait_ge(self.q_kept, n * 4 + b + 1)
            for m in range(4):
                u = b * 4 + m
                last = nc.tensor.matmul(g.bank(4 + b, cols=P, at=m * P), self.qT[:, u, :],
                                        self.keys[:, u, :], start=True, stop=True)
            last.then_inc(self.s_ps, 1)

        for b in range(4):
            for m in range(4):
                for k in range(KD):
                    last = nc.tensor.matmul(g.bank(4 + b, cols=P, at=m * P), self.wq[:, b, k, m * P:(m + 1) * P],
                                            self.h2T[:, k, :], start=(k == 0), stop=(k == KD - 1))
                if m == 3:
                    last.then_inc(self.q_ps, 1)
                if m % 2:
                    yield
            if b:
                scores(b - 1)
                yield
        scores(3)
        yield

    def scalar(self, act, n):
        g, A = self.g, self.g.nc.scalar.activation
        act.wait_ge(self.h2T_ps, n + 1)
        A(self.h2T[:].rearrange("p k r -> p (k r)"), g.ps[:, 2 * 512:4 * 512], ACT.Copy).then_inc(self.h2T_kept, 1)
        yield

        def scores(b):
            act.wait_ge(self.s_ps, n * 4 + b + 1)
            A(self.work[:, b * 4:(b + 1) * 4, :].rearrange("p k r -> p (k r)"), g.bank(4 + b),
              ACT.Copy).then_inc(self.s_kept, 1)

        for b in range(4):
            act.wait_ge(self.q_ps, n * 4 + b + 1)
            A(self.qT[:, b * 4:(b + 1) * 4, :].rearrange("p k r -> p (k r)"), g.bank(4 + b), ACT.Copy).then_inc(self.q_kept, 1)
            yield
            if b:
                scores(b - 1)
                yield
        scores(3)
        yield
        act.wait_ge(self.shifted, n + 1)
        A(self.e[:], self.e[:], ACT.Exp).then_inc(self.e_ready, 1)
        yield

    def top16(self, ch, vals, idxs, src, n):
        V = self.g.nc.vector
        for first in (0, 8):
            for u in range(n):
                last = V.max(vals[:, u, first:first + 8], src(u))
            ch.step_apart(last)
            yield
            for u in range(n):
                last = V.max_index(idxs[:, u, first:first + 8], vals[:, u, first:first + 8], src(u))
            ch.step_apart(last)
            yield
            if first == 0:
                for u in range(n):
                    last = V.match_replace(src(u), vals[:, u, 0:8], src(u), LOWEST)
                ch.step_apart(last)
                yield

    def vector(self, dve, n):
        V = self.g.nc.vector
        ch = Chain(dve, self.vch, n * self.VSTEPS)
        wait_apart(dve, self.s_kept, n * 4 + 4)
        yield from self.top16(ch, self.v, self.iu, lambda u: self.work[:, u, :], 2 * PH)
        ch.mark(V.tensor_copy(self.inum[:], self.iu[:]))
        sides = self.v[:].rearrange("p (h s) k -> p h s k", s=2)
        pair = [P, PH, TOPK, TOPK]
        cand = self.work[:].rearrange("p (h s) k -> p h (s k)", s=2)
        square = cand.rearrange("p h (a b) -> p h a b", b=TOPK)
        ch.step_apart(V.tensor_tensor(square, bcast(sides[:, :, 0, :].unsqueeze(3), pair),
                                bcast(sides[:, :, 1, :].unsqueeze(2), pair), ALU.add))
        yield
        yield from self.top16(ch, self.top, self.pos, lambda h: cand[:, h, :], PH)
        V.tensor_tensor(self.e[:], self.top[:], bcast(self.top[:, :, 0:1], [P, PH, TOPK]),
                        ALU.subtract).then_inc(self.shifted, 1)
        ch.mark(V.tensor_single_scalar(self.part[:, 0], self.pos[:], 4, ALU.logical_shift_right))
        ch.step(V.tensor_single_scalar(self.part[:, 1], self.pos[:], TOPK - 1, ALU.bitwise_and))
        yield
        numbers = self.inum[:].rearrange("p (h s) k -> p h s k", s=2)
        for side in range(2):
            hit = square
            ch.step(V.tensor_tensor(hit, bcast(self.g.iota16[:].unsqueeze(1).unsqueeze(1), pair),
                                    bcast(self.part[:, side].unsqueeze(3), pair), ALU.is_equal))
            yield
            ch.step(V.tensor_tensor(hit, hit, bcast(numbers[:, :, side, :].unsqueeze(2), pair), ALU.mult))
            summed = V.tensor_reduce(self.row[:, side], hit, AXX, ALU.add)
            if side == 0:
                ch.step(summed)
                yield
        summed.then_inc(self.chosen, 1)
        dve.wait_ge(self.chosen, n * 2 + 1)
        V.scalar_tensor_tensor(out=self.num[:], in0=self.row[:, 0].rearrange("p h k -> p (h k)"),
                               scalar=float(P), in1=self.row[:, 1].rearrange("p h k -> p (h k)"),
                               op0=ALU.mult, op1=ALU.add).then_inc(self.chosen, 1)
        dve.wait_ge(self.chosen, n * 2 + 2)
        V.tensor_copy(self.idx[:], self.num[:]).then_inc(self.numbered, 1)
        yield
        dve.wait_ge(self.e_ready, n + 1)
        ch.step(V.tensor_reduce(self.total[:], self.e[:], AXX, ALU.add))
        ch.step(V.reciprocal(self.total[:], self.total[:]))
        assert ch.n == self.VSTEPS, ch.n
        V.tensor_tensor(self.gate[:].rearrange("p (h k) -> p h k", k=TOPK), self.e[:],
                        bcast(self.total[:].unsqueeze(2), [P, PH, TOPK]), ALU.mult).then_inc(self.gated, 1)
        yield


class Finish:

    def __init__(self, g, st):
        self.g = g
        sb = lambda n, s: st.enter_context(g.nc.sbuf_tensor("f_" + n, s, F32))
        sem = lambda n: g.sem("f_" + n)
        self.x1, self.gate2, self.final, self.y = sb("x1", [P, D]), sb("gate2", [P, D]), sb("final", [P, D]), sb("y", [P, D])
        self.ms, self.r = sb("ms", [P, 2]), sb("r", [P, 1])
        self.consts_in, self.x1_in, self.ach = sem("consts_in"), sem("x1_in"), sem("ach")
        self.sum_read, self.x2_ready, self.r_ready, self.y_ready = (sem("sum_read"), sem("x2_ready"), sem("r_ready"),
                                                                    sem("y_ready"))
        self.stored, self.y_free = sem("stored"), sem("y_free")

    def vector(self, dve, n, rs):
        g, V = self.g, self.g.nc.vector
        dve.wait_ge(self.x1_in, n * 16 + 16)
        dve.wait_ge(self.y_free, n + 1)
        V.tensor_tensor(self.y[0:rs, :], g.ps[0:rs, 0:D], self.gate2[0:rs, :], ALU.mult).then_inc(self.sum_read, 1)
        dve.wait_ge(self.sum_read, n + 1)
        V.tensor_tensor(self.x1[0:rs, :], self.y[0:rs, :], self.x1[0:rs, :], ALU.add).then_inc(self.x2_ready, 1)
        dve.wait_ge(self.r_ready, n + 1)
        V.scalar_tensor_tensor(out=self.y[0:rs, :], in0=self.x1[0:rs, :], scalar=self.r[0:rs, :],
                               in1=self.final[0:rs, :], op0=ALU.mult, op1=ALU.mult).then_inc(self.y_ready, 1)

    def scalar(self, act, n, rs):
        g, A = self.g, self.g.nc.scalar.activation
        act.wait_ge(self.x2_ready, n + 1)
        ch = Chain(act, self.ach, n * 2)
        ch.step(A(self.y[0:rs, :], self.x1[0:rs, :], ACT.Square, accum_out=self.ms[0:rs, 0:1]))
        ch.step(A(self.ms[0:rs, 1:2], self.ms[0:rs, 0:1], ACT.Ln, scale=1.0 / D, bias=g.eps[0:rs, :]))
        A(self.r[0:rs, :], self.ms[0:rs, 1:2], ACT.Exp, scale=-0.5).then_inc(self.r_ready, 1)
        act.wait_ge(self.r_ready, n + 1)


PE_PIECES = {q: 1 for q in range(1, 14)}
ACT_PIECES = {q: 1 for q in (2, 4, 6, 7, 9, 10, 12, 13, 14, 24)}
DVE_PIECES = {q: 1 if q < 19 else 2 for q in range(15, 26)}


def drive(pieces, count):
    for _ in range(count):
        next(pieces, None)


def experts(g):
    nc, io = g.nc, g.io
    NG = SLOTS // GROUP
    with ExitStack() as st:
        sb = lambda n, s, dt=F32: st.enter_context(nc.sbuf_tensor("e_" + n, s, dt))
        sem = lambda n: g.sem("e_" + n)
        rt, fin = Router(g, st), Finish(g, st)
        buf = [sb(f"buf{s}", [P, 2 * D]) for s in range(RING)]
        idx, gate, h2 = sb("idx", [P, SLOTS], U32), sb("gate", [P, SLOTS]), sb("h2", [P, D])
        dots, acts, wts = sb("dots", [P, SLOTS]), sb("acts", [P, SLOTS]), sb("wts", [P, SLOTS])
        diag = sb("diag", [P, RING, P])
        h2_kept, idx_kept, generated = sem("h2_kept"), sem("idx_kept"), sem("generated")
        landed = [sem(f"landed{s}") for s in range(RING)]
        dotted, wch, weighed, summed = sem("dotted"), sem("wch"), sem("weighed"), sem("summed")
        idxT, turned = sb("idxT", [P, NS], U32), sb("turned", [P, 2, NS])
        wpad = sb("wpad", [P, NS, NS])
        turn_ps, turn_kept, idxT_ready, spread_in, gates_in = (sem("turn_ps"), sem("turn_kept"), sem("idxT_ready"),
                                                               sem("spread_in"), sem("gates_in"))
        s_dotted, s_acted, s_weighed, s_summed = sem("s_dotted"), sem("s_acted"), sem("s_weighed"), sem("s_summed")
        wide = rt.wq[:].rearrange("p n k c -> p (n k c)")
        spread = lambda b: wide[:, b * D:(b + 1) * D]
        block = st.enter_context(nc.Block())
        PER = 16 * (SLOTS // RING)

        @block.sync
        def _(sp):
            sp.sem_inc(fin.y_free, 1)
            sp.dma_start(rt.h2[:], g.h2_d[0:P, :]).then_inc(rt.h2_in, 16)
            rt.load_constants(sp)
            sp.dma_start(fin.gate2[:], g.mod_d[NS, 5 * D:6 * D].partition_broadcast(P)).then_inc(fin.consts_in, 16)
            sp.dma_start(fin.final[:], io["norm_final"].partition_broadcast(P)).then_inc(fin.consts_in, 16)
            with sp.Fori(0, NT) as n:
                sp.dma_start(fin.x1[:], g.x1_d[bass.ds(n * P, P), :]).then_inc(fin.x1_in, 16)
                sp.wait_ge(h2_kept, n + 1)
                sp.dma_start(rt.h2[:], g.h2_d[bass.ds(n * P + P, P), :]).then_inc(rt.h2_in, 16)
                sp.wait_ge(fin.y_ready, n + 1)
                sp.dma_start(io["y_p"][bass.ds(n * P, P), :], fin.y[:]).then_inc(fin.stored, 16)
                sp.wait_ge(fin.stored, n * 16 + 16)
                sp.sem_inc(fin.y_free, 1)
            sp.dma_start(fin.x1[0:NS, :], g.x1_d[SEQ:ROWS, :]).then_inc(fin.x1_in, 16)
            sp.dma_start(fin.gate2[0:NS, :], g.mod_d[0:NS, 5 * D:6 * D]).then_inc(gates_in, 16)
            sp.wait_ge(rt.q_ps, 4 * (NT + 1))
            for b in range(NS):
                sp.dma_start(spread(b), g.h2_d[SEQ + b, :].partition_broadcast(P)).then_inc(spread_in, 16)
            sp.wait_ge(fin.y_ready, NT + 1)
            sp.dma_start(io["y_s"], fin.y[0:NS, :]).then_inc(fin.stored, 16)
            sp.wait_ge(fin.stored, 16 * (NT + 1))

        @block.gpsimd
        def _(pool):
            def gather(s, numbers, **kw):
                return pool.indirect_dma_start(out=buf[s][:], out_offset=None, in_=io["experts"],
                                               in_offset=bass.IndirectOffsetOnAxis(ap=numbers, axis=0), **kw)

            with pool.Fori(0, NT) as n:
                wait_apart(pool, rt.numbered, n + 1)
                nc.gpsimd.tensor_copy(idx[:, 0:SLOTS - RING], rt.idx[:, 0:SLOTS - RING]).then_inc(idx_kept, 1)
                wait_apart(pool, idx_kept, n * 2 + 1)
                for k in range(SLOTS):
                    wait_apart(pool, summed, n * SLOTS + k + 1)
                    if k == RING:
                        nc.gpsimd.tensor_copy(idx[:, SLOTS - RING:], rt.idx[:, SLOTS - RING:]).then_inc(idx_kept, 1)
                        wait_apart(pool, idx_kept, n * 2 + 2)
                    gather(k % RING, idx[:, k:k + 1]).then_inc(landed[k % RING], 16)
            pool.wait_ge(idxT_ready, 1)
            for b in range(NS):
                wait_apart(pool, summed, NT * SLOTS + b + 1)
                gather(b % RING, idxT[:, b:b + 1]).then_inc(landed[b % RING], 16)

        @block.tensor
        def _(pe):
            pe.sem_inc(summed, RING)
            drive(rt.tensor(pe, 0), 99)
            with pe.Fori(0, NT) as n:
                route = rt.tensor(pe, n + 1)
                for k in range(SLOTS):
                    if k == 0:
                        pe.wait_ge(fin.y_free, n + 1)
                    pe.wait_ge(weighed, n * SLOTS + k + 1)
                    for cols in range(2):
                        last = nc.tensor.matmul(g.bank(cols), diag[:, k % RING, :],
                                                buf[k % RING][:, D + cols * 512:D + (cols + 1) * 512],
                                                start=(k == 0), stop=(k == SLOTS - 1))
                    last.then_inc(summed, 1)
                    if k % GROUP == GROUP - 1:
                        drive(route, PE_PIECES.get(k // GROUP, 0))
            pe.wait_ge(rt.gated, NT + 1)
            for m, src in enumerate((rt.num, rt.gate)):
                last = nc.tensor.transpose(g.bank(2, cols=NS, at=m * NS), src[0:NS, :], g.ident[0:NS, 0:NS])
            last.then_inc(turn_ps, 1)
            pe.wait_ge(fin.sum_read, NT)
            for b in range(NS):
                pe.wait_ge(s_weighed, b + 1)
                for cols in range(2):
                    last = nc.tensor.matmul(g.bank(cols, rows=NS), wpad[:, b, :],
                                            buf[b % RING][:, D + cols * 512:D + (cols + 1) * 512],
                                            start=(b == 0), stop=(b == NS - 1))
                last.then_inc(s_summed, 1)

        @block.scalar
        def _(act):
            A = nc.scalar.activation
            drive(rt.scalar(act, 0), 99)
            with act.Fori(0, NT) as n:
                ch = Chain(act, wch, n * (1 + 2 * NG))
                route = rt.scalar(act, n + 1)
                act.wait_ge(rt.gated, n + 1)
                ch.step(A(gate[:], rt.gate[:], ACT.Copy))
                for q in range(NG):
                    ks = slice(q * GROUP, (q + 1) * GROUP)
                    act.wait_ge(dotted, n * SLOTS + (q + 1) * GROUP)
                    ch.step(A(acts[:, ks], dots[:, ks], ACT.Gelu))
                    for k in range(q * GROUP, (q + 1) * GROUP):
                        last = A(wts[:, k:k + 1], acts[:, k:k + 1], ACT.Copy, scale=gate[:, k:k + 1])
                    ch.step(last)
                    for k in range(q * GROUP, (q + 1) * GROUP):
                        act.wait_ge(summed, n * SLOTS + k + 1)
                        A(diag[:, k % RING, :], g.ident[:], ACT.Copy, scale=wts[:, k:k + 1]).then_inc(weighed, 1)
                    drive(route, ACT_PIECES.get(q, 0))
                fin.scalar(act, n, P)
            act.wait_ge(turn_ps, 1)
            A(turned[:].rearrange("p a b -> p (a b)"), g.bank(2, cols=2 * NS), ACT.Copy).then_inc(turn_kept, 1)
            for b in range(NS):
                act.wait_ge(s_dotted, b + 1)
                A(wts[:, b:b + 1], dots[:, b:b + 1], ACT.Gelu).then_inc(s_acted, 1)
            fin.scalar(act, NT, NS)

        @block.vector
        def _(dve):
            V = nc.vector

            def dot(s, row, out, sem):
                down = buf[s][:, 0:D]
                V.scalar_tensor_tensor(out=down, in0=down, scalar=1.0, in1=row, op0=ALU.mult, op1=ALU.mult,
                                       accum_out=out).then_inc(sem, 1)

            drive(rt.vector(dve, 0), 99)
            dve.wait_ge(fin.consts_in, 32)
            with dve.Fori(0, NT) as n:
                route = rt.vector(dve, n + 1)
                V.tensor_copy(h2[:], rt.h2[:]).then_inc(h2_kept, 1)
                dve.wait_ge(h2_kept, n + 1)
                for k in range(SLOTS):
                    dve.wait_ge(landed[k % RING], n * PER + 16 * (k // RING) + 16)
                    dot(k % RING, h2[:], dots[:, k:k + 1], dotted)
                    if k % GROUP == GROUP - 1:
                        drive(route, DVE_PIECES.get(k // GROUP, 0))
                dve.wait_ge(summed, n * SLOTS + SLOTS + RING)
                fin.vector(dve, n, P)
            dve.wait_ge(turn_kept, 1)
            V.tensor_copy(idxT[:], turned[:, 0, :]).then_inc(idxT_ready, 1)
            dve.wait_ge(spread_in, 16 * NS)
            dve.wait_ge(gates_in, 16)

            def weigh(b):
                dve.wait_ge(s_acted, b + 1)
                V.scalar_tensor_tensor(out=wpad[:, b, :], in0=g.eye8[:, b, :], scalar=wts[:, b:b + 1],
                                       in1=bcast(turned[:, 1, b:b + 1], [P, NS]), op0=ALU.mult,
                                       op1=ALU.mult).then_inc(s_weighed, 1)

            for b in range(NS):
                dve.wait_ge(landed[b % RING], NT * PER + 16 * (b // RING + 1))
                dot(b % RING, spread(b), dots[:, b:b + 1], s_dotted)
                if b:
                    weigh(b - 1)
            weigh(NS - 1)
            dve.wait_ge(s_summed, NS)
            fin.vector(dve, NT, NS)


def build(nc, io):
    with ExitStack() as stack:
        g = Prog(nc, stack, io)
        g.phase(modulation)
        with ExitStack() as st:
            hT = st.enter_context(nc.sbuf_tensor("hT", [P, KD, ROWS], F32))
            g.phase(norm_in, hT)
            g.phase(projections, hT)
        g.phase(mix_sample)
        g.phase(mix_prompt)
        g.phase(experts)


def laid_out(np, x):
    f = {k: np.asarray(v) for k, v in x.items()}
    chunks = lambda w, n: w.reshape(KD, P, w.shape[1] // n, n).transpose(2, 1, 0, 3)
    wide = lambda w: w.reshape(w.shape[0] // P, P, w.shape[1]).transpose(1, 0, 2)
    w_in = f["w_in"][0]
    cuts = np.cumsum([0, D, NXBC * P, HS, GH * P, GH * P, D, D, 16])
    z, xbc, dt, q, k, v, go, gate = (w_in[:, a:b] for a, b in zip(cuts[:-1], cuts[1:]))
    per_chunk = lambda a: a.reshape(-1, NXBC, P).transpose(1, 2, 0)
    heads = lambda s: s.transpose(3, 0, 1, 2)
    return {
        "c_all": np.concatenate([f["c_sample"], f["c_prompt"]]),
        "w_mod": chunks(f["w_mod"][0], 512), "b_mod": f["b_mod"][0],
        "norm_mix": f["norm_mix"][0], "norm_ffn": f["norm_ffn"][0], "norm_final": f["norm_final"],
        "x_prompt": f["x_prompt"][0], "x_sample": f["x_sample"][:, 0],
        "w_chan": chunks(np.concatenate([xbc, q, k], axis=1), P),
        "w_rows": chunks(np.concatenate([z, go, v], axis=1), 512),
        "w_dt": wide(dt), "w_gate": wide(gate),
        "conv_par": np.concatenate([per_chunk(f["w_conv"][0]), per_chunk(f["b_conv"][0]),
                                    per_chunk(f["state_conv"][0].transpose(1, 0, 2))], axis=2),
        "dt_bias": f["dt_bias"][0], "a_log": f["a_log"][0],
        "w_gate_up": f["w_gate_up"][0], "b_gate": f["b_gate"][0].reshape(GH, P).T,
        "state_ssm": f["state_ssm"][0].reshape(NS, HS // 2, P, P).transpose(2, 0, 1, 3),
        "state_gla": f["state_gla"][0].transpose(2, 0, 1, 3),
        "d_skip": f["d_skip"][0], "ssd_norm": f["ssd_norm"][0], "gla_norm": f["gla_norm"][0],
        "w_out": wide(f["w_out"][0]),
        "w_query": chunks(f["w_query"][0], 512),
        "sub_keys": np.stack([f["sub_keys1"][0], f["sub_keys2"][0]], axis=1).reshape(2 * PH, P, P).transpose(2, 0, 1),
        "experts": np.concatenate([f["expert_down"][0], f["expert_up"][0]], axis=1),
    }


OUTS = {"y_p": (SEQ, D), "y_s": (NS, D), "conv_p": (NXBC, P, 3), "ssm_p": (P, HS * HP), "gla_p": (P, GH * GV),
        "conv_s": (NXBC, P, 3 * NS), "ssm_s": (P, NS, HS // 2, P), "gla_s": (P, NS, GH, GV)}


def program(nc, arrays):
    io = {}
    for n, a in arrays.items():
        io[n] = nc.dram_tensor(f"in_{n}", a.shape, mybir.dt.from_np(a.dtype), kind="ExternalInput").ap()
    for n, shape in OUTS.items():
        io[n] = nc.dram_tensor(f"out_{n}", shape, F32, kind="ExternalOutput").ap()
    build(nc, io)


def kernel(**inputs):
    import numpy as np
    import concourse.bacc as bacc
    from concourse.bass_utils import run_bass_kernel_spmd

    nc = bacc.Bacc("TRN2", target_bir_lowering=False, num_devices=1)
    arrays = {n: np.ascontiguousarray(a) for n, a in laid_out(np, inputs).items()}
    program(nc, arrays)
    r = run_bass_kernel_spmd(nc, [{f"in_{n}": a for n, a in arrays.items()}], core_ids=[0]).results[0]
    o = {n: np.asarray(r[f"out_{n}"]) for n in OUTS}
    state = lambda a: a.reshape(NXBC * P, 3, -1).transpose(2, 1, 0)[None]
    return (o["y_p"][None], o["y_s"][:, None], state(o["conv_p"]),
            o["ssm_p"].T.reshape(1, 1, HS, HP, P), o["gla_p"].reshape(P, GH, GV).transpose(1, 0, 2)[None, None],
            state(o["conv_s"]), o["ssm_s"].transpose(1, 2, 0, 3).reshape(1, NS, HS, HP, P),
            o["gla_s"].transpose(1, 2, 0, 3)[None])
```

```python
from contextlib import ExitStack

import concourse.bass as bass
from concourse import mybir

F32 = mybir.dt.float32
U32 = mybir.dt.uint32
ACT = mybir.ActivationFunctionType
ALU = mybir.AluOpType
AXX = mybir.AxisListType.X

P = 128
D = 1024
KD = D // P
SEQ = 1024
NT = SEQ // P
NS = 8
ROWS = SEQ + NS
TILED = (NT + 1) * P
THIRD = ROWS // 3
MODS = 6 * D
NXBC = 12
NQK = 8
HS = 16
HP = 64
GH = 4
GV = 256
HALF = 64
PH = 8
TOPK = 16
SLOTS = PH * TOPK
RING = 8
GROUP = 4
EPS = 1e-6
LOWEST = -3.0e38


def bcast(ap, shape):
    return ap.to_broadcast(shape)


def wait_apart(eng, sem, value):
    eng.wait_ge(sem, value)
    eng.nop(nofuse=True)


class Chain:

    def __init__(self, eng, sem, base=0):
        self.eng, self.sem, self.base, self.n = eng, sem, base, 0

    def step(self, ins):
        ins.then_inc(self.sem, 1)
        self.n += 1
        self.eng.wait_ge(self.sem, self.base + self.n)

    def step_apart(self, ins):
        ins.then_inc(self.sem, 1)
        self.n += 1
        wait_apart(self.eng, self.sem, self.base + self.n)

    def mark(self, ins):
        ins.then_inc(self.sem, 1)
        self.n += 1

    def join(self):
        self.eng.wait_ge(self.sem, self.base + self.n)


class Prog:

    def __init__(self, nc, stack, io):
        self.nc, self.io = nc, io
        self.stack = stack
        d = lambda name, shape: nc.dram_tensor(name, shape, F32, kind="Internal").ap()
        self.mod_d = d("mod_d", (NS + 1, MODS))
        self.proj_d = d("proj_d", (ROWS, 3, D))
        self.xbc_d = d("xbc_d", (NXBC, P, ROWS))
        self.qk_d = d("qk_d", (NQK, P, ROWS))
        self.cum_d = d("cum_d", (GH, P, ROWS))
        self.x1_d = d("x1_d", (ROWS, D))
        self.h2_d = d("h2_d", (TILED, D))
        s = lambda name, shape: stack.enter_context(nc.sbuf_tensor(name, shape, F32))
        self.ident = s("ident", [P, P])
        self.tri = s("tri", [P, P])
        self.later = s("later", [P, P])
        self.blk = s("blk", [P, P])
        self.ones = s("ones", [P, P])
        self.sel8 = s("sel8", [NS, NS, P])
        self.eye8 = s("eye8", [P, NS, NS])
        self.iota16 = s("iota16", [P, TOPK])
        self.eps = s("eps", [P, 1])
        self.dt = s("dt", [P, NT + 1, HS])
        self.dta = s("dta", [P, NT + 1, HS])
        self.ecum = s("ecum", [P, NT, HS])
        self.etoend = s("etoend", [P, NT, HS])
        self.etot = s("etot", [P, NT, HS])
        self.edta = s("edta", [NS, HS])
        self.ps = stack.enter_context(nc.psum_tensor("ps", [P, 8 * 512], F32))

    def sem(self, name):
        handle = self.nc.alloc_semaphore(name=name)
        self.sems.append(handle)
        return handle

    def phase(self, emit, *args):
        self.sems = []
        emit(self, *args)
        self.nc.clear_and_free_semaphores(self.sems)
        self.nc.all_engine_barrier()

    def bank(self, n, rows=P, cols=512, at=0):
        return self.ps[0:rows, n * 512 + at:n * 512 + at + cols]


def modulation(g, x, r):
    nc, io = g.nc, g.io
    NB = MODS // 512
    with ExitStack() as st:
        sb = lambda n, s: st.enter_context(nc.sbuf_tensor(n, s, F32))
        sem = lambda n: g.sem(n)
        c_sb = sb("c_sb", [NS + 1, D])
        sc_sb = sb("sc_sb", [NS + 1, D])
        cT = sb("cT", [P, KD, NS + 1])
        w = sb("w_mod_sb", [P, 2, KD, 512])
        bm = sb("bm", [NS + 1, MODS])
        mod = sb("mod", [NS + 1, MODS])
        sq, ms, lr = sb("m_sq", [P, D]), sb("m_ms", [P, NT + 1]), sb("m_lr", [P, NT + 1])
        x_in, xs_in, ms_set, squared, logged, r_ready = (sem("m_x_in"), sem("m_xs_in"), sem("m_ms_set"),
                                                         sem("m_squared"), sem("m_logged"), sem("m_r_ready"))
        c_in, bm_in = sem("m_c_in"), sem("m_bm_in")
        w_in = [sem("m_w_in0"), sem("m_w_in1")]
        consts0, consts = sem("m_consts0"), sem("m_consts")
        silu_done, cT_ps, cT_done = sem("m_silu_done"), sem("m_cT_ps"), sem("m_cT_done")
        prod, summed, stored = sem("m_prod"), sem("m_summed"), sem("m_stored")
        block = st.enter_context(nc.Block())

        @block.sync
        def _(sp):
            sp.dma_start(c_sb[:], io["c_all"]).then_inc(c_in, 16)
            sp.dma_start(bm[:], io["b_mod"].partition_broadcast(NS + 1)).then_inc(bm_in, 16)
            for b in range(2):
                sp.dma_start(w[:, b], io["w_mod"][b]).then_inc(w_in[b], 16)
            sp.dma_start(x[:, 0:NT, :], io["x_prompt"].rearrange("(t p) d -> p t d", p=P)).then_inc(x_in, 16)
            sp.dma_start(x[0:NS, NT, :], io["x_sample"]).then_inc(xs_in, 16)
            with sp.Fori(0, NB // 2 - 1) as i:
                for b in range(2):
                    sp.wait_ge(prod, i * 2 + b + 1)
                    sp.dma_start(w[:, b], io["w_mod"][bass.ds(i * 2 + b + 2, 1)].squeeze(0)).then_inc(w_in[b], 16)
            sp.wait_ge(summed, NB)
            sp.dma_start(g.mod_d, mod[:]).then_inc(stored, 16)
            sp.wait_ge(stored, 16)

        @block.gpsimd
        def _(pool):
            for t, v in ((g.ident, 0.0), (g.tri, 1.0), (g.later, 1.0), (g.ones, 1.0),
                         (g.sel8, 1.0), (g.eye8, 1.0), (g.eps, EPS)):
                nc.gpsimd.memset(t[:], v).then_inc(consts0, 1)
            nc.gpsimd.iota(g.iota16[:], [[1, TOPK]], base=0, channel_multiplier=0,
                           allow_small_or_imprecise_dtypes=True).then_inc(consts0, 1)
            pool.wait_ge(consts0, 8)
            sel = nc.gpsimd.affine_select
            sel(out=g.ident[:], in_=g.ident[:], compare_op=ALU.not_equal, fill=1.0, base=0,
                pattern=[[-1, P]], channel_multiplier=1).then_inc(consts, 1)
            sel(out=g.tri[:], in_=g.tri[:], compare_op=ALU.is_ge, fill=0.0, base=0,
                pattern=[[1, P]], channel_multiplier=-1).then_inc(consts, 1)
            sel(out=g.later[:], in_=g.later[:], compare_op=ALU.is_gt, fill=0.0, base=0,
                pattern=[[-1, P]], channel_multiplier=1).then_inc(consts, 1)
            sel(out=g.sel8[:], in_=g.sel8[:], compare_op=ALU.is_equal, fill=0.0, base=0,
                pattern=[[-1, NS], [0, P]], channel_multiplier=1).then_inc(consts, 1)
            sel(out=g.eye8[:], in_=g.eye8[:], compare_op=ALU.is_equal, fill=0.0, base=0,
                pattern=[[-1, NS], [1, NS]], channel_multiplier=0).then_inc(consts, 1)
            pool.wait_ge(consts, 5)
            nc.gpsimd.tensor_copy(g.blk[:], g.tri[:]).then_inc(consts, 1)
            pool.wait_ge(consts, 6)
            nc.gpsimd.memset(g.blk[0:HALF, HALF:P], 0.0).then_inc(consts, 1)
            pool.wait_ge(consts, 7)

        @block.scalar
        def _(act):
            act.wait_ge(c_in, 16)
            nc.scalar.activation(sc_sb[:], c_sb[:], ACT.Silu).then_inc(silu_done, 1)
            act.wait_ge(cT_ps, 1)
            nc.scalar.activation(cT[:].rearrange("p k r -> p (k r)"), g.bank(0, cols=KD * (NS + 1)),
                                 ACT.Copy).then_inc(cT_done, 1)
            act.wait_ge(ms_set, 1)
            act.wait_ge(x_in, 16)
            act.wait_ge(xs_in, 16)
            for t in range(NT + 1):
                rs = P if t < NT else NS
                nc.scalar.activation(sq[0:rs, :], x[0:rs, t, :], ACT.Square,
                                     accum_out=ms[0:rs, t:t + 1]).then_inc(squared, 1)
                act.wait_ge(squared, t + 1)
            act.wait_ge(consts0, 8)
            nc.scalar.activation(lr[:], ms[:], ACT.Ln, scale=1.0 / D, bias=g.eps[:]).then_inc(logged, 1)
            act.wait_ge(logged, 1)
            nc.scalar.activation(r[:], lr[:], ACT.Exp, scale=-0.5).then_inc(r_ready, 1)
            act.wait_ge(r_ready, 1)

        @block.tensor
        def _(pe):
            pe.wait_ge(silu_done, 1)
            pe.wait_ge(consts, 1)
            for k in range(KD):
                last = nc.tensor.transpose(g.bank(0, cols=NS + 1, at=k * (NS + 1)),
                                           sc_sb[:, k * P:(k + 1) * P], g.ident[0:NS + 1, 0:NS + 1])
            last.then_inc(cT_ps, 1)
            pe.wait_ge(cT_done, 1)
            with pe.Fori(0, NB // 2) as i:
                for b in range(2):
                    pe.wait_ge(w_in[b], i * 16 + 16)
                    for k in range(KD):
                        last = nc.tensor.matmul(g.bank(2 + b, rows=NS + 1), cT[:, k, :], w[:, b, k, :],
                                                start=(k == 0), stop=(k == KD - 1))
                    last.then_inc(prod, 1)
                pe.wait_ge(summed, i * 2 + 2)

        @block.vector
        def _(dve):
            nc.vector.memset(ms[:], 0.0).then_inc(ms_set, 1)
            dve.wait_ge(bm_in, 16)
            with dve.Fori(0, NB // 2) as i:
                for b in range(2):
                    dve.wait_ge(prod, i * 2 + b + 1)
                    cols = bass.ds((i * 2 + b) * 512, 512)
                    nc.vector.tensor_tensor(mod[:, cols], g.bank(2 + b, rows=NS + 1), bm[:, cols],
                                            ALU.add).then_inc(summed, 1)


def norm_in(g, x, r, hT):
    nc, io = g.nc, g.io
    with ExitStack() as st:
        sb = lambda n, s: st.enter_context(nc.sbuf_tensor(n, s, F32))
        sem = lambda n: g.sem(n)
        h = [sb(f"n_h{b}", [P, D]) for b in range(2)]
        scale = [sb("n_scale_s", [P, D]), sb("n_scale_p", [P, D])]
        shift = [sb("n_shift_s", [P, D]), sb("n_shift_p", [P, D])]
        norm = sb("n_norm", [P, D])
        mods_in, scales = sem("n_mods_in"), sem("n_scales")
        normed, hchain = sem("n_normed"), sem("n_hchain")
        flipped, kept = sem("n_flipped"), sem("n_kept")
        block = st.enter_context(nc.Block())

        @block.sync
        def _(sp):
            sp.dma_start(norm[:], io["norm_mix"].partition_broadcast(P)).then_inc(mods_in, 16)
            sp.dma_start(shift[1][:], g.mod_d[NS, 0:D].partition_broadcast(P)).then_inc(mods_in, 16)
            sp.dma_start(scale[1][:], g.mod_d[NS, D:2 * D].partition_broadcast(P)).then_inc(mods_in, 16)
            sp.dma_start(shift[0][0:NS, :], g.mod_d[0:NS, 0:D]).then_inc(mods_in, 16)
            sp.dma_start(scale[0][0:NS, :], g.mod_d[0:NS, D:2 * D]).then_inc(mods_in, 16)

        def each(eng, tile):
            for b in range(2):
                tile(b, b, P, False)
            with eng.Fori(1, NT // 2) as i:
                for b in range(2):
                    tile(i * 2 + b, b, P, True)
            tile(NT, 0, NS, True)

        @block.scalar
        def _(act):
            def tile(n, b, rs, later):
                act.wait_ge(flipped, n + 1)
                src = g.ps[:, 2 * b * 512:2 * b * 512 + KD * P].rearrange("p (k r) -> p k r", r=P)[:, :, 0:rs]
                cols = slice(SEQ, ROWS) if rs == NS else bass.ds(n * P, P)
                nc.scalar.activation(hT[:, :, cols], src, ACT.Copy).then_inc(kept, 1)

            each(act, tile)
            act.wait_ge(kept, NT + 1)

        @block.vector
        def _(dve):
            dve.wait_ge(mods_in, 80)
            for kind, rs in ((1, P), (0, NS)):
                s = scale[kind][0:rs, :]
                nc.vector.scalar_tensor_tensor(out=s, in0=s, scalar=1.0, in1=norm[0:rs, :],
                                               op0=ALU.add, op1=ALU.mult).then_inc(scales, 1)
            dve.wait_ge(scales, 2)

            def tile(n, b, rs, later):
                kind = 0 if rs == NS else 1
                if later:
                    dve.wait_ge(flipped, n - 1)
                row = x[0:rs, bass.ds(n, 1), :].squeeze(1)
                nc.vector.scalar_tensor_tensor(out=h[b][0:rs, :], in0=row, scalar=r[0:rs, bass.ds(n, 1)],
                                               in1=scale[kind][0:rs, :], op0=ALU.mult,
                                               op1=ALU.mult).then_inc(hchain, 1)
                dve.wait_ge(hchain, n + 1)
                nc.vector.tensor_tensor(h[b][0:rs, :], h[b][0:rs, :], shift[kind][0:rs, :], ALU.add).then_inc(normed, 1)

            each(dve, tile)

        @block.tensor
        def _(pe):
            def tile(n, b, rs, later):
                pe.wait_ge(normed, n + 1)
                if later:
                    pe.wait_ge(kept, n - 1)
                for k in range(KD):
                    at = 2 * b * 512 + k * P
                    last = nc.tensor.transpose(g.ps[:, at:at + rs], h[b][0:rs, k * P:(k + 1) * P],
                                               g.ident[0:rs, 0:rs])
                last.then_inc(flipped, 1)

            each(pe, tile)


def projections(g, hT):
    nc, io = g.nc, g.io
    with ExitStack() as st:
        sb = lambda n, s: st.enter_context(nc.sbuf_tensor(n, s, F32))
        sem = lambda n: g.sem(n)
        NPAR = 4 + 1 + 3 * NS
        w = [sb(f"p_w{b}", [P, KD, P]) for b in range(2)]
        par = [sb(f"p_par{b}", [P, NPAR]) for b in range(2)]
        raw = [sb(f"p_raw{b}", [P, 3 + ROWS]) for b in range(2)]
        acc = [sb(f"p_acc{b}", [P, ROWS]) for b in range(2)]
        res = [sb(f"p_res{b}", [P, ROWS]) for b in range(2)]
        w_in, par_in = [sem("p_w_in0"), sem("p_w_in1")], [sem("p_par_in0"), sem("p_par_in1")]
        cleared, chan, evac = sem("p_cleared"), sem("p_chan"), sem("p_evac")
        convd, cchain, silud, cstored = sem("p_convd"), sem("p_cchain"), sem("p_silud"), sem("p_cstored")
        bstored = [sem("p_bstored0"), sem("p_bstored1")]
        NC = NXBC + NQK
        STEPS = 7

        with nc.Block() as block:
            @block.sync
            def _(sp):
                for b in range(2):
                    sp.dma_start(w[b][:], io["w_chan"][b]).then_inc(w_in[b], 16)
                with sp.Fori(0, NC // 2 - 1) as i:
                    for b in range(2):
                        sp.wait_ge(chan, i * 2 + b + 1)
                        sp.dma_start(w[b][:], io["w_chan"][bass.ds(i * 2 + b + 2, 1)].squeeze(0)).then_inc(w_in[b], 16)

            @block.gpsimd
            def _(pool):
                for b in range(2):
                    pool.dma_start(par[b][:], io["conv_par"][b]).then_inc(par_in[b], 16)

                def store(i, more):
                    for b in range(2):
                        c = i * 2 + b
                        one = lambda t: t[bass.ds(c, 1)].squeeze(0)
                        wait_apart(pool, silud, c + 1)
                        pool.dma_start(one(g.xbc_d), res[b][:]).then_inc(bstored[b], 16)
                        pool.dma_start(one(io["conv_p"]), raw[b][:, SEQ:SEQ + 3]).then_inc(bstored[b], 16)
                        pool.dma_start(one(io["conv_s"])[:, 0:2 * NS], par[b][:, 5 + NS:5 + 3 * NS]).then_inc(bstored[b], 16)
                        pool.dma_start(one(io["conv_s"])[:, 2 * NS:3 * NS], raw[b][:, SEQ + 3:ROWS + 3]).then_inc(bstored[b], 16)
                        if more:
                            wait_apart(pool, bstored[b], i * 64 + 64)
                            pool.dma_start(par[b][:], io["conv_par"][bass.ds(c + 2, 1)].squeeze(0)).then_inc(par_in[b], 16)

                with pool.Fori(0, NXBC // 2 - 1) as i:
                    store(i, True)
                store(NXBC // 2 - 1, False)
                with pool.Fori(0, NQK // 2) as i:
                    for b in range(2):
                        wait_apart(pool, evac, i * 2 + b + NXBC + 1)
                        pool.dma_start(g.qk_d[bass.ds(i * 2 + b, 1)].squeeze(0), raw[b][:, 3:3 + ROWS]).then_inc(bstored[b], 16)
                        wait_apart(pool, bstored[b], i * 16 + 16 + 64 * (NXBC // 2))

            @block.tensor
            def _(pe):
                def chunk(b, c, wait):
                    pe.wait_ge(w_in[b], wait)
                    for j in range(3):
                        for k in range(KD):
                            last = nc.tensor.matmul(g.bank(3 * b + j, cols=THIRD), w[b][:, k, :],
                                                    hT[:, k, j * THIRD:(j + 1) * THIRD],
                                                    start=(k == 0), stop=(k == KD - 1))
                    last.then_inc(chan, 1)

                chunk(0, 0, 16)
                chunk(1, 1, 16)
                with pe.Fori(1, NC // 2) as i:
                    for b in range(2):
                        pe.wait_ge(evac, i * 2 + b - 1)
                        chunk(b, i * 2 + b, i * 16 + 16)

            @block.scalar
            def _(act):
                def evacuate(b, c):
                    act.wait_ge(chan, c + 1)
                    src = g.ps[:, 3 * b * 512:(3 * b + 3) * 512].rearrange("p (j c) -> p j c", c=512)[:, :, 0:THIRD]
                    nc.scalar.activation(raw[b][:, 3:3 + ROWS].rearrange("p (j c) -> p j c", c=THIRD), src,
                                         ACT.Copy).then_inc(evac, 1)

                def silu(b, c):
                    act.wait_ge(convd, c + 1)
                    nc.scalar.activation(res[b][:], acc[b][:], ACT.Silu).then_inc(silud, 1)

                act.wait_ge(cleared, 2)
                evacuate(0, 0)
                evacuate(1, 1)
                silu(0, 0)
                silu(1, 1)
                with act.Fori(1, NXBC // 2) as i:
                    for b in range(2):
                        act.wait_ge(bstored[b], i * 64)
                        evacuate(b, i * 2 + b)
                    for b in range(2):
                        silu(b, i * 2 + b)
                with act.Fori(0, NQK // 2) as i:
                    for b in range(2):
                        act.wait_ge(bstored[b], i * 16 + 64 * (NXBC // 2))
                        evacuate(b, i * 2 + b + NXBC)
                act.wait_ge(evac, NC)

            @block.vector
            def _(dve):
                for b in range(2):
                    nc.vector.memset(raw[b][:, 0:3], 0.0).then_inc(cleared, 1)
                with dve.Fori(0, NXBC // 2) as i:
                    for b in range(2):
                        c = i * 2 + b
                        ch = Chain(dve, cchain, c * STEPS)
                        dve.wait_ge(par_in[b], i * 16 + 16)
                        dve.wait_ge(evac, c + 1)
                        tap = lambda j: par[b][:, j:j + 1]
                        late, new = acc[b][:, SEQ:ROWS], raw[b][:, SEQ + 3:ROWS + 3]
                        body = acc[b][:, 0:SEQ]
                        ch.mark(nc.vector.tensor_scalar(body, raw[b][:, 0:SEQ], tap(0), tap(4), ALU.mult, ALU.add))
                        ch.step(nc.vector.tensor_scalar(late, new, tap(3), tap(4), ALU.mult, ALU.add))
                        for j in range(1, 4):
                            old = par[b][:, 5 + (j - 1) * NS:5 + j * NS]
                            mul_add = nc.vector.scalar_tensor_tensor
                            ins = mul_add(out=late, in0=old, scalar=tap(j - 1), in1=late, op0=ALU.mult, op1=ALU.add)
                            ch.mark(ins)
                            ins = mul_add(out=body, in0=raw[b][:, j:j + SEQ], scalar=tap(j), in1=body,
                                          op0=ALU.mult, op1=ALU.add)
                            if j < 3:
                                ch.step(ins)
                            else:
                                ins.then_inc(convd, 1)
                        assert ch.n == STEPS

        wt = [sb(f"p_wt{b}", [P, KD, 512]) for b in range(2)]
        evs = [sb(f"p_ev{s}", [P, 512]) for s in range(6)]
        wdt, wgate = sb("p_wdt", [P, KD, HS]), sb("p_wgate", [P, KD, 16])
        wt_in, wd_in = [sem("p_wt_in0"), sem("p_wt_in1")], sem("p_wd_in")
        tprod, tevac = sem("p_tprod"), sem("p_tevac")
        tstored = [sem(f"p_tstored{s}") for s in range(6)]
        NRT = NT + 1

        with nc.Block() as block:
            @block.sync
            def _(sp):
                for b in range(2):
                    sp.dma_start(wt[b][:], io["w_rows"][b]).then_inc(wt_in[b], 16)
                with sp.Fori(0, 2) as i:
                    for b in range(2):
                        sp.wait_ge(tprod, (i * 2 + b + 1) * NRT)
                        sp.dma_start(wt[b][:], io["w_rows"][bass.ds(i * 2 + b + 2, 1)].squeeze(0)).then_inc(wt_in[b], 16)

            @block.gpsimd
            def _(pool):
                with pool.Fori(0, 3) as i:
                    for b in range(2):
                        for t in range(NRT):
                            n = b * NRT + t
                            rs = P if t < NT else NS
                            wait_apart(pool, tevac, i * (2 * NRT) + n + 1)
                            dst = g.proj_d[t * P:t * P + rs, bass.ds(i, 1), b * 512:(b + 1) * 512].squeeze(1)
                            pool.dma_start(dst, evs[n % 6][0:rs, :]).then_inc(tstored[n % 6], 16)
                for s in range(6):
                    pool.wait_ge(tstored[s], 16 * 3 * (2 * NRT // 6))

            @block.tensor
            def _(pe):
                def block_rows(i, first):
                    for b in range(2):
                        pe.wait_ge(wt_in[b], i * 16 + 16)
                        for t in range(NRT):
                            n = b * NRT + t
                            rs = P if t < NT else NS
                            if n >= 6 or not first:
                                pe.wait_ge(tevac, i * (2 * NRT) + n - 5)
                            for k in range(KD):
                                last = nc.tensor.matmul(g.bank(n % 6, rows=rs), hT[:, k, t * P:t * P + rs],
                                                        wt[b][:, k, :], start=(k == 0), stop=(k == KD - 1))
                            last.then_inc(tprod, 1)

                block_rows(0, True)
                with pe.Fori(1, 3) as i:
                    block_rows(i, False)

            @block.scalar
            def _(act):
                def block_rows(i, first, func):
                    for b in range(2):
                        for t in range(NRT):
                            n = b * NRT + t
                            rs = P if t < NT else NS
                            if n >= 6 or not first:
                                act.wait_ge(tstored[n % 6], i * (16 * (2 * NRT // 6)) + 16 * (n // 6))
                            act.wait_ge(tprod, i * (2 * NRT) + n + 1)
                            nc.scalar.activation(evs[n % 6][0:rs, :], g.bank(n % 6, rows=rs), func).then_inc(tevac, 1)

                block_rows(0, True, ACT.Silu)
                block_rows(1, False, ACT.Silu)
                block_rows(2, False, ACT.Copy)

        dbias, an = sb("p_dbias", [P, HS]), sb("p_an", [P, HS])
        al = sb("p_al", [P, HS])
        dx, dm = sb("p_dx", [P, NT + 1, HS]), sb("p_dm", [P, NT + 1, HS])
        wgu, bg = sb("p_wgu", [16, GH * P]), sb("p_bg", [P, GH])
        gT = sb("p_gT", [16, ROWS])
        xg, ab, cum = sb("p_xg", [P, ROWS]), sb("p_ab", [P, ROWS]), sb("p_cum", [P, ROWS])
        keep, mn = sb("p_keep", [P, ROWS]), sb("p_mn", [P, ROWS])
        small_in, a_neg = sem("p_small_in"), sem("p_a_neg")
        dtps, dch, dabs, dlog, dready = sem("p_dtps"), sem("p_dch"), sem("p_dabs"), sem("p_dlog"), sem("p_dready")
        decps, decs = sem("p_decps"), sem("p_decs")
        gps, gts, gup, gch, gabs, glog = (sem("p_gps"), sem("p_gts"), sem("p_gup"), sem("p_gch"),
                                          sem("p_gabs"), sem("p_glog"))
        ach, cumd, cums, keepd = sem("p_ach"), sem("p_cumd"), sem("p_cums"), sem("p_keepd")

        with nc.Block() as block:
            @block.sync
            def _(sp):
                sp.dma_start(wdt[:], io["w_dt"]).then_inc(small_in, 16)
                sp.dma_start(wgate[:], io["w_gate"]).then_inc(small_in, 16)
                sp.dma_start(dbias[:], io["dt_bias"].partition_broadcast(P)).then_inc(small_in, 16)
                sp.dma_start(al[:], io["a_log"].partition_broadcast(P)).then_inc(small_in, 16)
                sp.dma_start(wgu[:], io["w_gate_up"]).then_inc(small_in, 16)
                sp.dma_start(bg[:], io["b_gate"]).then_inc(small_in, 16)
                for c in range(GH):
                    sp.wait_ge(cumd, c + 1)
                    sp.dma_start(g.cum_d[c], cum[:]).then_inc(cums, 16)
                sp.wait_ge(cums, 16 * GH)

            @block.tensor
            def _(pe):
                pe.wait_ge(small_in, 96)
                for t in range(NRT):
                    rs = P if t < NT else NS
                    for k in range(KD):
                        last = nc.tensor.matmul(g.bank(0, rows=rs, cols=HS, at=t * HS), hT[:, k, t * P:t * P + rs],
                                                wdt[:, k, :], start=(k == 0), stop=(k == KD - 1))
                last.then_inc(dtps, 1)
                for j in range(3):
                    for k in range(KD):
                        last = nc.tensor.matmul(g.bank(1 + j, rows=16, cols=THIRD), wgate[:, k, :],
                                                hT[:, k, j * THIRD:(j + 1) * THIRD], start=(k == 0), stop=(k == KD - 1))
                last.then_inc(gps, 1)
                pe.wait_ge(dready, 2)
                for n, lhs in enumerate((g.tri, g.later, g.ones)):
                    last = nc.tensor.matmul(g.bank(4, cols=P, at=n * P), lhs[:],
                                            g.dta[:, 0:NT, :].rearrange("p t h -> p (t h)"), start=True, stop=True)
                last.then_inc(decps, 1)
                pe.wait_ge(gts, 1)
                for c in range(GH):
                    if c:
                        pe.wait_ge(gabs, c)
                    for j in range(3):
                        last = nc.tensor.matmul(g.bank(5 + j, cols=THIRD), wgu[:, c * P:(c + 1) * P],
                                                gT[:, j * THIRD:(j + 1) * THIRD], start=True, stop=True)
                    last.then_inc(gup, 1)

            @block.vector
            def _(dve):
                V = nc.vector
                V.memset(keep[:], 1.0).then_inc(keepd, 1)
                dve.wait_ge(keepd, 1)
                V.memset(keep[:, 0:SEQ].rearrange("p (t s) -> p t s", s=P)[:, :, 0:1], 0.0).then_inc(keepd, 1)
                V.memset(keep[:, SEQ:ROWS], 0.0).then_inc(keepd, 1)
                ch = Chain(dve, dch)
                dve.wait_ge(dtps, 1)
                dve.wait_ge(small_in, 96)
                parts = ((P, slice(0, NT), NT), (NS, slice(NT, NT + 1), 1))
                for rs, ts, n in parts:
                    src = g.ps[0:rs, ts.start * HS:ts.stop * HS].rearrange("p (t h) -> p t h", h=HS)
                    V.tensor_tensor(dx[0:rs, ts, :], src, bcast(dbias[0:rs, :].unsqueeze(1), [rs, n, HS]),
                                    ALU.add).then_inc(dabs, 1)
                dve.wait_ge(dabs, 2)
                for rs, ts, n in parts:
                    ch.step(V.tensor_scalar(g.dt[0:rs, ts, :], dx[0:rs, ts, :], 0.0, None, ALU.max))
                dve.wait_ge(dlog, 2)
                for rs, ts, n in parts:
                    ch.step(V.tensor_tensor(g.dt[0:rs, ts, :], g.dt[0:rs, ts, :], dm[0:rs, ts, :], ALU.add))
                dve.wait_ge(a_neg, 1)
                for rs, ts, n in parts:
                    V.scalar_tensor_tensor(out=g.dta[0:rs, ts, :], in0=g.dt[0:rs, ts, :], scalar=-1.0,
                                           in1=bcast(an[0:rs, :].unsqueeze(1), [rs, n, HS]),
                                           op0=ALU.mult, op1=ALU.mult).then_inc(dready, 1)
                dve.wait_ge(keepd, 3)
                gc = Chain(dve, gch)
                for c in range(GH):
                    dve.wait_ge(gup, c + 1)
                    if c:
                        dve.wait_ge(glog, c)
                    src = g.ps[:, 5 * 512:8 * 512].rearrange("p (j c) -> p j c", c=512)[:, :, 0:THIRD]
                    V.tensor_scalar(xg[:].rearrange("p (j c) -> p j c", c=THIRD), src, bg[:, c:c + 1], None,
                                    ALU.add).then_inc(gabs, 1)
                    dve.wait_ge(gabs, c + 1)
                    gc.step(V.tensor_scalar(mn[:], xg[:], 0.0, None, ALU.min))
                    dve.wait_ge(glog, c + 1)
                    gc.step(V.tensor_tensor(ab[:], mn[:], ab[:], ALU.subtract))
                    if c:
                        dve.wait_ge(cums, 16 * c)
                    gc.step(V.tensor_tensor_scan(xg[:], keep[:], ab[:], 0.0, ALU.mult, ALU.add))
                    V.tensor_scalar(cum[:], xg[:], 1.0 / 16.0, None, ALU.mult).then_inc(cumd, 1)
                    dve.wait_ge(cumd, c + 1)

            @block.scalar
            def _(act):
                A = nc.scalar.activation
                act.wait_ge(small_in, 96)
                A(an[:], al[:], ACT.Exp).then_inc(a_neg, 1)
                ch = Chain(act, ach)
                for n, (rs, ts) in enumerate(((P, slice(0, NT)), (NS, slice(NT, NT + 1)))):
                    act.wait_ge(dabs, n + 1)
                    ch.step(A(dm[0:rs, ts, :], dx[0:rs, ts, :], ACT.Abs))
                    ch.step(A(dm[0:rs, ts, :], dm[0:rs, ts, :], ACT.Exp, scale=-1.0))
                    A(dm[0:rs, ts, :], dm[0:rs, ts, :], ACT.Ln, bias=1.0).then_inc(dlog, 1)
                act.wait_ge(gps, 1)
                src = g.ps[0:16, 512:4 * 512].rearrange("p (j c) -> p j c", c=512)[:, :, 0:THIRD]
                A(gT[:].rearrange("p (j c) -> p j c", c=THIRD), src, ACT.Copy).then_inc(gts, 1)
                act.wait_ge(decps, 1)
                for n, dst in enumerate((g.ecum, g.etoend, g.etot)):
                    A(dst[:].rearrange("p t h -> p (t h)"), g.bank(4, cols=P, at=n * P), ACT.Exp).then_inc(decs, 1)
                act.wait_ge(dready, 2)
                A(g.edta[:], g.dta[0:NS, NT, :], ACT.Exp).then_inc(decs, 1)
                for c in range(GH):
                    act.wait_ge(gabs, c + 1)
                    if c:
                        act.wait_ge(cumd, c)
                    ch.step(A(ab[:], xg[:], ACT.Abs))
                    ch.step(A(ab[:], ab[:], ACT.Exp, scale=-1.0))
                    A(ab[:], ab[:], ACT.Ln, bias=1.0).then_inc(glog, 1)
                act.wait_ge(decs, 4)


class Output:

    def __init__(self, g, st, pre, rows):
        nc = g.nc
        self.g, self.rows = g, rows
        sb = lambda n, s: st.enter_context(nc.sbuf_tensor(pre + n, s, F32))
        sem = lambda n: g.sem(pre + n)
        self.w = sb("w_out", [P, 2 * KD, D])
        self.cat, self.catT = sb("cat", [P, 2 * D]), sb("catT", [P, 2 * KD, P])
        self.x, self.x1, self.h2 = sb("x", [P, D]), sb("x1", [P, D]), sb("h2", [P, D])
        self.junk = sb("junk", [P, D])
        self.ms, self.r = sb("ms2", [P, 2]), sb("r2", [P, 1])
        self.gate1, self.scale2, self.shift2 = sb("gate1", [P, D]), sb("scale2", [P, D]), sb("shift2", [P, D])
        self.norm = self.junk
        self.w_in, self.mods_in, self.scaled = sem("w_out_in"), sem("mods_in"), sem("scaled")
        self.x_in, self.cat_ready = sem("x_in"), sem("cat_ready")
        self.catT_ps, self.catT_kept, self.prod = sem("catT_ps"), sem("catT_kept"), sem("prod")
        self.gated, self.x1_ready, self.r2_ready = sem("gated"), sem("x1_ready"), sem("r2_ready")
        self.h2_scaled, self.h2_ready = sem("h2_scaled"), sem("h2_ready")
        self.ach, self.x1_stored, self.h2_stored = sem("oach"), sem("x1_stored"), sem("h2_stored")

    def load_constants(self, sp):
        g, io, rs = self.g, self.g.io, self.rows
        take = lambda a: (g.mod_d[0:NS, a * D:(a + 1) * D] if rs == NS
                          else g.mod_d[NS, a * D:(a + 1) * D].partition_broadcast(P))
        sp.dma_start(self.norm[0:rs, :], io["norm_ffn"].partition_broadcast(rs)).then_inc(self.mods_in, 16)
        sp.dma_start(self.gate1[0:rs, :], take(2)).then_inc(self.mods_in, 16)
        sp.dma_start(self.shift2[0:rs, :], take(3)).then_inc(self.mods_in, 16)
        sp.dma_start(self.scale2[0:rs, :], take(4)).then_inc(self.mods_in, 16)
        sp.dma_start(self.w[:], io["w_out"]).then_inc(self.w_in, 16)

    def prepare(self, dve):
        rs = self.rows
        dve.wait_ge(self.mods_in, 64)
        s = self.scale2[0:rs, :]
        self.g.nc.vector.scalar_tensor_tensor(out=s, in0=s, scalar=1.0, in1=self.norm[0:rs, :],
                                              op0=ALU.add, op1=ALU.mult).then_inc(self.scaled, 1)
        dve.wait_ge(self.scaled, 1)

    def turn(self, pe, n):
        g, rs = self.g, self.rows
        pe.wait_ge(self.cat_ready, n + 1)
        for half in range(2):
            for k in range(KD):
                c = half * KD + k
                last = g.nc.tensor.transpose(g.ps[:, (4 + 2 * half) * 512 + k * P:][:, 0:rs],
                                             self.cat[0:rs, c * P:(c + 1) * P], g.ident[0:rs, 0:rs])
            last.then_inc(self.catT_ps, 1)

    def product(self, pe, n, ks, first):
        g, rs = self.g, self.rows
        if ks.start == 0:
            pe.wait_ge(self.w_in, 16)
            pe.wait_ge(self.catT_kept, n * 2 + 2)
            if not first:
                pe.wait_ge(self.x1_ready, n)
        for k in ks:
            for cols in range(2):
                last = g.nc.tensor.matmul(g.bank(cols, rows=rs), self.catT[:, k, 0:rs],
                                          self.w[:, k, cols * 512:(cols + 1) * 512],
                                          start=(k == 0), stop=(k == 2 * KD - 1))
        if ks.stop == 2 * KD:
            last.then_inc(self.prod, 1)

    def keep_turned(self, act, n):
        g, A, rs = self.g, self.g.nc.scalar.activation, self.rows
        for half in range(2):
            act.wait_ge(self.catT_ps, n * 2 + half + 1)
            src = g.ps[:, (4 + 2 * half) * 512:][:, 0:KD * P].rearrange("p (k r) -> p k r", r=P)[:, :, 0:rs]
            A(self.catT[:, half * KD:(half + 1) * KD, 0:rs], src, ACT.Copy).then_inc(self.catT_kept, 1)

    def norm2(self, act, n):
        g, A, rs = self.g, self.g.nc.scalar.activation, self.rows
        act.wait_ge(self.x1_ready, n + 1)
        act.wait_ge(self.scaled, 1)
        ch = Chain(act, self.ach, n * 2)
        ch.step(A(self.junk[0:rs, :], self.x1[0:rs, :], ACT.Square, accum_out=self.ms[0:rs, 0:1]))
        ch.step(A(self.ms[0:rs, 1:2], self.ms[0:rs, 0:1], ACT.Ln, scale=1.0 / D, bias=g.eps[0:rs, :]))
        A(self.r[0:rs, :], self.ms[0:rs, 1:2], ACT.Exp, scale=-0.5).then_inc(self.r2_ready, 1)
        act.wait_ge(self.r2_ready, n + 1)

    def residual(self, dve, n, first):
        g, V, rs = self.g, self.g.nc.vector, self.rows
        dve.wait_ge(self.prod, n + 1)
        dve.wait_ge(self.x_in, n * 16 + 16)
        if not first:
            dve.wait_ge(self.x1_stored, n * 16)
        V.tensor_tensor(self.x1[0:rs, :], g.ps[0:rs, 0:D], self.gate1[0:rs, :], ALU.mult).then_inc(self.gated, 1)
        dve.wait_ge(self.gated, n + 1)
        V.tensor_tensor(self.x1[0:rs, :], self.x1[0:rs, :], self.x[0:rs, :], ALU.add).then_inc(self.x1_ready, 1)

    def modulate(self, dve, n, first):
        V, rs = self.g.nc.vector, self.rows
        dve.wait_ge(self.r2_ready, n + 1)
        if not first:
            dve.wait_ge(self.h2_stored, n * 16)
        V.scalar_tensor_tensor(out=self.h2[0:rs, :], in0=self.x1[0:rs, :], scalar=self.r[0:rs, :],
                               in1=self.scale2[0:rs, :], op0=ALU.mult, op1=ALU.mult).then_inc(self.h2_scaled, 1)
        dve.wait_ge(self.h2_scaled, n + 1)
        V.tensor_tensor(self.h2[0:rs, :], self.h2[0:rs, :], self.shift2[0:rs, :], ALU.add).then_inc(self.h2_ready, 1)
        dve.wait_ge(self.h2_ready, n + 1)

    def store(self, eng, n, row):
        g, rs = self.g, self.rows
        rows = bass.ds(row, rs)
        wait_apart(eng, self.x1_ready, n + 1)
        eng.dma_start(g.x1_d[rows, :], self.x1[0:rs, :]).then_inc(self.x1_stored, 16)
        wait_apart(eng, self.h2_ready, n + 1)
        eng.dma_start(g.h2_d[rows, :], self.h2[0:rs, :]).then_inc(self.h2_stored, 16)


def mix_prompt(g):
    nc, io = g.nc, g.io
    R = HS // 2
    QS = float(P) ** -0.5
    with ExitStack() as st:
        sb = lambda n, s: st.enter_context(nc.sbuf_tensor("x_" + n, s, F32))
        sem = lambda n: g.sem("x_" + n)
        out = Output(g, st, "xo_", P)
        xbc, zgv, qk, cum = sb("xbc", [P, NXBC, P]), sb("zgv", [P, 3, D]), sb("qk", [P, NQK, P]), sb("cum", [P, GH, P])
        dec = sb("dec", [P, HS, P])
        xs, xdt, xend = sb("xs", [P, HS, HP]), sb("xdt", [P, HS, HP]), sb("xend", [P, HS, HP])
        b_rows, cb = sb("b_rows", [P, 2, P]), sb("cb", [P, 2, P])
        S, GS = sb("S", [P, HS, HP]), sb("GS", [P, GH, GV])
        yb, yt = sb("yb", [P, HS, HP]), sb("yt", [P, HS, HP])
        d1, ref2, end = sb("d1", [P, GH, P]), sb("ref2", [P, GH, P]), sb("end", [P, GH, P])
        qd, kd, qi, ecg = sb("qd", [P, GH, P]), sb("kd", [P, GH, P]), sb("qi", [P, GH, P]), sb("ecg", [P, GH, P])
        att, keT = sb("att", [P, GH, P]), sb("keT", [P, GH, P])
        dskip, ssdn, glan = sb("dskip", [P, HS]), sb("ssdn", [P, D]), sb("glan", [P, GV])
        msy, ry, mso, ro = sb("msy", [P, 4]), sb("ry", [P, 2]), sb("mso", [P, 8]), sb("ro", [P, GH])
        consts_in, xbc_in, gla_in, zgv_in = sem("consts_in"), sem("xbc_in"), sem("gla_in"), sem("zgv_in")
        seg_in, xs_ps, xs_kept, xdt_ready, xend_ready = (sem("seg_in"), sem("xs_ps"), sem("xs_kept"),
                                                         sem("xdt_ready"), sem("xend_ready"))
        seg_ps, dec_ready, m_ready, y_ps, su_ps = (sem("seg_ps"), sem("dec_ready"), sem("m_ready"), sem("y_ps"),
                                                   sem("su_ps"))
        y_used, y_sum, ry_ready, s_ready, gs_ready = (sem("y_used"), sem("y_sum"), sem("ry_ready"), sem("s_ready"),
                                                      sem("gs_ready"))
        gdiff, gexp, gprod, att_ps, att_ready = (sem("gdiff"), sem("gexp"), sem("gprod"), sem("att_ps"),
                                                 sem("att_ready"))
        ke_ps, ke_kept, o_ps, gs_ps, ro_ready = sem("ke_ps"), sem("ke_kept"), sem("o_ps"), sem("gs_ps"), sem("ro_ready")
        vch, ach, s_out = sem("vch"), sem("ach"), sem("s_out")
        VSTEPS, ASTEPS = 6, 4
        block = st.enter_context(nc.Block())
        head = lambda t, h: t[:, h, :]
        per_head = lambda t, n: bcast(t[:, bass.ds(n, 1), :].squeeze(1).unsqueeze(2), [P, HS, HP])

        @block.sync
        def _(sp):
            sp.dma_start(dskip[:], io["d_skip"].partition_broadcast(P)).then_inc(consts_in, 16)
            sp.dma_start(ssdn[:], io["ssd_norm"].partition_broadcast(P)).then_inc(consts_in, 16)
            sp.dma_start(glan[:], io["gla_norm"].partition_broadcast(P)).then_inc(consts_in, 16)

            def load(n, first):
                rows = bass.ds(n * P, P)
                if not first:
                    sp.wait_ge(y_ps, n)
                sp.dma_start(xbc[:], g.xbc_d[:, :, rows].rearrange("c p t -> p c t")).then_inc(xbc_in, 16)
                if not first:
                    sp.wait_ge(gprod, n)
                sp.dma_start(qk[:], g.qk_d[:, :, rows].rearrange("c p t -> p c t")).then_inc(gla_in, 16)
                sp.dma_start(cum[:], g.cum_d[:, :, rows].rearrange("c p t -> p c t")).then_inc(gla_in, 16)
                if not first:
                    sp.wait_ge(out.cat_ready, n)
                    sp.wait_ge(gs_ps, n)
                sp.dma_start(zgv[:], g.proj_d[rows, :, :]).then_inc(zgv_in, 16)

            def load_x(n, first):
                if not first:
                    sp.wait_ge(out.x1_ready, n)
                sp.dma_start(out.x[:], io["x_prompt"][bass.ds(n * P, P), :]).then_inc(out.x_in, 16)

            load(0, True)
            out.load_constants(sp)
            load_x(0, True)
            load(1, False)
            with sp.Fori(2, NT) as n:
                load(n, False)
                load_x(n - 1, False)
            load_x(NT - 1, False)
            sp.wait_ge(s_ready, NT + 1)
            sp.dma_start(io["ssm_p"], S[:].rearrange("p h c -> p (h c)")).then_inc(s_out, 16)
            sp.wait_ge(gs_ready, NT + 1)
            sp.dma_start(io["gla_p"], GS[:].rearrange("p h c -> p (h c)")).then_inc(s_out, 16)
            sp.wait_ge(s_out, 32)

        @block.gpsimd
        def _(pool):
            with pool.Fori(0, NT) as n:
                out.store(pool, n, n * P)
            pool.wait_ge(out.x1_stored, 16 * NT)
            pool.wait_ge(out.h2_stored, 16 * NT)

        @block.tensor
        def _(pe):
            mm, tr = nc.tensor.matmul, nc.tensor.transpose

            def tile(n, stage):
                before = lambda a, b: out.product(pe, n - 1, range(a, b), stage == 1) if stage else None
                pe.wait_ge(xbc_in, n * 16 + 16)
                if stage:
                    pe.wait_ge(gs_ready, n + 1)
                for c in range(KD):
                    tr(g.ps[:, 2 * 512 + c * P:2 * 512 + (c + 1) * P], xbc[:, c, :], g.ident[:])
                if stage:
                    pe.wait_ge(out.catT_kept, n * 2)
                for c in range(2):
                    tr(g.bank(4, cols=P, at=c * P), xbc[:, KD + c, :], g.ident[:])
                    last = mm(g.bank(4, cols=P, at=(2 + c) * P), xbc[:, KD + c, :], xbc[:, KD + 2 + c, :],
                              start=True, stop=True)
                last.then_inc(xs_ps, 1)
                pe.wait_ge(seg_in, n + 1)
                for half in range(2):
                    if half:
                        pe.wait_ge(xs_kept, n + 1)
                    for q in range(2):
                        h = half * R + q * 4
                        last = mm(g.bank((6, 2)[half] + q), g.later[:], dec[:, h:h + 4, :], start=True, stop=True)
                    last.then_inc(seg_ps, 1)
                before(0, 5)
                pe.wait_ge(xdt_ready, n + 1)
                for c in range(2):
                    pe.wait_ge(m_ready, n * 2 + c + 1)
                    for r in range(R):
                        h = c * R + r
                        mm(g.ps[:, 6 * 512 + h * HP:6 * 512 + (h + 1) * HP], dec[:, h, :], xdt[:, h, :],
                           start=True, stop=True)
                pe.wait_ge(s_ready, n + 1)
                for c in range(2):
                    last = mm(g.bank(2 + c), xbc[:, KD + 2 + c, :], S[:, c * R:(c + 1) * R, :], start=True, stop=True)
                last.then_inc(y_ps, 1)
                pe.wait_ge(xend_ready, n + 1)
                for c in range(2):
                    last = mm(g.bank(4 + c), b_rows[:, c, :], xend[:, c * R:(c + 1) * R, :], start=True, stop=True)
                last.then_inc(su_ps, 1)
                before(5, 9)
                pe.wait_ge(gprod, n + 1)
                pe.wait_ge(y_used, n + 1)
                for h in range(GH):
                    mm(g.bank(2, cols=P, at=h * P), head(kd, h), head(qd, h), start=True, stop=True)
                for h in range(GH):
                    last = mm(g.bank(3, rows=HALF, cols=HALF, at=h * HALF), ref2[:, h, 0:HALF], ref2[:, h, HALF:P],
                              start=True, stop=True)
                last.then_inc(att_ps, 1)
                pe.wait_ge(s_ready, n + 2)
                for h in range(GH):
                    last = tr(g.bank(4, cols=P, at=h * P), head(end, h), g.ident[:])
                last.then_inc(ke_ps, 1)
                before(9, 12)
                pe.wait_ge(att_ready, n + 1)
                pe.wait_ge(zgv_in, n * 16 + 16)
                pe.wait_ge(gs_ready, n + 1)
                for h in range(GH):
                    v, o = zgv[:, 2, h * GV:(h + 1) * GV], g.ps[:, 6 * 512 + h * GV:6 * 512 + (h + 1) * GV]
                    mm(o, head(att, h), v, start=True, stop=False)
                    last = mm(o, head(qi, h), head(GS, h), start=False, stop=True)
                last.then_inc(o_ps, 1)
                pe.wait_ge(ke_kept, n + 1)
                for h in range(GH):
                    last = mm(g.ps[:, 2 * 512 + h * GV:2 * 512 + (h + 1) * GV], head(keT, h),
                              zgv[:, 2, h * GV:(h + 1) * GV], start=True, stop=True)
                last.then_inc(gs_ps, 1)
                before(12, 2 * KD)
                out.turn(pe, n)

            for n in range(3):
                tile(n, n)
            with pe.Fori(3, NT) as n:
                tile(n, 3)
            out.product(pe, NT - 1, range(0, 2 * KD), False)

        @block.scalar
        def _(act):
            A = nc.scalar.activation

            def tile(n, stage):
                ch = Chain(act, ach, n * ASTEPS)
                act.wait_ge(xs_ps, n + 1)
                A(xs[:].rearrange("p h c -> p (h c)"), g.ps[:, 2 * 512:4 * 512], ACT.Copy)
                A(b_rows[:].rearrange("p c n -> p (c n)"), g.bank(4, cols=2 * P), ACT.Copy).then_inc(xs_kept, 1)
                for half in range(2):
                    act.wait_ge(seg_ps, n * 2 + half + 1)
                    A(dec[:, half * R:(half + 1) * R, :].rearrange("p h t -> p (h t)"),
                      g.ps[:, (6, 2)[half] * 512:((6, 2)[half] + 2) * 512], ACT.Exp).then_inc(dec_ready, 1)
                act.wait_ge(gdiff, n * 4 + 4)
                A(qd[:], d1[:], ACT.Exp)
                A(kd[:], d1[:], ACT.Exp, scale=-1.0)
                A(ref2[:], ref2[:], ACT.Exp)
                A(end[:], end[:], ACT.Exp)
                A(ecg[:], cum[:], ACT.Exp).then_inc(gexp, 1)
                if stage >= 2:
                    out.norm2(act, n - 2)
                act.wait_ge(y_sum, n + 1)
                for c in range(2):
                    ins = A(yt[:, c * R:(c + 1) * R, :], yb[:, c * R:(c + 1) * R, :], ACT.Square,
                            accum_out=msy[:, c:c + 1])
                ch.step(ins)
                ch.step(A(msy[:, 2:4], msy[:, 0:2], ACT.Ln, scale=2.0 / D, bias=g.eps[:]))
                A(ry[:], msy[:, 2:4], ACT.Exp, scale=-0.5).then_inc(ry_ready, 1)
                act.wait_ge(ry_ready, n + 1)
                act.wait_ge(ke_ps, n + 1)
                A(keT[:].rearrange("p h d -> p (h d)"), g.bank(4), ACT.Copy).then_inc(ke_kept, 1)
                act.wait_ge(o_ps, n + 1)
                for h in range(GH):
                    ins = A(yt[:, h * 4:(h + 1) * 4, :].rearrange("p h c -> p (h c)"), g.ps[:, 6 * 512 + h * GV:6 * 512 + (h + 1) * GV],
                            ACT.Square, accum_out=mso[:, h:h + 1])
                ch.step(ins)
                ch.step(A(mso[:, 4:8], mso[:, 0:4], ACT.Ln, scale=1.0 / GV, bias=g.eps[:]))
                A(ro[:], mso[:, 4:8], ACT.Exp, scale=-0.5).then_inc(ro_ready, 1)
                act.wait_ge(ro_ready, n + 1)
                assert ch.n == ASTEPS
                out.keep_turned(act, n)

            for n in range(3):
                tile(n, n)
            with act.Fori(3, NT) as n:
                tile(n, 3)
            for n in (NT - 2, NT - 1):
                out.norm2(act, n)

        @block.vector
        def _(dve):
            V, stt = nc.vector, nc.vector.scalar_tensor_tensor
            V.memset(S[:], 0.0).then_inc(s_ready, 1)
            V.memset(GS[:], 0.0).then_inc(gs_ready, 1)
            dve.wait_ge(s_ready, 1)
            dve.wait_ge(gs_ready, 1)
            dve.wait_ge(consts_in, 48)

            def tile(n, stage):
                ch = Chain(dve, vch, n * VSTEPS)
                dta = g.dta[:, bass.ds(n, 1), :].squeeze(1)
                V.tensor_tensor(dec[:], bcast(dta.unsqueeze(2), [P, HS, P]), bcast(g.tri[:].unsqueeze(1), [P, HS, P]),
                                ALU.mult).then_inc(seg_in, 1)
                dve.wait_ge(xs_kept, n + 1)
                V.tensor_tensor(xdt[:], xs[:], per_head(g.dt, n), ALU.mult)
                V.tensor_tensor(cb[:], g.bank(4, cols=2 * P, at=2 * P).rearrange("p (c t) -> p c t", c=2),
                                bcast(g.tri[:].unsqueeze(1), [P, 2, P]), ALU.mult).then_inc(xdt_ready, 1)
                dve.wait_ge(xdt_ready, n + 1)
                V.tensor_tensor(xend[:], xdt[:], per_head(g.etoend, n), ALU.mult).then_inc(xend_ready, 1)
                dve.wait_ge(gla_in, n * 32 + 32)
                by_half = lambda t: t[:].rearrange("p h (c t) -> p (h c) t", c=2)
                V.tensor_tensor(by_half(d1), by_half(cum), bcast(by_half(cum)[:, :, HALF // 2:HALF // 2 + 1],
                                                                 [P, 2 * GH, HALF]), ALU.subtract).then_inc(gdiff, 1)
                seam = bcast(cum[:, :, HALF - 1:HALF], [P, GH, HALF])
                V.tensor_tensor(ref2[:, :, 0:HALF], seam, cum[:, :, 0:HALF], ALU.subtract).then_inc(gdiff, 1)
                V.tensor_tensor(ref2[:, :, HALF:P], cum[:, :, HALF:P], seam, ALU.subtract).then_inc(gdiff, 1)
                V.tensor_tensor(end[:], bcast(cum[:, :, P - 1:P], [P, GH, P]), cum[:], ALU.subtract).then_inc(gdiff, 1)
                for c in range(2):
                    dve.wait_ge(dec_ready, n * 2 + c + 1)
                    m = dec[:, c * R:(c + 1) * R, :]
                    V.tensor_tensor(m, m, bcast(cb[:, c:c + 1, :], [P, R, P]), ALU.mult).then_inc(m_ready, 1)
                dve.wait_ge(gexp, n + 1)
                q, k = qk[:, 0:GH, :], qk[:, GH:NQK, :]
                stt(out=qd[:], in0=q, scalar=QS, in1=qd[:], op0=ALU.mult, op1=ALU.mult)
                V.tensor_tensor(kd[:], k, kd[:], ALU.mult)
                stt(out=ref2[:, :, HALF:P], in0=q[:, :, HALF:P], scalar=QS, in1=ref2[:, :, HALF:P],
                    op0=ALU.mult, op1=ALU.mult)
                V.tensor_tensor(ref2[:, :, 0:HALF], k[:, :, 0:HALF], ref2[:, :, 0:HALF], ALU.mult)
                stt(out=qi[:], in0=q, scalar=QS, in1=ecg[:], op0=ALU.mult, op1=ALU.mult)
                V.tensor_tensor(end[:], k, end[:], ALU.mult).then_inc(gprod, 1)
                if stage >= 2:
                    out.modulate(dve, n - 2, stage == 2)
                dve.wait_ge(y_ps, n + 1)
                V.tensor_tensor(yt[:], xs[:], bcast(dskip[:].unsqueeze(2), [P, HS, HP]), ALU.mult)
                ch.step(V.tensor_tensor(yb[:], g.ps[:, 2 * 512:4 * 512].rearrange("p (h c) -> p h c", c=HP),
                                        per_head(g.ecum, n), ALU.mult))
                V.tensor_tensor(yb[:], yb[:], g.ps[:, 6 * 512:8 * 512].rearrange("p (h c) -> p h c", c=HP), ALU.add).then_inc(y_used, 1)
                dve.wait_ge(y_used, n + 1)
                ch.mark(V.tensor_tensor(S[:], S[:], per_head(g.etot, n), ALU.mult))
                ch.step(V.tensor_tensor(yb[:], yb[:], yt[:], ALU.add))
                dve.wait_ge(zgv_in, n * 16 + 16)
                V.tensor_tensor(yb[:].rearrange("p h c -> p (h c)"), yb[:].rearrange("p h c -> p (h c)"), zgv[:, 0, :],
                                ALU.mult).then_inc(y_sum, 1)
                dve.wait_ge(su_ps, n + 1)
                V.tensor_tensor(S[:], S[:], g.ps[:, 4 * 512:6 * 512].rearrange("p (h c) -> p h c", c=HP),
                                ALU.add).then_inc(s_ready, 1)
                dve.wait_ge(att_ps, n + 1)
                ch.step(V.tensor_tensor(att[:], g.bank(2).rearrange("p (h t) -> p h t", h=GH),
                                        bcast(g.blk[:].unsqueeze(1), [P, GH, P]), ALU.mult))
                V.tensor_copy(att[0:HALF, :, HALF:P], g.bank(3, rows=HALF, cols=GH * HALF).rearrange(
                    "p (h t) -> p h t", h=GH)).then_inc(att_ready, 1)
                dve.wait_ge(ry_ready, n + 1)
                for c in range(2):
                    ins = stt(out=out.cat[:, c * 512:(c + 1) * 512], in0=yb[:, c * R:(c + 1) * R, :].rearrange(
                        "p h c -> p (h c)"), scalar=ry[:, c:c + 1], in1=ssdn[:, c * 512:(c + 1) * 512],
                        op0=ALU.mult, op1=ALU.mult)
                ch.mark(ins)
                dve.wait_ge(ro_ready, n + 1)
                for h in range(GH):
                    ins = stt(out=out.cat[:, D + h * GV:D + (h + 1) * GV], in0=g.ps[:, 6 * 512 + h * GV:6 * 512 + (h + 1) * GV],
                              scalar=ro[:, h:h + 1], in1=glan[:], op0=ALU.mult, op1=ALU.mult)
                ch.step(ins)
                V.tensor_tensor(out.cat[:, D:2 * D], out.cat[:, D:2 * D], zgv[:, 1, :], ALU.mult).then_inc(out.cat_ready, 1)
                dve.wait_ge(gs_ps, n + 1)
                for h in range(GH):
                    ins = stt(out=head(GS, h), in0=head(GS, h), scalar=ecg[:, h, P - 1:P],
                              in1=g.ps[:, 2 * 512 + h * GV:2 * 512 + (h + 1) * GV], op0=ALU.mult, op1=ALU.add)
                ins.then_inc(gs_ready, 1)
                dve.wait_ge(gs_ready, n + 2)
                ch.join()
                assert ch.n == VSTEPS
                if stage:
                    out.residual(dve, n - 1, stage == 1)

            out.prepare(dve)
            for n in range(3):
                tile(n, n)
            with dve.Fori(3, NT) as n:
                tile(n, 3)
            out.modulate(dve, NT - 2, False)
            out.residual(dve, NT - 1, False)
            out.modulate(dve, NT - 1, False)


def mix_sample(g):
    nc, io = g.nc, g.io
    HC = HS // 2
    QS = float(P) ** -0.5
    with ExitStack() as st:
        sb = lambda n, s: st.enter_context(nc.sbuf_tensor("s_" + n, s, F32))
        sem = lambda n: g.sem("s_" + n)
        out = Output(g, st, "so_", NS)
        xbc, qk, cum, zgv = sb("xbc", [P, NXBC, NS]), sb("qk", [P, NQK, NS]), sb("cum", [P, GH, NS]), sb("zgv", [NS, 3, D])
        S = sb("S", [P, NS, HC, P])
        xr, bc, dtx, da = sb("xr", [NS, D]), sb("bc", [NS, 4 * P]), sb("dtx", [NS, D]), sb("da", [NS, D])
        turned = sb("turned", [P, 2, HC, NS])
        t, yT = sb("t", [P, HC, P]), sb("yT", [P, HC, NS])
        ela, qpad = sb("ela", [P, GH, NS]), sb("qpad", [P, GH, NS, NS])
        dskip, ssdn, glan = sb("dskip", [NS, HS]), sb("ssdn", [NS, D]), sb("glan", [NS, GV])
        y, junk = sb("y", [NS, D]), sb("junk", [NS, D])
        ms, r = sb("ms", [NS, 12]), sb("r", [NS, 6])
        none, none_ready, none_stored = sb("none", [TILED - ROWS, D]), sem("none_ready"), sem("none_stored")
        small_in, xbc_in, S_in, GS_in = sem("small_in"), sem("xbc_in"), sem("S_in"), sem("GS_in")
        rows_ps, rows_kept, pre, turn_ps, turn_kept = (sem("rows_ps"), sem("rows_kept"), sem("pre"), sem("turn_ps"),
                                                       sem("turn_kept"))
        bc_ps, s_new, yT_ps, y_done, yr = sem("bc_ps"), sem("s_new"), sem("yT_ps"), sem("y_done"), sem("yr")
        e_ready, v_ps, g_new, o_ps, o_r = sem("e_ready"), sem("v_ps"), sem("g_new"), sem("o_ps"), sem("o_r")
        vch, ach, s_out, g_out = sem("vch"), sem("ach"), sem("s_out"), sem("g_out")
        block = st.enter_context(nc.Block())

        @block.sync
        def _(sp):
            sp.dma_start(xbc[:], g.xbc_d[:, :, SEQ:ROWS].rearrange("c p t -> p c t")).then_inc(xbc_in, 16)
            sp.dma_start(S[:], io["state_ssm"]).then_inc(S_in, 16)
            sp.dma_start(qk[:], g.qk_d[:, :, SEQ:ROWS].rearrange("c p t -> p c t")).then_inc(small_in, 16)
            sp.dma_start(cum[:], g.cum_d[:, :, SEQ:ROWS].rearrange("c p t -> p c t")).then_inc(small_in, 16)
            sp.dma_start(zgv[:], g.proj_d[SEQ:ROWS, :, :]).then_inc(small_in, 16)
            sp.dma_start(dskip[:], io["d_skip"].partition_broadcast(NS)).then_inc(small_in, 16)
            sp.dma_start(ssdn[:], io["ssd_norm"].partition_broadcast(NS)).then_inc(small_in, 16)
            sp.dma_start(glan[:], io["gla_norm"].partition_broadcast(NS)).then_inc(small_in, 16)
            sp.dma_start(out.x[0:NS, :], io["x_sample"]).then_inc(out.x_in, 16)
            out.load_constants(sp)
            sp.wait_ge(s_new, NS)
            sp.dma_start(io["ssm_s"], S[:]).then_inc(s_out, 16)
            sp.wait_ge(y_done, 1)
            sp.wait_ge(s_out, 16)
            sp.dma_start(S[:].rearrange("p b c n -> p (b c n)"),
                         io["state_gla"].rearrange("p b h v -> p (b h v)")).then_inc(GS_in, 16)
            sp.wait_ge(g_new, NS)
            sp.dma_start(io["gla_s"].rearrange("p b h v -> p (b h v)"),
                         S[:].rearrange("p b c n -> p (b c n)")).then_inc(g_out, 16)
            out.store(sp, 0, SEQ)
            sp.wait_ge(g_out, 16)
            sp.wait_ge(out.x1_stored, 16)
            sp.wait_ge(out.h2_stored, 16)

        @block.gpsimd
        def _(pool):
            nc.gpsimd.memset(none[:], 0.0).then_inc(none_ready, 1)
            pool.wait_ge(none_ready, 1)
            pool.dma_start(g.h2_d[ROWS:TILED, :], none[:]).then_inc(none_stored, 16)
            pool.wait_ge(none_stored, 16)

        GS = S[:].rearrange("p b c n -> p b (c n)").rearrange("p b (h v) -> p b h v", h=GH)

        @block.tensor
        def _(pe):
            mm, tr = nc.tensor.matmul, nc.tensor.transpose
            pe.wait_ge(xbc_in, 16)
            for c in range(NXBC):
                last = tr(g.ps[0:NS, c * P:(c + 1) * P], xbc[:, c, :], g.ident[:])
            last.then_inc(rows_ps, 1)
            pe.wait_ge(pre, 2)
            for n, src in enumerate((dtx, da)):
                for c in range(HC):
                    last = tr(g.bank(3, cols=NS, at=(n * HC + c) * NS), src[:, c * P:(c + 1) * P], g.ident[0:NS, 0:NS])
            last.then_inc(turn_ps, 1)
            for b in range(NS):
                if b >= 2:
                    pe.wait_ge(s_new, b - 1)
                mm(g.bank(4 + b % 2), g.sel8[:, b, :], bc[:], start=True, stop=True).then_inc(bc_ps, 1)
            pe.wait_ge(s_new, NS)
            for c in range(HC):
                last = tr(g.ps[0:NS, c * P:(c + 1) * P], yT[:, c, :], g.ident[:])
            last.then_inc(yT_ps, 1)
            pe.wait_ge(small_in, 96)
            for b in range(NS):
                if b >= 1:
                    pe.wait_ge(g_new, b)
                for half in range(2):
                    last = mm(g.bank(6 + half), g.sel8[:, b, :], zgv[:, 2, half * 512:(half + 1) * 512],
                              start=True, stop=True)
                last.then_inc(v_ps, 1)
            pe.wait_ge(g_new, NS)
            for h in range(GH):
                for b in range(NS):
                    last = mm(g.ps[0:NS, 4 * 512 + h * GV:4 * 512 + (h + 1) * GV], qpad[:, h, b, :], GS[:, b, h, :],
                              start=(b == 0), stop=(b == NS - 1))
            last.then_inc(o_ps, 1)
            out.turn(pe, 0)
            out.product(pe, 0, range(0, 2 * KD), True)

        @block.scalar
        def _(act):
            A = nc.scalar.activation
            ch = Chain(act, ach)
            act.wait_ge(rows_ps, 1)
            A(xr[:], g.ps[0:NS, 0:D], ACT.Copy)
            A(bc[:], g.bank(2, rows=NS), ACT.Copy).then_inc(rows_kept, 1)
            act.wait_ge(turn_ps, 1)
            A(turned[:].rearrange("p a c b -> p (a c b)"), g.bank(3, cols=2 * HC * NS), ACT.Copy).then_inc(turn_kept, 1)
            act.wait_ge(small_in, 96)
            A(ela[:], cum[:], ACT.Exp).then_inc(e_ready, 1)
            act.wait_ge(y_done, 1)
            for c in range(2):
                ins = A(junk[:, c * 512:(c + 1) * 512], y[:, c * 512:(c + 1) * 512], ACT.Square, accum_out=ms[:, c:c + 1])
            ch.step(ins)
            ch.step(A(ms[:, 2:4], ms[:, 0:2], ACT.Ln, scale=2.0 / D, bias=g.eps[0:NS, :]))
            A(r[:, 0:2], ms[:, 2:4], ACT.Exp, scale=-0.5).then_inc(yr, 1)
            act.wait_ge(o_ps, 1)
            for h in range(GH):
                ins = A(junk[:, h * GV:(h + 1) * GV], g.ps[0:NS, 4 * 512 + h * GV:4 * 512 + (h + 1) * GV], ACT.Square,
                        accum_out=ms[:, 4 + h:5 + h])
            ch.step(ins)
            ch.step(A(ms[:, 8:12], ms[:, 4:8], ACT.Ln, scale=1.0 / GV, bias=g.eps[0:NS, :]))
            A(r[:, 2:6], ms[:, 8:12], ACT.Exp, scale=-0.5).then_inc(o_r, 1)
            out.keep_turned(act, 0)
            out.norm2(act, 0)

        @block.vector
        def _(dve):
            V, stt = nc.vector, nc.vector.scalar_tensor_tensor
            ch = Chain(dve, vch)
            heads = lambda ap: ap.rearrange("p (h c) -> p h c", c=HP)
            per_head = lambda ap: bcast(ap.unsqueeze(2), [NS, HS, HP])
            V.tensor_copy(heads(da[:]), per_head(g.edta[:])).then_inc(pre, 1)
            dve.wait_ge(rows_kept, 1)
            V.tensor_tensor(heads(dtx[:]), heads(xr[:]), per_head(g.dt[0:NS, NT, :]), ALU.mult).then_inc(pre, 1)
            dve.wait_ge(turn_kept, 1)
            dve.wait_ge(S_in, 16)
            for b in range(NS):
                s_b = S[:, b]
                ch.mark(V.tensor_tensor(s_b, s_b, bcast(turned[:, 1, :, b:b + 1], [P, HC, P]), ALU.mult))
                dve.wait_ge(bc_ps, b + 1)
                row = lambda n: bcast(g.bank(4 + b % 2, cols=2 * P, at=n * 2 * P).rearrange(
                    "p (g n) -> p g n", g=2).unsqueeze(2), [P, 2, HC // 2, P])
                by_group = lambda ap: ap.rearrange("p (g r) n -> p g r n", g=2)
                ch.step(V.tensor_tensor(by_group(t[:]), row(0), by_group(bcast(turned[:, 0, :, b:b + 1], [P, HC, P])),
                                        ALU.mult))
                ch.step(V.tensor_tensor(s_b, s_b, t[:], ALU.add))
                ch.step(V.tensor_tensor(by_group(t[:]), by_group(s_b), row(1), ALU.mult))
                V.tensor_reduce(yT[:, :, b:b + 1].squeeze(2), t[:], AXX, ALU.add).then_inc(s_new, 1)
                dve.wait_ge(s_new, b + 1)
            dve.wait_ge(small_in, 96)
            dve.wait_ge(yT_ps, 1)
            ch.step(V.tensor_tensor(heads(xr[:]), heads(xr[:]), per_head(dskip[:]), ALU.mult))
            ch.step(V.tensor_tensor(y[:], g.ps[0:NS, 0:D], xr[:], ALU.add))
            V.tensor_tensor(y[:], y[:], zgv[:, 0, :], ALU.mult).then_inc(y_done, 1)
            ch.step(V.tensor_scalar(qk[:, 0:GH, :], qk[:, 0:GH, :], QS, None, ALU.mult))
            ch.mark(V.tensor_tensor(qpad[:], bcast(qk[:, 0:GH, :].unsqueeze(3), [P, GH, NS, NS]),
                                    bcast(g.eye8[:].unsqueeze(1), [P, GH, NS, NS]), ALU.mult))
            dve.wait_ge(GS_in, 16)
            dve.wait_ge(e_ready, 1)
            tv = t[:].rearrange("p c n -> p (c n)").rearrange("p (h v) -> p h v", h=GH)
            for b in range(NS):
                gs_b = GS[:, b]
                ch.mark(V.tensor_tensor(gs_b, gs_b, bcast(ela[:, :, b:b + 1], [P, GH, GV]), ALU.mult))
                dve.wait_ge(v_ps, b + 1)
                ch.step(V.tensor_tensor(tv, g.ps[:, 6 * 512:8 * 512].rearrange("p (h v) -> p h v", h=GH),
                                        bcast(qk[:, GH:NQK, b:b + 1], [P, GH, GV]), ALU.mult))
                V.tensor_tensor(gs_b, gs_b, tv, ALU.add).then_inc(g_new, 1)
                dve.wait_ge(g_new, b + 1)
            out.prepare(dve)
            dve.wait_ge(yr, 1)
            for c in range(2):
                cols = slice(c * 512, (c + 1) * 512)
                stt(out=out.cat[0:NS, cols], in0=y[:, cols], scalar=r[:, c:c + 1], in1=ssdn[:, cols],
                    op0=ALU.mult, op1=ALU.mult)
            dve.wait_ge(o_r, 1)
            for h in range(GH):
                ins = stt(out=out.cat[0:NS, D + h * GV:D + (h + 1) * GV],
                          in0=g.ps[0:NS, 4 * 512 + h * GV:4 * 512 + (h + 1) * GV], scalar=r[:, 2 + h:3 + h],
                          in1=glan[:], op0=ALU.mult, op1=ALU.mult)
            ch.step(ins)
            V.tensor_tensor(out.cat[0:NS, D:2 * D], out.cat[0:NS, D:2 * D], zgv[:, 1, :], ALU.mult).then_inc(out.cat_ready, 1)
            out.residual(dve, 0, True)
            out.modulate(dve, 0, True)



class Router:

    VSTEPS = 36

    def __init__(self, g, st):
        nc = g.nc
        self.g = g
        sb = lambda n, s, dt=F32: st.enter_context(nc.sbuf_tensor("r_" + n, s, dt))
        sem = lambda n: g.sem("r_" + n)
        self.wq, self.keys = sb("wq", [P, 4, KD, 512]), sb("keys", [P, 2 * PH, P])
        self.h2 = sb("h2", [P, D])
        self.h2T, self.qT = sb("h2T", [P, KD, P]), sb("qT", [P, 2 * PH, P])
        self.work = sb("work", [P, 2 * PH, P])
        self.v, self.iu, self.inum = (sb("v", [P, 2 * PH, TOPK]), sb("iu", [P, 2 * PH, TOPK], U32),
                                      sb("inum", [P, 2 * PH, TOPK]))
        self.top, self.pos = sb("top", [P, PH, TOPK]), sb("pos", [P, PH, TOPK], U32)
        self.part = sb("part", [P, 2, PH, TOPK], U32)
        self.row = sb("row", [P, 2, PH, TOPK])
        self.total, self.e = sb("total", [P, PH]), sb("e", [P, PH, TOPK])
        self.gate, self.num = sb("gate", [P, SLOTS]), sb("num", [P, SLOTS])
        self.idx = sb("idx", [P, SLOTS], U32)
        self.wq_in, self.keys_in, self.h2_in = [sem(f"wq_in{b}") for b in range(4)], sem("keys_in"), sem("h2_in")
        self.h2T_ps, self.h2T_kept, self.q_ps, self.q_kept = sem("h2T_ps"), sem("h2T_kept"), sem("q_ps"), sem("q_kept")
        self.s_ps, self.s_kept, self.vch = sem("s_ps"), sem("s_kept"), sem("vch")
        self.shifted, self.e_ready, self.chosen, self.numbered, self.gated = (
            sem("shifted"), sem("e_ready"), sem("chosen"), sem("numbered"), sem("gated"))

    def load_constants(self, sp):
        for b in range(4):
            sp.dma_start(self.wq[:, b], self.g.io["w_query"][b]).then_inc(self.wq_in[b], 16)
            if b == 0:
                sp.dma_start(self.keys[:], self.g.io["sub_keys"]).then_inc(self.keys_in, 16)

    def tensor(self, pe, n):
        g, nc = self.g, self.g.nc
        pe.wait_ge(self.h2_in, n * 16 + 16)
        for k in range(KD):
            last = nc.tensor.transpose(g.ps[:, 2 * 512 + k * P:2 * 512 + (k + 1) * P], self.h2[:, k * P:(k + 1) * P],
                                       g.ident[:])
        last.then_inc(self.h2T_ps, 1)
        yield
        pe.wait_ge(self.h2T_kept, n + 1)

        def scores(b):
            pe.wait_ge(self.keys_in, 16)
            pe.wait_ge(self.q_kept, n * 4 + b + 1)
            for m in range(4):
                u = b * 4 + m
                last = nc.tensor.matmul(g.bank(4 + b, cols=P, at=m * P), self.qT[:, u, :],
                                        self.keys[:, u, :], start=True, stop=True)
            last.then_inc(self.s_ps, 1)

        for b in range(4):
            pe.wait_ge(self.wq_in[b], 16)
            for m in range(4):
                for k in range(KD):
                    last = nc.tensor.matmul(g.bank(4 + b, cols=P, at=m * P), self.wq[:, b, k, m * P:(m + 1) * P],
                                            self.h2T[:, k, :], start=(k == 0), stop=(k == KD - 1))
                if m == 3:
                    last.then_inc(self.q_ps, 1)
                if m % 2:
                    yield
            if b:
                scores(b - 1)
                yield
        scores(3)
        yield

    def scalar(self, act, n):
        g, A = self.g, self.g.nc.scalar.activation
        act.wait_ge(self.h2T_ps, n + 1)
        A(self.h2T[:].rearrange("p k r -> p (k r)"), g.ps[:, 2 * 512:4 * 512], ACT.Copy).then_inc(self.h2T_kept, 1)
        yield

        def scores(b):
            act.wait_ge(self.s_ps, n * 4 + b + 1)
            A(self.work[:, b * 4:(b + 1) * 4, :].rearrange("p k r -> p (k r)"), g.bank(4 + b),
              ACT.Copy).then_inc(self.s_kept, 1)

        for b in range(4):
            act.wait_ge(self.q_ps, n * 4 + b + 1)
            A(self.qT[:, b * 4:(b + 1) * 4, :].rearrange("p k r -> p (k r)"), g.bank(4 + b), ACT.Copy).then_inc(self.q_kept, 1)
            yield
            if b:
                scores(b - 1)
                yield
        scores(3)
        yield
        act.wait_ge(self.shifted, n + 1)
        A(self.e[:], self.e[:], ACT.Exp).then_inc(self.e_ready, 1)
        yield

    def top16(self, ch, vals, idxs, src, us):
        V = self.g.nc.vector
        for first in (0, 8):
            for u in us:
                last = V.max(vals[:, u, first:first + 8], src(u))
            ch.step_apart(last)
            yield
            for u in us:
                last = V.max_index(idxs[:, u, first:first + 8], vals[:, u, first:first + 8], src(u))
            ch.step_apart(last)
            yield
            if first == 0:
                for u in us:
                    last = V.match_replace(src(u), vals[:, u, 0:8], src(u), LOWEST)
                ch.step_apart(last)
                yield

    def vector(self, dve, n):
        V = self.g.nc.vector
        ch = Chain(dve, self.vch, n * self.VSTEPS)
        for b in range(4):
            wait_apart(dve, self.s_kept, n * 4 + b + 1)
            yield from self.top16(ch, self.v, self.iu, lambda u: self.work[:, u, :], range(b * 4, b * 4 + 4))
        ch.mark(V.tensor_copy(self.inum[:], self.iu[:]))
        sides = self.v[:].rearrange("p (h s) k -> p h s k", s=2)
        pair = [P, PH, TOPK, TOPK]
        cand = self.work[:].rearrange("p (h s) k -> p h (s k)", s=2)
        square = cand.rearrange("p h (a b) -> p h a b", b=TOPK)
        ch.step_apart(V.tensor_tensor(square, bcast(sides[:, :, 0, :].unsqueeze(3), pair),
                                bcast(sides[:, :, 1, :].unsqueeze(2), pair), ALU.add))
        yield
        yield from self.top16(ch, self.top, self.pos, lambda h: cand[:, h, :], range(PH))
        V.tensor_tensor(self.e[:], self.top[:], bcast(self.top[:, :, 0:1], [P, PH, TOPK]),
                        ALU.subtract).then_inc(self.shifted, 1)
        ch.mark(V.tensor_single_scalar(self.part[:, 0], self.pos[:], 4, ALU.logical_shift_right))
        ch.step(V.tensor_single_scalar(self.part[:, 1], self.pos[:], TOPK - 1, ALU.bitwise_and))
        yield
        numbers = self.inum[:].rearrange("p (h s) k -> p h s k", s=2)
        for side in range(2):
            hit = square
            ch.step(V.tensor_tensor(hit, bcast(self.g.iota16[:].unsqueeze(1).unsqueeze(1), pair),
                                    bcast(self.part[:, side].unsqueeze(3), pair), ALU.is_equal))
            yield
            ch.step(V.tensor_tensor(hit, hit, bcast(numbers[:, :, side, :].unsqueeze(2), pair), ALU.mult))
            summed = V.tensor_reduce(self.row[:, side], hit, AXX, ALU.add)
            if side == 0:
                ch.step(summed)
                yield
        summed.then_inc(self.chosen, 1)
        dve.wait_ge(self.chosen, n * 2 + 1)
        V.scalar_tensor_tensor(out=self.num[:], in0=self.row[:, 0].rearrange("p h k -> p (h k)"),
                               scalar=float(P), in1=self.row[:, 1].rearrange("p h k -> p (h k)"),
                               op0=ALU.mult, op1=ALU.add).then_inc(self.chosen, 1)
        dve.wait_ge(self.chosen, n * 2 + 2)
        V.tensor_copy(self.idx[:], self.num[:]).then_inc(self.numbered, 1)
        yield
        dve.wait_ge(self.e_ready, n + 1)
        ch.step(V.tensor_reduce(self.total[:], self.e[:], AXX, ALU.add))
        ch.step(V.reciprocal(self.total[:], self.total[:]))
        assert ch.n == self.VSTEPS, ch.n
        V.tensor_tensor(self.gate[:].rearrange("p (h k) -> p h k", k=TOPK), self.e[:],
                        bcast(self.total[:].unsqueeze(2), [P, PH, TOPK]), ALU.mult).then_inc(self.gated, 1)
        yield


class Finish:

    def __init__(self, g, st):
        self.g = g
        sb = lambda n, s: st.enter_context(g.nc.sbuf_tensor("f_" + n, s, F32))
        sem = lambda n: g.sem("f_" + n)
        self.x1, self.gate2, self.final, self.y = sb("x1", [P, D]), sb("gate2", [P, D]), sb("final", [P, D]), sb("y", [P, D])
        self.ms, self.r = sb("ms", [P, 2]), sb("r", [P, 1])
        self.consts_in, self.x1_in, self.ach = sem("consts_in"), sem("x1_in"), sem("ach")
        self.sum_read, self.x2_ready, self.r_ready, self.y_ready = (sem("sum_read"), sem("x2_ready"), sem("r_ready"),
                                                                    sem("y_ready"))
        self.stored = sem("stored")

    def add(self, dve, n, rs):
        g, V = self.g, self.g.nc.vector
        dve.wait_ge(self.x1_in, n * 16 + 16)
        dve.wait_ge(self.stored, n * 16 + 16)
        V.tensor_tensor(self.y[0:rs, :], g.ps[0:rs, 0:D], self.gate2[0:rs, :], ALU.mult).then_inc(self.sum_read, 1)
        dve.wait_ge(self.sum_read, n + 1)
        V.tensor_tensor(self.x1[0:rs, :], self.y[0:rs, :], self.x1[0:rs, :], ALU.add).then_inc(self.x2_ready, 1)

    def scale(self, dve, n, rs):
        dve.wait_ge(self.r_ready, n + 1)
        self.g.nc.vector.scalar_tensor_tensor(out=self.y[0:rs, :], in0=self.x1[0:rs, :], scalar=self.r[0:rs, :],
                                              in1=self.final[0:rs, :], op0=ALU.mult, op1=ALU.mult).then_inc(self.y_ready, 1)

    def scalar(self, act, n, rs):
        g, A = self.g, self.g.nc.scalar.activation
        act.wait_ge(self.x2_ready, n + 1)
        ch = Chain(act, self.ach, n * 2)
        ch.step(A(self.y[0:rs, :], self.x1[0:rs, :], ACT.Square, accum_out=self.ms[0:rs, 0:1]))
        ch.step(A(self.ms[0:rs, 1:2], self.ms[0:rs, 0:1], ACT.Ln, scale=1.0 / D, bias=g.eps[0:rs, :]))
        A(self.r[0:rs, :], self.ms[0:rs, 1:2], ACT.Exp, scale=-0.5).then_inc(self.r_ready, 1)
        act.wait_ge(self.r_ready, n + 1)


PE_PIECES = {q: 1 for q in range(1, 14)}
ACT_PIECES = {q: 1 for q in (2, 4, 6, 7, 9, 10, 12, 13, 14, 22)}
DVE_PIECES = {8: 2, 9: 3, 11: 2, 12: 3, 14: 2, 15: 3, 16: 2, 17: 3, **{q: 2 for q in range(18, 25)}}


def drive(pieces, count):
    for _ in range(count):
        next(pieces, None)


def experts(g):
    nc, io = g.nc, g.io
    NG = SLOTS // GROUP
    with ExitStack() as st:
        sb = lambda n, s, dt=F32: st.enter_context(nc.sbuf_tensor("e_" + n, s, dt))
        sem = lambda n: g.sem("e_" + n)
        rt, fin = Router(g, st), Finish(g, st)
        buf = [sb(f"buf{s}", [P, 2 * D]) for s in range(RING)]
        idx, gate, h2 = sb("idx", [P, SLOTS], U32), sb("gate", [P, SLOTS]), sb("h2", [P, D])
        dots, acts, wts = sb("dots", [P, SLOTS]), sb("acts", [P, SLOTS]), sb("wts", [P, SLOTS])
        diag = sb("diag", [P, RING, P])
        h2_kept, idx_kept, generated = sem("h2_kept"), sem("idx_kept"), sem("generated")
        landed = [sem(f"landed{s}") for s in range(RING)]
        dotted, wch, weighed, summed = sem("dotted"), sem("wch"), sem("weighed"), sem("summed")
        idxT, turned = sb("idxT", [P, NS], U32), sb("turned", [P, 2, NS])
        wpad = sb("wpad", [P, NS, NS])
        turn_ps, turn_kept, idxT_ready, spread_in, gates_in = (sem("turn_ps"), sem("turn_kept"), sem("idxT_ready"),
                                                               sem("spread_in"), sem("gates_in"))
        s_dotted, s_acted, s_weighed, s_summed = sem("s_dotted"), sem("s_acted"), sem("s_weighed"), sem("s_summed")
        wide = rt.wq[:].rearrange("p n k c -> p (n k c)")
        spread = lambda b: wide[:, b * D:(b + 1) * D]
        block = st.enter_context(nc.Block())
        PER = 16 * (SLOTS // RING)

        @block.sync
        def _(sp):
            sp.sem_inc(fin.stored, 16)
            sp.dma_start(rt.h2[:], g.h2_d[0:P, :]).then_inc(rt.h2_in, 16)
            rt.load_constants(sp)
            sp.dma_start(fin.gate2[:], g.mod_d[NS, 5 * D:6 * D].partition_broadcast(P)).then_inc(fin.consts_in, 16)
            sp.dma_start(fin.final[:], io["norm_final"].partition_broadcast(P)).then_inc(fin.consts_in, 16)

            def store_y(n):
                sp.wait_ge(fin.y_ready, n + 1)
                sp.dma_start(io["y_p"][bass.ds(n * P, P), :], fin.y[:]).then_inc(fin.stored, 16)

            def tile(n, first):
                sp.wait_ge(h2_kept, n + 1)
                sp.dma_start(rt.h2[:], g.h2_d[bass.ds(n * P + P, P), :]).then_inc(rt.h2_in, 16)
                if not first:
                    store_y(n - 1)
                sp.dma_start(fin.x1[:], g.x1_d[bass.ds(n * P, P), :]).then_inc(fin.x1_in, 16)

            tile(0, True)
            with sp.Fori(1, NT) as n:
                tile(n, False)
            sp.wait_ge(rt.q_ps, 4 * (NT + 1))
            for b in range(NS):
                sp.dma_start(spread(b), g.h2_d[SEQ + b, :].partition_broadcast(P)).then_inc(spread_in, 16)
            sp.wait_ge(fin.sum_read, NT)
            sp.dma_start(fin.gate2[0:NS, :], g.mod_d[0:NS, 5 * D:6 * D]).then_inc(gates_in, 16)
            store_y(NT - 1)
            sp.dma_start(fin.x1[0:NS, :], g.x1_d[SEQ:ROWS, :]).then_inc(fin.x1_in, 16)
            sp.wait_ge(fin.y_ready, NT + 1)
            sp.dma_start(io["y_s"], fin.y[0:NS, :]).then_inc(fin.stored, 16)
            sp.wait_ge(fin.stored, 16 * (NT + 2))

        @block.gpsimd
        def _(pool):
            def gather(s, numbers, **kw):
                return pool.indirect_dma_start(out=buf[s][:], out_offset=None, in_=io["experts"],
                                               in_offset=bass.IndirectOffsetOnAxis(ap=numbers, axis=0), **kw)

            def tile(n):
                wait_apart(pool, rt.numbered, n + 1)
                nc.gpsimd.tensor_copy(idx[:, 0:SLOTS - RING], rt.idx[:, 0:SLOTS - RING]).then_inc(idx_kept, 1)
                wait_apart(pool, idx_kept, n * 2 + 1)
                for k in range(SLOTS):
                    wait_apart(pool, summed, n * SLOTS + k + 1)
                    if k == RING:
                        nc.gpsimd.tensor_copy(idx[:, SLOTS - RING:], rt.idx[:, SLOTS - RING:]).then_inc(idx_kept, 1)
                        wait_apart(pool, idx_kept, n * 2 + 2)
                    gather(k % RING, idx[:, k:k + 1]).then_inc(landed[k % RING], 16)

            with pool.Fori(0, NT) as n:
                tile(n)
            pool.wait_ge(idxT_ready, 1)
            for b in range(NS):
                wait_apart(pool, summed, NT * SLOTS + b + 1)
                gather(b % RING, idxT[:, b:b + 1]).then_inc(landed[b % RING], 16)

        @block.tensor
        def _(pe):
            pe.sem_inc(summed, RING)
            drive(rt.tensor(pe, 0), 99)
            def tile(n, first):
                route = rt.tensor(pe, n + 1)
                for k in range(SLOTS):
                    if k == 0 and not first:
                        pe.wait_ge(fin.sum_read, n)
                    pe.wait_ge(weighed, n * SLOTS + k + 1)
                    for cols in range(2):
                        last = nc.tensor.matmul(g.bank(cols), diag[:, k % RING, :],
                                                buf[k % RING][:, D + cols * 512:D + (cols + 1) * 512],
                                                start=(k == 0), stop=(k == SLOTS - 1))
                    last.then_inc(summed, 1)
                    if k % GROUP == GROUP - 1:
                        drive(route, PE_PIECES.get(k // GROUP, 0))

            tile(0, True)
            with pe.Fori(1, NT) as n:
                tile(n, False)
            pe.wait_ge(rt.gated, NT + 1)
            for m, src in enumerate((rt.num, rt.gate)):
                last = nc.tensor.transpose(g.bank(2, cols=NS, at=m * NS), src[0:NS, :], g.ident[0:NS, 0:NS])
            last.then_inc(turn_ps, 1)
            pe.wait_ge(fin.sum_read, NT)
            for b in range(NS):
                pe.wait_ge(s_weighed, b + 1)
                for cols in range(2):
                    last = nc.tensor.matmul(g.bank(cols, rows=NS), wpad[:, b, :],
                                            buf[b % RING][:, D + cols * 512:D + (cols + 1) * 512],
                                            start=(b == 0), stop=(b == NS - 1))
                last.then_inc(s_summed, 1)

        @block.scalar
        def _(act):
            A = nc.scalar.activation
            drive(rt.scalar(act, 0), 99)
            def tile(n, first):
                ch = Chain(act, wch, n * (1 + 2 * NG))
                route = rt.scalar(act, n + 1)
                act.wait_ge(rt.gated, n + 1)
                ch.step(A(gate[:], rt.gate[:], ACT.Copy))
                for q in range(NG):
                    ks = slice(q * GROUP, (q + 1) * GROUP)
                    act.wait_ge(dotted, n * SLOTS + (q + 1) * GROUP)
                    ch.step(A(acts[:, ks], dots[:, ks], ACT.Gelu))
                    for k in range(q * GROUP, (q + 1) * GROUP):
                        last = A(wts[:, k:k + 1], acts[:, k:k + 1], ACT.Copy, scale=gate[:, k:k + 1])
                    ch.step(last)
                    for k in range(q * GROUP, (q + 1) * GROUP):
                        act.wait_ge(summed, n * SLOTS + k + 1)
                        A(diag[:, k % RING, :], g.ident[:], ACT.Copy, scale=wts[:, k:k + 1]).then_inc(weighed, 1)
                    drive(route, ACT_PIECES.get(q, 0))
                    if q == 0 and not first:
                        fin.scalar(act, n - 1, P)

            tile(0, True)
            with act.Fori(1, NT) as n:
                tile(n, False)
            act.wait_ge(turn_ps, 1)
            A(turned[:].rearrange("p a b -> p (a b)"), g.bank(2, cols=2 * NS), ACT.Copy).then_inc(turn_kept, 1)
            fin.scalar(act, NT - 1, P)
            for b in range(NS):
                act.wait_ge(s_dotted, b + 1)
                A(wts[:, b:b + 1], dots[:, b:b + 1], ACT.Gelu).then_inc(s_acted, 1)
            fin.scalar(act, NT, NS)

        @block.vector
        def _(dve):
            V = nc.vector

            def dot(s, row, out, sem):
                down = buf[s][:, 0:D]
                V.scalar_tensor_tensor(out=down, in0=down, scalar=1.0, in1=row, op0=ALU.mult, op1=ALU.mult,
                                       accum_out=out).then_inc(sem, 1)

            drive(rt.vector(dve, 0), 99)
            dve.wait_ge(fin.consts_in, 32)
            def tile(n, first):
                route = rt.vector(dve, n + 1)
                if not first:
                    dve.wait_ge(dotted, n * SLOTS)
                V.tensor_copy(h2[:], rt.h2[:]).then_inc(h2_kept, 1)
                dve.wait_ge(h2_kept, n + 1)
                for k in range(SLOTS):
                    dve.wait_ge(landed[k % RING], n * PER + 16 * (k // RING) + 16)
                    dot(k % RING, h2[:], dots[:, k:k + 1], dotted)
                    if k % GROUP == GROUP - 1:
                        drive(route, DVE_PIECES.get(k // GROUP, 0))
                    if k == GROUP - 1 and not first:
                        dve.wait_ge(summed, n * SLOTS + RING)
                        fin.add(dve, n - 1, P)
                    if k == 2 * GROUP - 1 and not first:
                        fin.scale(dve, n - 1, P)

            tile(0, True)
            with dve.Fori(1, NT) as n:
                tile(n, False)
            dve.wait_ge(turn_kept, 1)
            V.tensor_copy(idxT[:], turned[:, 0, :]).then_inc(idxT_ready, 1)
            dve.wait_ge(summed, NT * SLOTS + RING)
            fin.add(dve, NT - 1, P)
            fin.scale(dve, NT - 1, P)
            dve.wait_ge(spread_in, 16 * NS)
            dve.wait_ge(gates_in, 16)

            def weigh(b):
                dve.wait_ge(s_acted, b + 1)
                V.scalar_tensor_tensor(out=wpad[:, b, :], in0=g.eye8[:, b, :], scalar=wts[:, b:b + 1],
                                       in1=bcast(turned[:, 1, b:b + 1], [P, NS]), op0=ALU.mult,
                                       op1=ALU.mult).then_inc(s_weighed, 1)

            for b in range(NS):
                dve.wait_ge(landed[b % RING], NT * PER + 16 * (b // RING + 1))
                dot(b % RING, spread(b), dots[:, b:b + 1], s_dotted)
                if b:
                    weigh(b - 1)
            weigh(NS - 1)
            dve.wait_ge(s_summed, NS)
            fin.add(dve, NT, NS)
            fin.scale(dve, NT, NS)


def build(nc, io):
    with ExitStack() as stack:
        g = Prog(nc, stack, io)
        with ExitStack() as st:
            hT = st.enter_context(nc.sbuf_tensor("hT", [P, KD, ROWS], F32))
            with ExitStack() as rows:
                x = rows.enter_context(nc.sbuf_tensor("x_rows", [P, NT + 1, D], F32))
                r = rows.enter_context(nc.sbuf_tensor("x_rms", [P, NT + 1], F32))
                g.phase(modulation, x, r)
                g.phase(norm_in, x, r, hT)
            g.phase(projections, hT)
        g.phase(mix_sample)
        g.phase(mix_prompt)
        g.phase(experts)


def laid_out(np, x):
    f = {k: np.asarray(v) for k, v in x.items()}
    chunks = lambda w, n: w.reshape(KD, P, w.shape[1] // n, n).transpose(2, 1, 0, 3)
    wide = lambda w: w.reshape(w.shape[0] // P, P, w.shape[1]).transpose(1, 0, 2)
    w_in = f["w_in"][0]
    cuts = np.cumsum([0, D, NXBC * P, HS, GH * P, GH * P, D, D, 16])
    z, xbc, dt, q, k, v, go, gate = (w_in[:, a:b] for a, b in zip(cuts[:-1], cuts[1:]))
    per_chunk = lambda a: a.reshape(-1, NXBC, P).transpose(1, 2, 0)
    heads = lambda s: s.transpose(3, 0, 1, 2)
    return {
        "c_all": np.concatenate([f["c_sample"], f["c_prompt"]]),
        "w_mod": chunks(f["w_mod"][0], 512), "b_mod": f["b_mod"][0],
        "norm_mix": f["norm_mix"][0], "norm_ffn": f["norm_ffn"][0], "norm_final": f["norm_final"],
        "x_prompt": f["x_prompt"][0], "x_sample": f["x_sample"][:, 0],
        "w_chan": chunks(np.concatenate([xbc, q, k], axis=1), P),
        "w_rows": chunks(np.concatenate([z, go, v], axis=1), 512),
        "w_dt": wide(dt), "w_gate": wide(gate),
        "conv_par": np.concatenate([per_chunk(f["w_conv"][0]), per_chunk(f["b_conv"][0]),
                                    per_chunk(f["state_conv"][0].transpose(1, 0, 2))], axis=2),
        "dt_bias": f["dt_bias"][0], "a_log": f["a_log"][0],
        "w_gate_up": f["w_gate_up"][0], "b_gate": f["b_gate"][0].reshape(GH, P).T,
        "state_ssm": f["state_ssm"][0].reshape(NS, HS // 2, P, P).transpose(2, 0, 1, 3),
        "state_gla": f["state_gla"][0].transpose(2, 0, 1, 3),
        "d_skip": f["d_skip"][0], "ssd_norm": f["ssd_norm"][0], "gla_norm": f["gla_norm"][0],
        "w_out": wide(f["w_out"][0]),
        "w_query": chunks(f["w_query"][0], 512),
        "sub_keys": np.stack([f["sub_keys1"][0], f["sub_keys2"][0]], axis=1).reshape(2 * PH, P, P).transpose(2, 0, 1),
        "experts": np.concatenate([f["expert_down"][0], f["expert_up"][0]], axis=1),
    }


OUTS = {"y_p": (SEQ, D), "y_s": (NS, D), "conv_p": (NXBC, P, 3), "ssm_p": (P, HS * HP), "gla_p": (P, GH * GV),
        "conv_s": (NXBC, P, 3 * NS), "ssm_s": (P, NS, HS // 2, P), "gla_s": (P, NS, GH, GV)}


def program(nc, arrays):
    io = {}
    for n, a in arrays.items():
        io[n] = nc.dram_tensor(f"in_{n}", a.shape, mybir.dt.from_np(a.dtype), kind="ExternalInput").ap()
    for n, shape in OUTS.items():
        io[n] = nc.dram_tensor(f"out_{n}", shape, F32, kind="ExternalOutput").ap()
    build(nc, io)


def kernel(**inputs):
    import numpy as np
    import concourse.bacc as bacc
    from concourse.bass_utils import run_bass_kernel_spmd

    nc = bacc.Bacc("TRN2", target_bir_lowering=False, num_devices=1)
    arrays = {n: np.ascontiguousarray(a) for n, a in laid_out(np, inputs).items()}
    program(nc, arrays)
    r = run_bass_kernel_spmd(nc, [{f"in_{n}": a for n, a in arrays.items()}], core_ids=[0]).results[0]
    o = {n: np.asarray(r[f"out_{n}"]) for n in OUTS}
    state = lambda a: a.reshape(NXBC * P, 3, -1).transpose(2, 1, 0)[None]
    return (o["y_p"][None], o["y_s"][:, None], state(o["conv_p"]),
            o["ssm_p"].T.reshape(1, 1, HS, HP, P), o["gla_p"].reshape(P, GH, GV).transpose(1, 0, 2)[None, None],
            state(o["conv_s"]), o["ssm_s"].transpose(1, 2, 0, 3).reshape(1, NS, HS, HP, P),
            o["gla_s"].transpose(1, 2, 0, 3)[None])
```

```python
from contextlib import ExitStack

import concourse.bass as bass
from concourse import mybir

F32 = mybir.dt.float32
F32R = mybir.dt.float32r
U32 = mybir.dt.uint32
ACT = mybir.ActivationFunctionType
ALU = mybir.AluOpType
AXX = mybir.AxisListType.X

P = 128
D = 1024
KD = D // P
SEQ = 1024
NT = SEQ // P
NS = 8
ROWS = SEQ + NS
TILED = (NT + 1) * P
THIRD = ROWS // 3
MODS = 6 * D
NXBC = 12
NQK = 8
HS = 16
HP = 64
GH = 4
GV = 256
HALF = 64
PH = 8
TOPK = 16
SLOTS = PH * TOPK
RING = 8
GROUP = 4
EPS = 1e-6
LOWEST = -3.0e38


def bcast(ap, shape):
    return ap.to_broadcast(shape)


def wait_apart(eng, sem, value):
    eng.wait_ge(sem, value)
    eng.nop(nofuse=True)


def split_high(nc, high, x):
    return nc.vector.tensor_copy(high, x)


def split_low(nc, low, high, x):
    return nc.vector.tensor_tensor(low, x, high.bitcast(F32), ALU.subtract)


def matmul_split(nc, out, lhsT, rhs, start, stop):
    nc.tensor.matmul(out, lhsT[0], rhs[0], start=start, stop=False)
    nc.tensor.matmul(out, lhsT[0], rhs[1], start=False, stop=False)
    return nc.tensor.matmul(out, lhsT[1], rhs[0], start=False, stop=stop)


class Chain:

    def __init__(self, eng, sem, base=0):
        self.eng, self.sem, self.base, self.n = eng, sem, base, 0

    def step(self, ins):
        ins.then_inc(self.sem, 1)
        self.n += 1
        self.eng.wait_ge(self.sem, self.base + self.n)

    def step_apart(self, ins):
        ins.then_inc(self.sem, 1)
        self.n += 1
        wait_apart(self.eng, self.sem, self.base + self.n)

    def mark(self, ins):
        ins.then_inc(self.sem, 1)
        self.n += 1

    def join(self):
        self.eng.wait_ge(self.sem, self.base + self.n)


class Prog:

    def __init__(self, nc, stack, io):
        self.nc, self.io = nc, io
        self.stack = stack
        d = lambda name, shape: nc.dram_tensor(name, shape, F32, kind="Internal").ap()
        self.mod_d = d("mod_d", (NS + 1, MODS))
        self.proj_d = d("proj_d", (ROWS, 3, D))
        self.xbc_d = d("xbc_d", (NXBC, P, ROWS))
        self.qk_d = d("qk_d", (NQK, P, ROWS))
        self.cum_d = d("cum_d", (GH, P, ROWS))
        self.x1_d = d("x1_d", (ROWS, D))
        self.h2_d = d("h2_d", (TILED, D))
        s = lambda name, shape: stack.enter_context(nc.sbuf_tensor(name, shape, F32))
        self.ident = s("ident", [P, P])
        self.tri = s("tri", [P, P])
        self.later = s("later", [P, P])
        self.blk = s("blk", [P, P])
        self.ones = s("ones", [P, P])
        self.sel8 = s("sel8", [NS, NS, P])
        self.eye8 = s("eye8", [P, NS, NS])
        self.iota16 = s("iota16", [P, TOPK])
        self.eps = s("eps", [P, 1])
        self.dt = s("dt", [P, NT + 1, HS])
        self.dta = s("dta", [P, NT + 1, HS])
        self.ecum = s("ecum", [P, NT, HS])
        self.etoend = s("etoend", [P, NT, HS])
        self.etot = s("etot", [P, NT, HS])
        self.edta = s("edta", [NS, HS])
        self.ps = stack.enter_context(nc.psum_tensor("ps", [P, 8 * 512], F32))

    def sem(self, name):
        handle = self.nc.alloc_semaphore(name=name)
        self.sems.append(handle)
        return handle

    def phase(self, emit, *args):
        self.sems = []
        emit(self, *args)
        self.nc.clear_and_free_semaphores(self.sems)
        self.nc.all_engine_barrier()

    def bank(self, n, rows=P, cols=512, at=0):
        return self.ps[0:rows, n * 512 + at:n * 512 + at + cols]


def modulation(g, x, r):
    nc, io = g.nc, g.io
    NB = MODS // 512
    with ExitStack() as st:
        sb = lambda n, s: st.enter_context(nc.sbuf_tensor(n, s, F32))
        sem = lambda n: g.sem(n)
        c_sb = sb("c_sb", [NS + 1, D])
        sc_sb = sb("sc_sb", [NS + 1, D])
        cT = sb("cT", [P, KD, NS + 1])
        w = sb("w_mod_sb", [P, 2, KD, 512])
        bm = sb("bm", [NS + 1, MODS])
        mod = sb("mod", [NS + 1, MODS])
        sq, ms, lr = sb("m_sq", [P, D]), sb("m_ms", [P, NT + 1]), sb("m_lr", [P, NT + 1])
        x_in = [sem(f"m_x_in{t}") for t in range(NT)]
        xs_in, ms_set, squared, logged, r_ready = (sem("m_xs_in"), sem("m_ms_set"),
                                                   sem("m_squared"), sem("m_logged"), sem("m_r_ready"))
        c_in, bm_in = sem("m_c_in"), sem("m_bm_in")
        w_in = [sem("m_w_in0"), sem("m_w_in1")]
        consts0, consts = sem("m_consts0"), sem("m_consts")
        silu_done, cT_ps, cT_done = sem("m_silu_done"), sem("m_cT_ps"), sem("m_cT_done")
        prod, summed, stored = sem("m_prod"), sem("m_summed"), sem("m_stored")
        block = st.enter_context(nc.Block())

        @block.sync
        def _(sp):
            sp.dma_start(c_sb[:], io["c_all"]).then_inc(c_in, 16)
            sp.dma_start(bm[:], io["b_mod"].partition_broadcast(NS + 1)).then_inc(bm_in, 16)
            for b in range(2):
                sp.dma_start(w[:, b], io["w_mod"][b]).then_inc(w_in[b], 16)
            sp.dma_start(x[0:NS, NT, :], io["x_sample"]).then_inc(xs_in, 16)

            for n in range(2, NB):
                sp.wait_ge(prod, n - 1)
                sp.dma_start(w[:, n % 2], io["w_mod"][n]).then_inc(w_in[n % 2], 16)
                if n - 2 < NT:
                    t = n - 2
                    sp.dma_start(x[:, t, :], io["x_prompt"][t * P:(t + 1) * P, :]).then_inc(x_in[t], 16)
            sp.wait_ge(summed, NB)
            sp.dma_start(g.mod_d, mod[:]).then_inc(stored, 16)
            sp.wait_ge(stored, 16)

        @block.gpsimd
        def _(pool):
            for t, v in ((g.ident, 0.0), (g.tri, 1.0), (g.later, 1.0), (g.ones, 1.0),
                         (g.sel8, 1.0), (g.eye8, 1.0), (g.eps, EPS)):
                nc.gpsimd.memset(t[:], v).then_inc(consts0, 1)
            nc.gpsimd.iota(g.iota16[:], [[1, TOPK]], base=0, channel_multiplier=0,
                           allow_small_or_imprecise_dtypes=True).then_inc(consts0, 1)
            pool.wait_ge(consts0, 8)
            sel = nc.gpsimd.affine_select
            sel(out=g.ident[:], in_=g.ident[:], compare_op=ALU.not_equal, fill=1.0, base=0,
                pattern=[[-1, P]], channel_multiplier=1).then_inc(consts, 1)
            sel(out=g.tri[:], in_=g.tri[:], compare_op=ALU.is_ge, fill=0.0, base=0,
                pattern=[[1, P]], channel_multiplier=-1).then_inc(consts, 1)
            sel(out=g.later[:], in_=g.later[:], compare_op=ALU.is_gt, fill=0.0, base=0,
                pattern=[[-1, P]], channel_multiplier=1).then_inc(consts, 1)
            sel(out=g.sel8[:], in_=g.sel8[:], compare_op=ALU.is_equal, fill=0.0, base=0,
                pattern=[[-1, NS], [0, P]], channel_multiplier=1).then_inc(consts, 1)
            sel(out=g.eye8[:], in_=g.eye8[:], compare_op=ALU.is_equal, fill=0.0, base=0,
                pattern=[[-1, NS], [1, NS]], channel_multiplier=0).then_inc(consts, 1)
            pool.wait_ge(consts, 5)
            nc.gpsimd.tensor_copy(g.blk[:], g.tri[:]).then_inc(consts, 1)
            pool.wait_ge(consts, 6)
            nc.gpsimd.memset(g.blk[0:HALF, HALF:P], 0.0).then_inc(consts, 1)
            pool.wait_ge(consts, 7)

        @block.scalar
        def _(act):
            act.wait_ge(c_in, 16)
            nc.scalar.activation(sc_sb[:], c_sb[:], ACT.Silu).then_inc(silu_done, 1)
            act.wait_ge(cT_ps, 1)
            nc.scalar.activation(cT[:].rearrange("p k r -> p (k r)"), g.bank(0, cols=KD * (NS + 1)),
                                 ACT.Copy).then_inc(cT_done, 1)
            act.wait_ge(ms_set, 1)
            for t in range(NT + 1):
                rs = P if t < NT else NS
                if t < NT:
                    act.wait_ge(x_in[t], 16)
                else:
                    act.wait_ge(xs_in, 16)
                nc.scalar.activation(sq[0:rs, :], x[0:rs, t, :], ACT.Square,
                                     accum_out=ms[0:rs, t:t + 1]).then_inc(squared, 1)
                act.wait_ge(squared, t + 1)
            act.wait_ge(consts0, 8)
            nc.scalar.activation(lr[:], ms[:], ACT.Ln, scale=1.0 / D, bias=g.eps[:]).then_inc(logged, 1)
            act.wait_ge(logged, 1)
            nc.scalar.activation(r[:], lr[:], ACT.Exp, scale=-0.5).then_inc(r_ready, 1)
            act.wait_ge(r_ready, 1)

        @block.tensor
        def _(pe):
            pe.wait_ge(silu_done, 1)
            pe.wait_ge(consts, 1)
            for k in range(KD):
                last = nc.tensor.transpose(g.bank(0, cols=NS + 1, at=k * (NS + 1)),
                                           sc_sb[:, k * P:(k + 1) * P], g.ident[0:NS + 1, 0:NS + 1])
            last.then_inc(cT_ps, 1)
            pe.wait_ge(cT_done, 1)
            with pe.Fori(0, NB // 2) as i:
                for b in range(2):
                    pe.wait_ge(w_in[b], i * 16 + 16)
                    for k in range(KD):
                        last = nc.tensor.matmul(g.bank(2 + b, rows=NS + 1), cT[:, k, :], w[:, b, k, :],
                                                start=(k == 0), stop=(k == KD - 1))
                    last.then_inc(prod, 1)
                pe.wait_ge(summed, i * 2 + 2)

        @block.vector
        def _(dve):
            nc.vector.memset(ms[:], 0.0).then_inc(ms_set, 1)
            dve.wait_ge(bm_in, 16)
            with dve.Fori(0, NB // 2) as i:
                for b in range(2):
                    dve.wait_ge(prod, i * 2 + b + 1)
                    cols = bass.ds((i * 2 + b) * 512, 512)
                    nc.vector.tensor_tensor(mod[:, cols], g.bank(2 + b, rows=NS + 1), bm[:, cols],
                                            ALU.add).then_inc(summed, 1)


def norm_in(g, x, r, hT):
    nc, io = g.nc, g.io
    with ExitStack() as st:
        sb = lambda n, s: st.enter_context(nc.sbuf_tensor(n, s, F32))
        sem = lambda n: g.sem(n)
        h = [sb(f"n_h{b}", [P, D]) for b in range(2)]
        scale = [sb("n_scale_s", [P, D]), sb("n_scale_p", [P, D])]
        shift = [sb("n_shift_s", [P, D]), sb("n_shift_p", [P, D])]
        norm = sb("n_norm", [P, D])
        mods_in, scales = sem("n_mods_in"), sem("n_scales")
        normed, hchain = sem("n_normed"), sem("n_hchain")
        flipped, high, low = sem("n_flipped"), sem("n_high"), sem("n_low")
        block = st.enter_context(nc.Block())

        @block.sync
        def _(sp):
            sp.dma_start(norm[:], io["norm_mix"].partition_broadcast(P)).then_inc(mods_in, 16)
            sp.dma_start(shift[1][:], g.mod_d[NS, 0:D].partition_broadcast(P)).then_inc(mods_in, 16)
            sp.dma_start(scale[1][:], g.mod_d[NS, D:2 * D].partition_broadcast(P)).then_inc(mods_in, 16)
            sp.dma_start(shift[0][0:NS, :], g.mod_d[0:NS, 0:D]).then_inc(mods_in, 16)
            sp.dma_start(scale[0][0:NS, :], g.mod_d[0:NS, D:2 * D]).then_inc(mods_in, 16)

        def each(eng, tile, between=None):
            for b in range(2):
                tile(b, b, P, False)
            if between:
                between()
            with eng.Fori(1, NT // 2) as i:
                for b in range(2):
                    tile(i * 2 + b, b, P, True)
            tile(NT, 0, NS, True)

        @block.scalar
        def _(act):
            def tile(n, b, rs, later):
                act.wait_ge(flipped, n + 1)
                src = g.ps[:, 2 * b * 512:2 * b * 512 + KD * P].rearrange("p (k r) -> p k r", r=P)[:, :, 0:rs]
                cols = slice(SEQ, ROWS) if rs == NS else bass.ds(n * P, P)
                nc.scalar.activation(hT[0][:, :, cols], src, ACT.Copy).then_inc(high, 1)

            each(act, tile)
            act.wait_ge(high, NT + 1)

        @block.vector
        def _(dve):
            dve.wait_ge(mods_in, 80)
            for kind, rs in ((1, P), (0, NS)):
                s = scale[kind][0:rs, :]
                nc.vector.scalar_tensor_tensor(out=s, in0=s, scalar=1.0, in1=norm[0:rs, :],
                                               op0=ALU.add, op1=ALU.mult).then_inc(scales, 1)
            dve.wait_ge(scales, 2)

            def tile(n, b, rs, later):
                kind = 0 if rs == NS else 1
                if later:
                    dve.wait_ge(flipped, n - 1)
                row = x[0:rs, bass.ds(n, 1), :].squeeze(1)
                nc.vector.scalar_tensor_tensor(out=h[b][0:rs, :], in0=row, scalar=r[0:rs, bass.ds(n, 1)],
                                               in1=scale[kind][0:rs, :], op0=ALU.mult,
                                               op1=ALU.mult).then_inc(hchain, 1)
                dve.wait_ge(hchain, n + 1)
                nc.vector.tensor_tensor(h[b][0:rs, :], h[b][0:rs, :], shift[kind][0:rs, :], ALU.add).then_inc(normed, 1)
                if later:
                    rest(n - 1, 1 - b, P)

            def rest(n, b, rs):
                cols = slice(SEQ, ROWS) if rs == NS else bass.ds(n * P, P)
                src = g.ps[:, 2 * b * 512:2 * b * 512 + KD * P].rearrange("p (k r) -> p k r", r=P)[:, :, 0:rs]
                dve.wait_ge(high, n + 1)
                split_low(nc, hT[1][:, :, cols], hT[0][:, :, cols], src).then_inc(low, 1)

            each(dve, tile, lambda: rest(0, 0, P))
            rest(NT, 0, NS)
            dve.wait_ge(low, NT + 1)

        @block.tensor
        def _(pe):
            def tile(n, b, rs, later):
                pe.wait_ge(normed, n + 1)
                if later:
                    pe.wait_ge(low, n - 1)
                for k in range(KD):
                    at = 2 * b * 512 + k * P
                    last = nc.tensor.transpose(g.ps[:, at:at + rs], h[b][0:rs, k * P:(k + 1) * P],
                                               g.ident[0:rs, 0:rs])
                last.then_inc(flipped, 1)

            each(pe, tile)


def projections(g, hT):
    nc, io = g.nc, g.io
    with ExitStack() as st:
        sb = lambda n, s: st.enter_context(nc.sbuf_tensor(n, s, F32))
        sem = lambda n: g.sem(n)
        NPAR = 4 + 1 + 3 * NS
        wth = [st.enter_context(nc.sbuf_tensor(f"p_wth{b}", [P, KD, 512], F32R)) for b in range(2)]
        wtl = [st.enter_context(nc.sbuf_tensor(f"p_wtl{b}", [P, KD, 512], F32R)) for b in range(2)]
        wt = sb("p_wt", [P, KD, 512])
        wt_in, wt_high, wt_split = sem("p_wt_in"), sem("p_wt_high"), sem("p_wt_split")
        ws, wsh, wsl = (st.enter_context(nc.sbuf_tensor(n, [P, KD, 48], dt))
                        for n, dt in (("p_ws", F32), ("p_wsh", F32R), ("p_wsl", F32R)))
        ws_in, ws_high, ws_split = sem("p_ws_in"), sem("p_ws_high"), sem("p_ws_split")
        dbias, al = sb("p_dbias", [P, HS]), sb("p_al", [P, HS])
        bg = sb("p_bg", [P, GH])
        small_in = sem("p_small_in")

        def split_rows(dve, i, b):
            dve.wait_ge(wt_in, (i * 2 + b) * 16 + 16)
            split_high(nc, wth[b][:], wt[:]).then_inc(wt_high, 1)
            dve.wait_ge(wt_high, i * 2 + b + 1)
            split_low(nc, wtl[b][:], wth[b][:], wt[:]).then_inc(wt_split, 1)

        chan_mem = ExitStack()
        sb = lambda n, s, dt=F32: chan_mem.enter_context(nc.sbuf_tensor(n, s, dt))
        wh = [sb(f"p_wh{b}", [P, KD, P], F32R) for b in range(2)]
        wl = [sb(f"p_wl{b}", [P, KD, P], F32R) for b in range(2)]
        w = [sb(f"p_w{b}", [P, KD, P]) for b in range(2)]
        w_high, w_split = sem("p_w_high"), sem("p_w_split")
        par = [sb(f"p_par{b}", [P, NPAR]) for b in range(2)]
        raw = [sb(f"p_raw{b}", [P, 3 + ROWS]) for b in range(2)]
        acc = [sb(f"p_acc{b}", [P, ROWS]) for b in range(2)]
        res = [sb(f"p_res{b}", [P, ROWS]) for b in range(2)]
        w_in, par_in = [sem("p_w_in0"), sem("p_w_in1")], [sem("p_par_in0"), sem("p_par_in1")]
        cleared, chan, evac = sem("p_cleared"), sem("p_chan"), sem("p_evac")
        convd, cchain, silud, cstored = sem("p_convd"), sem("p_cchain"), sem("p_silud"), sem("p_cstored")
        bstored = [sem("p_bstored0"), sem("p_bstored1")]
        NC = NXBC + NQK
        STEPS = 7

        with nc.Block() as block:
            @block.sync
            def _(sp):
                for b in range(2):
                    sp.dma_start(w[b][:], io["w_chan"][b]).then_inc(w_in[b], 16)
                with sp.Fori(0, NC // 2 - 1) as i:
                    for b in range(2):
                        sp.wait_ge(w_split, i * 2 + b + 1)
                        sp.dma_start(w[b][:], io["w_chan"][bass.ds(i * 2 + b + 2, 1)].squeeze(0)).then_inc(w_in[b], 16)
                sp.dma_start(wt[:], io["w_rows"][0]).then_inc(wt_in, 16)
                sp.dma_start(ws[:], io["w_small"]).then_inc(ws_in, 16)
                sp.dma_start(dbias[:], io["dt_bias"].partition_broadcast(P)).then_inc(small_in, 16)
                sp.dma_start(al[:], io["a_log"].partition_broadcast(P)).then_inc(small_in, 16)
                sp.dma_start(bg[:], io["b_gate"]).then_inc(small_in, 16)
                sp.wait_ge(wt_split, 1)
                sp.dma_start(wt[:], io["w_rows"][1]).then_inc(wt_in, 16)

            @block.gpsimd
            def _(pool):
                for b in range(2):
                    pool.dma_start(par[b][:], io["conv_par"][b]).then_inc(par_in[b], 16)

                def store(i, more):
                    for b in range(2):
                        c = i * 2 + b
                        one = lambda t: t[bass.ds(c, 1)].squeeze(0)
                        wait_apart(pool, silud, c + 1)
                        pool.dma_start(one(g.xbc_d), res[b][:]).then_inc(bstored[b], 16)
                        pool.dma_start(one(io["conv_p"]), raw[b][:, SEQ:SEQ + 3]).then_inc(bstored[b], 16)
                        pool.dma_start(one(io["conv_s"])[:, 0:2 * NS], par[b][:, 5 + NS:5 + 3 * NS]).then_inc(bstored[b], 16)
                        pool.dma_start(one(io["conv_s"])[:, 2 * NS:3 * NS], raw[b][:, SEQ + 3:ROWS + 3]).then_inc(bstored[b], 16)
                        if more:
                            wait_apart(pool, bstored[b], i * 64 + 64)
                            pool.dma_start(par[b][:], io["conv_par"][bass.ds(c + 2, 1)].squeeze(0)).then_inc(par_in[b], 16)

                with pool.Fori(0, NXBC // 2 - 1) as i:
                    store(i, True)
                store(NXBC // 2 - 1, False)
                with pool.Fori(0, NQK // 2) as i:
                    for b in range(2):
                        wait_apart(pool, evac, i * 2 + b + NXBC + 1)
                        pool.dma_start(g.qk_d[bass.ds(i * 2 + b, 1)].squeeze(0), raw[b][:, 3:3 + ROWS]).then_inc(bstored[b], 16)
                        wait_apart(pool, bstored[b], i * 16 + 16 + 64 * (NXBC // 2))

            @block.tensor
            def _(pe):
                def chunk(b, c):
                    pe.wait_ge(w_split, c + 1)
                    for j in range(3):
                        cols = slice(j * THIRD, (j + 1) * THIRD)
                        for k in range(KD):
                            last = matmul_split(nc, g.bank(3 * b + j, cols=THIRD), (wh[b][:, k, :], wl[b][:, k, :]),
                                                (hT[0][:, k, cols], hT[1][:, k, cols]), k == 0, k == KD - 1)
                    last.then_inc(chan, 1)

                chunk(0, 0)
                chunk(1, 1)
                with pe.Fori(1, NC // 2) as i:
                    for b in range(2):
                        pe.wait_ge(evac, i * 2 + b - 1)
                        chunk(b, i * 2 + b)

            @block.scalar
            def _(act):
                def evacuate(b, c):
                    act.wait_ge(chan, c + 1)
                    src = g.ps[:, 3 * b * 512:(3 * b + 3) * 512].rearrange("p (j c) -> p j c", c=512)[:, :, 0:THIRD]
                    nc.scalar.activation(raw[b][:, 3:3 + ROWS].rearrange("p (j c) -> p j c", c=THIRD), src,
                                         ACT.Copy).then_inc(evac, 1)

                def silu(b, c):
                    act.wait_ge(convd, c + 1)
                    nc.scalar.activation(res[b][:], acc[b][:], ACT.Silu).then_inc(silud, 1)

                act.wait_ge(cleared, 2)
                evacuate(0, 0)
                evacuate(1, 1)
                silu(0, 0)
                silu(1, 1)
                with act.Fori(1, NXBC // 2) as i:
                    for b in range(2):
                        act.wait_ge(bstored[b], i * 64)
                        evacuate(b, i * 2 + b)
                    for b in range(2):
                        silu(b, i * 2 + b)
                with act.Fori(0, NQK // 2) as i:
                    for b in range(2):
                        act.wait_ge(bstored[b], i * 16 + 64 * (NXBC // 2))
                        evacuate(b, i * 2 + b + NXBC)
                act.wait_ge(evac, NC)

            @block.vector
            def _(dve):
                def split(i, b, first=False):
                    dve.wait_ge(w_in[b], i * 16 + 16)
                    if not first:
                        dve.wait_ge(chan, i * 2 + b - 1)
                    split_high(nc, wh[b][:], w[b][:]).then_inc(w_high, 1)
                    dve.wait_ge(w_high, i * 2 + b + 1)
                    split_low(nc, wl[b][:], wh[b][:], w[b][:]).then_inc(w_split, 1)

                for b in range(2):
                    split(0, b, True)
                for b in range(2):
                    nc.vector.memset(raw[b][:, 0:3], 0.0).then_inc(cleared, 1)
                with dve.Fori(0, NXBC // 2) as i:
                    for b in range(2):
                        split(i + 1, b)
                        c = i * 2 + b
                        ch = Chain(dve, cchain, c * STEPS)
                        dve.wait_ge(par_in[b], i * 16 + 16)
                        dve.wait_ge(evac, c + 1)
                        tap = lambda j: par[b][:, j:j + 1]
                        late, new = acc[b][:, SEQ:ROWS], raw[b][:, SEQ + 3:ROWS + 3]
                        body = acc[b][:, 0:SEQ]
                        ch.mark(nc.vector.tensor_scalar(body, raw[b][:, 0:SEQ], tap(0), tap(4), ALU.mult, ALU.add))
                        ch.step(nc.vector.tensor_scalar(late, new, tap(3), tap(4), ALU.mult, ALU.add))
                        for j in range(1, 4):
                            old = par[b][:, 5 + (j - 1) * NS:5 + j * NS]
                            mul_add = nc.vector.scalar_tensor_tensor
                            ins = mul_add(out=late, in0=old, scalar=tap(j - 1), in1=late, op0=ALU.mult, op1=ALU.add)
                            ch.mark(ins)
                            ins = mul_add(out=body, in0=raw[b][:, j:j + SEQ], scalar=tap(j), in1=body,
                                          op0=ALU.mult, op1=ALU.add)
                            if j < 3:
                                ch.step(ins)
                            else:
                                ins.then_inc(convd, 1)
                        assert ch.n == STEPS
                with dve.Fori(NXBC // 2, NC // 2 - 1) as i:
                    for b in range(2):
                        split(i + 1, b)
                for b in range(2):
                    split_rows(dve, 0, b)
                dve.wait_ge(ws_in, 16)
                split_high(nc, wsh[:], ws[:]).then_inc(ws_high, 1)
                dve.wait_ge(ws_high, 1)
                split_low(nc, wsl[:], wsh[:], ws[:]).then_inc(ws_split, 1)

        chan_mem.close()
        row_mem = ExitStack()
        sb = lambda n, s, dt=F32: row_mem.enter_context(nc.sbuf_tensor(n, s, dt))
        evs = [sb(f"p_ev{s}", [P, 512]) for s in range(6)]
        tprod, tevac = sem("p_tprod"), sem("p_tevac")
        tstored = [sem(f"p_tstored{s}") for s in range(6)]
        NRT = NT + 1

        with nc.Block() as block:
            @block.sync
            def _(sp):
                with sp.Fori(0, 2) as i:
                    for b in range(2):
                        sp.wait_ge(wt_split, i * 2 + b + 2)
                        sp.dma_start(wt[:], io["w_rows"][bass.ds(i * 2 + b + 2, 1)].squeeze(0)).then_inc(wt_in, 16)

            @block.gpsimd
            def _(pool):
                with pool.Fori(0, 3) as i:
                    for b in range(2):
                        for t in range(NRT):
                            n = b * NRT + t
                            rs = P if t < NT else NS
                            wait_apart(pool, tevac, i * (2 * NRT) + n + 1)
                            dst = g.proj_d[t * P:t * P + rs, bass.ds(i, 1), b * 512:(b + 1) * 512].squeeze(1)
                            pool.dma_start(dst, evs[n % 6][0:rs, :]).then_inc(tstored[n % 6], 16)
                for s in range(6):
                    pool.wait_ge(tstored[s], 16 * 3 * (2 * NRT // 6))

            @block.tensor
            def _(pe):
                def block_rows(i, first):
                    for b in range(2):
                        pe.wait_ge(wt_split, i * 2 + b + 1)
                        for t in range(NRT):
                            n = b * NRT + t
                            rs = P if t < NT else NS
                            if n >= 6 or not first:
                                pe.wait_ge(tevac, i * (2 * NRT) + n - 5)
                            for k in range(KD):
                                rows = slice(t * P, t * P + rs)
                                last = matmul_split(nc, g.bank(n % 6, rows=rs), (hT[0][:, k, rows], hT[1][:, k, rows]),
                                                    (wth[b][:, k, :], wtl[b][:, k, :]), k == 0, k == KD - 1)
                            last.then_inc(tprod, 1)

                block_rows(0, True)
                with pe.Fori(1, 3) as i:
                    block_rows(i, False)

            @block.scalar
            def _(act):
                def block_rows(i, first, func):
                    for b in range(2):
                        for t in range(NRT):
                            n = b * NRT + t
                            rs = P if t < NT else NS
                            if n >= 6 or not first:
                                act.wait_ge(tstored[n % 6], i * (16 * (2 * NRT // 6)) + 16 * (n // 6))
                            act.wait_ge(tprod, i * (2 * NRT) + n + 1)
                            nc.scalar.activation(evs[n % 6][0:rs, :], g.bank(n % 6, rows=rs), func).then_inc(tevac, 1)

                block_rows(0, True, ACT.Silu)
                block_rows(1, False, ACT.Silu)
                block_rows(2, False, ACT.Copy)

            @block.vector
            def _(dve):
                with dve.Fori(1, 3) as i:
                    for b in range(2):
                        dve.wait_ge(tprod, (i * 2 + b - 1) * NRT)
                        split_rows(dve, i, b)

        row_mem.close()
        sb = lambda n, s, dt=F32: st.enter_context(nc.sbuf_tensor(n, s, dt))
        an, wgu, wgu_in = sb("p_an", [P, HS]), sb("p_wgu", [16, GH * P]), sem("p_wgu_in")
        dx, dm = sb("p_dx", [P, NT + 1, HS]), sb("p_dm", [P, NT + 1, HS])
        gT = sb("p_gT", [48, ROWS])
        xg, ab = [sb(f"p_xg{c}", [P, ROWS]) for c in range(GH)], [sb(f"p_ab{c}", [P, ROWS]) for c in range(GH)]
        keep = sb("p_keep", [P, ROWS])
        a_neg = sem("p_a_neg")
        dtps, dch, dabs, dlog, dready = sem("p_dtps"), sem("p_dch"), sem("p_dabs"), sem("p_dlog"), sem("p_dready")
        decps, decs = sem("p_decps"), sem("p_decs")
        gps, gts, gup, gch, gabs, glog = (sem("p_gps"), sem("p_gts"), sem("p_gup"), sem("p_gch"),
                                          sem("p_gabs"), sem("p_glog"))
        ach, cumd, cums, keepd = sem("p_ach"), sem("p_cumd"), sem("p_cums"), sem("p_keepd")

        with nc.Block() as block:
            @block.sync
            def _(sp):
                sp.dma_start(wgu[:], io["w_gate_up"]).then_inc(wgu_in, 16)
                for c in range(GH):
                    sp.wait_ge(cumd, c + 1)
                    sp.dma_start(g.cum_d[c], ab[c][:]).then_inc(cums, 16)
                sp.wait_ge(cums, 16 * GH)

            @block.tensor
            def _(pe):
                pe.wait_ge(small_in, 48)
                pe.wait_ge(ws_split, 1)
                for j in range(3):
                    cols = slice(j * THIRD, (j + 1) * THIRD)
                    for k in range(KD):
                        last = matmul_split(nc, g.bank(1 + j, rows=48, cols=THIRD), (wsh[:, k, :], wsl[:, k, :]),
                                            (hT[0][:, k, cols], hT[1][:, k, cols]), k == 0, k == KD - 1)
                last.then_inc(gps, 1)
                pe.wait_ge(gts, 1)
                for t in range(NRT):
                    rs = P if t < NT else NS
                    last = nc.tensor.transpose(g.bank(0, rows=rs, cols=HS, at=t * HS), gT[32:48, t * P:t * P + rs],
                                               g.ident[32:48, 32:48])
                last.then_inc(dtps, 1)
                pe.wait_ge(wgu_in, 16)
                for c in range(GH):
                    if c:
                        pe.wait_ge(gabs, c)
                    for j in range(3):
                        last = nc.tensor.matmul(g.bank(5 + j, cols=THIRD), wgu[:, c * P:(c + 1) * P],
                                                gT[0:16, j * THIRD:(j + 1) * THIRD], start=True, stop=True)
                    last.then_inc(gup, 1)
                pe.wait_ge(dready, 2)
                for n, lhs in enumerate((g.tri, g.later, g.ones)):
                    last = nc.tensor.matmul(g.bank(4, cols=P, at=n * P), lhs[:],
                                            g.dta[:, 0:NT, :].rearrange("p t h -> p (t h)"), start=True, stop=True)
                last.then_inc(decps, 1)

            @block.vector
            def _(dve):
                V = nc.vector
                dve.wait_ge(small_in, 48)
                V.memset(keep[:], 1.0).then_inc(keepd, 1)
                dve.wait_ge(keepd, 1)
                V.memset(keep[:, 0:SEQ].rearrange("p (t s) -> p t s", s=P)[:, :, 0:1], 0.0).then_inc(keepd, 1)
                V.memset(keep[:, SEQ:ROWS], 0.0).then_inc(keepd, 1)
                ch = Chain(dve, dch)
                dve.wait_ge(dtps, 1)
                dve.wait_ge(small_in, 48)
                parts = ((P, slice(0, NT), NT), (NS, slice(NT, NT + 1), 1))
                for rs, ts, n in parts:
                    src = g.ps[0:rs, ts.start * HS:ts.stop * HS].rearrange("p (t h) -> p t h", h=HS)
                    V.tensor_tensor(dx[0:rs, ts, :], src, bcast(dbias[0:rs, :].unsqueeze(1), [rs, n, HS]),
                                    ALU.add).then_inc(dabs, 1)
                dve.wait_ge(dabs, 2)
                for rs, ts, n in parts:
                    ch.step(V.tensor_scalar(g.dt[0:rs, ts, :], dx[0:rs, ts, :], 0.0, None, ALU.max))
                dve.wait_ge(dlog, 2)
                for rs, ts, n in parts:
                    ch.step(V.tensor_tensor(g.dt[0:rs, ts, :], g.dt[0:rs, ts, :], dm[0:rs, ts, :], ALU.add))
                dve.wait_ge(a_neg, 1)
                for rs, ts, n in parts:
                    V.scalar_tensor_tensor(out=g.dta[0:rs, ts, :], in0=g.dt[0:rs, ts, :], scalar=-1.0,
                                           in1=bcast(an[0:rs, :].unsqueeze(1), [rs, n, HS]),
                                           op0=ALU.mult, op1=ALU.mult).then_inc(dready, 1)
                for c in range(GH):
                    dve.wait_ge(gup, c + 1)
                    src = g.ps[:, 5 * 512:8 * 512].rearrange("p (j c) -> p j c", c=512)[:, :, 0:THIRD]
                    V.tensor_scalar(xg[c][:].rearrange("p (j c) -> p j c", c=THIRD), src, bg[:, c:c + 1], None,
                                    ALU.add).then_inc(gabs, 1)
                dve.wait_ge(gabs, GH)
                dve.wait_ge(keepd, 3)
                for c in range(GH):
                    dve.wait_ge(glog, c + 1)
                    V.scalar_tensor_tensor(out=ab[c][:], in0=xg[c][:], scalar=0.0, in1=ab[c][:], op0=ALU.min,
                                           op1=ALU.subtract).then_inc(gch, 1)
                    dve.wait_ge(gch, 2 * c + 1)
                    V.tensor_tensor_scan(xg[c][:], keep[:], ab[c][:], 0.0, ALU.mult, ALU.add).then_inc(gch, 1)
                    dve.wait_ge(gch, 2 * c + 2)
                    V.tensor_scalar(ab[c][:], xg[c][:], 1.0 / 16.0, None, ALU.mult).then_inc(cumd, 1)
                dve.wait_ge(cumd, GH)

            @block.scalar
            def _(act):
                A = nc.scalar.activation
                act.wait_ge(small_in, 48)
                A(an[:], al[:], ACT.Exp).then_inc(a_neg, 1)
                ch = Chain(act, ach)
                act.wait_ge(gps, 1)
                src = g.ps[0:48, 512:4 * 512].rearrange("p (j c) -> p j c", c=512)[:, :, 0:THIRD]
                A(gT[:].rearrange("p (j c) -> p j c", c=THIRD), src, ACT.Copy).then_inc(gts, 1)
                parts = ((P, slice(0, NT)), (NS, slice(NT, NT + 1)))
                for n, (rs, ts) in enumerate(parts):
                    act.wait_ge(dabs, n + 1)
                    ch.step(A(dm[0:rs, ts, :], dx[0:rs, ts, :], ACT.Abs))
                    ch.step(A(dm[0:rs, ts, :], dm[0:rs, ts, :], ACT.Exp, scale=-1.0))
                for n, (rs, ts) in enumerate(parts):
                    A(dm[0:rs, ts, :], dm[0:rs, ts, :], ACT.Ln, bias=1.0).then_inc(dlog, 1)
                for c in range(GH):
                    act.wait_ge(gabs, c + 1)
                    ch.step(A(ab[c][:], xg[c][:], ACT.Abs))
                    ch.step(A(ab[c][:], ab[c][:], ACT.Exp, scale=-1.0))
                act.wait_ge(decps, 1)
                for n, dst in enumerate((g.ecum, g.etoend, g.etot)):
                    A(dst[:].rearrange("p t h -> p (t h)"), g.bank(4, cols=P, at=n * P), ACT.Exp).then_inc(decs, 1)
                act.wait_ge(dready, 2)
                A(g.edta[:], g.dta[0:NS, NT, :], ACT.Exp).then_inc(decs, 1)
                for c in range(GH):
                    A(ab[c][:], ab[c][:], ACT.Ln, bias=1.0).then_inc(glog, 1)
                act.wait_ge(decs, 4)


class Output:

    def __init__(self, g, st, pre, rows):
        nc = g.nc
        self.g, self.rows = g, rows
        sb = lambda n, s: st.enter_context(nc.sbuf_tensor(pre + n, s, F32))
        sem = lambda n: g.sem(pre + n)
        self.w = sb("w_out", [P, 2 * KD, D])
        self.cat, self.catT = sb("cat", [P, 2 * D]), sb("catT", [P, 2 * KD, P])
        self.x, self.x1, self.h2 = sb("x", [P, D]), sb("x1", [P, D]), sb("h2", [P, D])
        self.junk = sb("junk", [P, D])
        self.ms, self.r = sb("ms2", [P, 2]), sb("r2", [P, 1])
        self.gate1, self.scale2, self.shift2 = sb("gate1", [P, D]), sb("scale2", [P, D]), sb("shift2", [P, D])
        self.norm = self.junk
        self.w_in, self.mods_in, self.scaled = sem("w_out_in"), sem("mods_in"), sem("scaled")
        self.x_in, self.cat_ready = sem("x_in"), sem("cat_ready")
        self.catT_ps, self.catT_kept, self.prod = sem("catT_ps"), sem("catT_kept"), sem("prod")
        self.gated, self.x1_ready, self.r2_ready = sem("gated"), sem("x1_ready"), sem("r2_ready")
        self.h2_scaled, self.h2_ready = sem("h2_scaled"), sem("h2_ready")
        self.ach, self.x1_stored, self.h2_stored = sem("oach"), sem("x1_stored"), sem("h2_stored")

    def load_constants(self, sp):
        g, io, rs = self.g, self.g.io, self.rows
        take = lambda a: (g.mod_d[0:NS, a * D:(a + 1) * D] if rs == NS
                          else g.mod_d[NS, a * D:(a + 1) * D].partition_broadcast(P))
        sp.dma_start(self.norm[0:rs, :], io["norm_ffn"].partition_broadcast(rs)).then_inc(self.mods_in, 16)
        sp.dma_start(self.gate1[0:rs, :], take(2)).then_inc(self.mods_in, 16)
        sp.dma_start(self.shift2[0:rs, :], take(3)).then_inc(self.mods_in, 16)
        sp.dma_start(self.scale2[0:rs, :], take(4)).then_inc(self.mods_in, 16)

    def load_weights(self, sp):
        sp.dma_start(self.w[:], self.g.io["w_out"]).then_inc(self.w_in, 16)

    def prepare(self, dve):
        rs = self.rows
        dve.wait_ge(self.mods_in, 64)
        s = self.scale2[0:rs, :]
        self.g.nc.vector.scalar_tensor_tensor(out=s, in0=s, scalar=1.0, in1=self.norm[0:rs, :],
                                              op0=ALU.add, op1=ALU.mult).then_inc(self.scaled, 1)
        dve.wait_ge(self.scaled, 1)

    def turn(self, pe, n):
        g, rs = self.g, self.rows
        pe.wait_ge(self.cat_ready, n + 1)
        for half in range(2):
            for k in range(KD):
                c = half * KD + k
                last = g.nc.tensor.transpose(g.ps[:, (4 + 2 * half) * 512 + k * P:][:, 0:rs],
                                             self.cat[0:rs, c * P:(c + 1) * P], g.ident[0:rs, 0:rs])
            last.then_inc(self.catT_ps, 1)

    def product(self, pe, n, ks, first):
        g, rs = self.g, self.rows
        if ks.start == 0:
            pe.wait_ge(self.w_in, 16)
            pe.wait_ge(self.catT_kept, n * 2 + 2)
            if not first:
                pe.wait_ge(self.x1_ready, n)
        for k in ks:
            for cols in range(2):
                last = g.nc.tensor.matmul(g.bank(cols, rows=rs), self.catT[:, k, 0:rs],
                                          self.w[:, k, cols * 512:(cols + 1) * 512],
                                          start=(k == 0), stop=(k == 2 * KD - 1))
        if ks.stop == 2 * KD:
            last.then_inc(self.prod, 1)

    def keep_turned(self, act, n):
        g, A, rs = self.g, self.g.nc.scalar.activation, self.rows
        for half in range(2):
            act.wait_ge(self.catT_ps, n * 2 + half + 1)
            src = g.ps[:, (4 + 2 * half) * 512:][:, 0:KD * P].rearrange("p (k r) -> p k r", r=P)[:, :, 0:rs]
            A(self.catT[:, half * KD:(half + 1) * KD, 0:rs], src, ACT.Copy).then_inc(self.catT_kept, 1)

    def norm2(self, act, n):
        g, A, rs = self.g, self.g.nc.scalar.activation, self.rows
        act.wait_ge(self.x1_ready, n + 1)
        act.wait_ge(self.scaled, 1)
        ch = Chain(act, self.ach, n * 2)
        ch.step(A(self.junk[0:rs, :], self.x1[0:rs, :], ACT.Square, accum_out=self.ms[0:rs, 0:1]))
        ch.step(A(self.ms[0:rs, 1:2], self.ms[0:rs, 0:1], ACT.Ln, scale=1.0 / D, bias=g.eps[0:rs, :]))
        A(self.r[0:rs, :], self.ms[0:rs, 1:2], ACT.Exp, scale=-0.5).then_inc(self.r2_ready, 1)
        act.wait_ge(self.r2_ready, n + 1)

    def residual(self, dve, n, first):
        g, V, rs = self.g, self.g.nc.vector, self.rows
        dve.wait_ge(self.prod, n + 1)
        dve.wait_ge(self.x_in, n * 16 + 16)
        if not first:
            dve.wait_ge(self.x1_stored, n * 16)
        V.tensor_tensor(self.x1[0:rs, :], g.ps[0:rs, 0:D], self.gate1[0:rs, :], ALU.mult).then_inc(self.gated, 1)
        dve.wait_ge(self.gated, n + 1)
        V.tensor_tensor(self.x1[0:rs, :], self.x1[0:rs, :], self.x[0:rs, :], ALU.add).then_inc(self.x1_ready, 1)

    def modulate(self, dve, n, first):
        V, rs = self.g.nc.vector, self.rows
        dve.wait_ge(self.r2_ready, n + 1)
        if not first:
            dve.wait_ge(self.h2_stored, n * 16)
        V.scalar_tensor_tensor(out=self.h2[0:rs, :], in0=self.x1[0:rs, :], scalar=self.r[0:rs, :],
                               in1=self.scale2[0:rs, :], op0=ALU.mult, op1=ALU.mult).then_inc(self.h2_scaled, 1)
        dve.wait_ge(self.h2_scaled, n + 1)
        V.tensor_tensor(self.h2[0:rs, :], self.h2[0:rs, :], self.shift2[0:rs, :], ALU.add).then_inc(self.h2_ready, 1)
        dve.wait_ge(self.h2_ready, n + 1)

    def store(self, eng, n, row):
        g, rs = self.g, self.rows
        rows = bass.ds(row, rs)
        wait_apart(eng, self.x1_ready, n + 1)
        eng.dma_start(g.x1_d[rows, :], self.x1[0:rs, :]).then_inc(self.x1_stored, 16)
        wait_apart(eng, self.h2_ready, n + 1)
        eng.dma_start(g.h2_d[rows, :], self.h2[0:rs, :]).then_inc(self.h2_stored, 16)


def mix_prompt(g):
    nc, io = g.nc, g.io
    R = HS // 2
    QS = float(P) ** -0.5
    with ExitStack() as st:
        sb = lambda n, s: st.enter_context(nc.sbuf_tensor("x_" + n, s, F32))
        sem = lambda n: g.sem("x_" + n)
        out = Output(g, st, "xo_", P)
        xbc, zgv, qk, cum = sb("xbc", [P, NXBC, P]), sb("zgv", [P, 3, D]), sb("qk", [P, NQK, P]), sb("cum", [P, GH, P])
        dec = sb("dec", [P, HS, P])
        xs, xdt, xend = sb("xs", [P, HS, HP]), sb("xdt", [P, HS, HP]), sb("xend", [P, HS, HP])
        b_rows, cb = sb("b_rows", [P, 2, P]), sb("cb", [P, 2, P])
        S, GS = sb("S", [P, HS, HP]), sb("GS", [P, GH, GV])
        yb, yt = sb("yb", [P, HS, HP]), sb("yt", [P, HS, HP])
        d1, ref2, end = sb("d1", [P, GH, P]), sb("ref2", [P, GH, P]), sb("end", [P, GH, P])
        qd, kd, qi, ecg = sb("qd", [P, GH, P]), sb("kd", [P, GH, P]), sb("qi", [P, GH, P]), sb("ecg", [P, GH, P])
        att, keT = sb("att", [P, GH, P]), sb("keT", [P, GH, P])
        dskip, ssdn, glan = sb("dskip", [P, HS]), sb("ssdn", [P, D]), sb("glan", [P, GV])
        msy, ry, mso, ro = sb("msy", [P, 4]), sb("ry", [P, 2]), sb("mso", [P, 8]), sb("ro", [P, GH])
        consts_in, xbc_in, gla_in, zgv_in = sem("consts_in"), sem("xbc_in"), sem("gla_in"), sem("zgv_in")
        seg_in, xs_ps, xs_kept, xdt_ready, xend_ready = (sem("seg_in"), sem("xs_ps"), sem("xs_kept"),
                                                         sem("xdt_ready"), sem("xend_ready"))
        seg_ps, dec_ready, m_ready, y_ps, su_ps = (sem("seg_ps"), sem("dec_ready"), sem("m_ready"), sem("y_ps"),
                                                   sem("su_ps"))
        y_used, y_sum, ry_ready, s_ready, gs_ready = (sem("y_used"), sem("y_sum"), sem("ry_ready"), sem("s_ready"),
                                                      sem("gs_ready"))
        gdiff, gexp, gprod, att_ps, att_ready = (sem("gdiff"), sem("gexp"), sem("gprod"), sem("att_ps"),
                                                 sem("att_ready"))
        ke_ps, ke_kept, o_ps, gs_ps, ro_ready = sem("ke_ps"), sem("ke_kept"), sem("o_ps"), sem("gs_ps"), sem("ro_ready")
        vch, ach, s_out = sem("vch"), sem("ach"), sem("s_out")
        VSTEPS, ASTEPS = 6, 4
        block = st.enter_context(nc.Block())
        head = lambda t, h: t[:, h, :]
        per_head = lambda t, n: bcast(t[:, bass.ds(n, 1), :].squeeze(1).unsqueeze(2), [P, HS, HP])

        @block.sync
        def _(sp):
            def load(n, first):
                rows = bass.ds(n * P, P)
                if not first:
                    sp.wait_ge(y_ps, n)
                sp.dma_start(xbc[:], g.xbc_d[:, :, rows].rearrange("c p t -> p c t")).then_inc(xbc_in, 16)
                if not first:
                    sp.wait_ge(gprod, n)
                sp.dma_start(qk[:], g.qk_d[:, :, rows].rearrange("c p t -> p c t")).then_inc(gla_in, 16)
                sp.dma_start(cum[:], g.cum_d[:, :, rows].rearrange("c p t -> p c t")).then_inc(gla_in, 16)
                if not first:
                    sp.wait_ge(out.cat_ready, n)
                    sp.wait_ge(gs_ps, n)
                sp.dma_start(zgv[:], g.proj_d[rows, :, :]).then_inc(zgv_in, 16)

            def load_x(n, first):
                if not first:
                    sp.wait_ge(out.x1_ready, n)
                sp.dma_start(out.x[:], io["x_prompt"][bass.ds(n * P, P), :]).then_inc(out.x_in, 16)

            load(0, True)
            sp.dma_start(dskip[:], io["d_skip"].partition_broadcast(P)).then_inc(consts_in, 16)
            sp.dma_start(ssdn[:], io["ssd_norm"].partition_broadcast(P)).then_inc(consts_in, 16)
            sp.dma_start(glan[:], io["gla_norm"].partition_broadcast(P)).then_inc(consts_in, 16)
            out.load_constants(sp)
            out.load_weights(sp)
            load_x(0, True)
            load(1, False)
            with sp.Fori(2, NT) as n:
                load(n, False)
                load_x(n - 1, False)
            load_x(NT - 1, False)
            sp.wait_ge(s_ready, NT + 1)
            sp.dma_start(io["ssm_p"], S[:].rearrange("p h c -> p (h c)")).then_inc(s_out, 16)
            sp.wait_ge(gs_ready, NT + 1)
            sp.dma_start(io["gla_p"], GS[:].rearrange("p h c -> p (h c)")).then_inc(s_out, 16)
            sp.wait_ge(s_out, 32)

        @block.gpsimd
        def _(pool):
            with pool.Fori(0, NT) as n:
                out.store(pool, n, n * P)
            pool.wait_ge(out.x1_stored, 16 * NT)
            pool.wait_ge(out.h2_stored, 16 * NT)

        @block.tensor
        def _(pe):
            mm, tr = nc.tensor.matmul, nc.tensor.transpose

            def tile(n, stage):
                before = lambda a, b: out.product(pe, n - 1, range(a, b), stage == 1) if stage else None
                pe.wait_ge(xbc_in, n * 16 + 16)
                if stage:
                    pe.wait_ge(gs_ready, n + 1)
                for c in range(KD):
                    tr(g.ps[:, 2 * 512 + c * P:2 * 512 + (c + 1) * P], xbc[:, c, :], g.ident[:])
                if stage:
                    pe.wait_ge(out.catT_kept, n * 2)
                for c in range(2):
                    tr(g.bank(4, cols=P, at=c * P), xbc[:, KD + c, :], g.ident[:])
                    last = mm(g.bank(4, cols=P, at=(2 + c) * P), xbc[:, KD + c, :], xbc[:, KD + 2 + c, :],
                              start=True, stop=True)
                last.then_inc(xs_ps, 1)
                pe.wait_ge(seg_in, n + 1)
                for half in range(2):
                    if half:
                        pe.wait_ge(xs_kept, n + 1)
                    for q in range(2):
                        h = half * R + q * 4
                        last = mm(g.bank((6, 2)[half] + q), g.later[:], dec[:, h:h + 4, :], start=True, stop=True)
                    last.then_inc(seg_ps, 1)
                before(0, 5)
                pe.wait_ge(xdt_ready, n + 1)
                for c in range(2):
                    pe.wait_ge(m_ready, n * 2 + c + 1)
                    for r in range(R):
                        h = c * R + r
                        mm(g.ps[:, 6 * 512 + h * HP:6 * 512 + (h + 1) * HP], dec[:, h, :], xdt[:, h, :],
                           start=True, stop=True)
                pe.wait_ge(s_ready, n + 1)
                for c in range(2):
                    last = mm(g.bank(2 + c), xbc[:, KD + 2 + c, :], S[:, c * R:(c + 1) * R, :], start=True, stop=True)
                last.then_inc(y_ps, 1)
                pe.wait_ge(xend_ready, n + 1)
                for c in range(2):
                    last = mm(g.bank(4 + c), b_rows[:, c, :], xend[:, c * R:(c + 1) * R, :], start=True, stop=True)
                last.then_inc(su_ps, 1)
                before(5, 9)
                pe.wait_ge(gprod, n + 1)
                pe.wait_ge(y_used, n + 1)
                for h in range(GH):
                    mm(g.bank(2, cols=P, at=h * P), head(kd, h), head(qd, h), start=True, stop=True)
                for h in range(GH):
                    last = mm(g.bank(3, rows=HALF, cols=HALF, at=h * HALF), ref2[:, h, 0:HALF], ref2[:, h, HALF:P],
                              start=True, stop=True)
                last.then_inc(att_ps, 1)
                pe.wait_ge(s_ready, n + 2)
                for h in range(GH):
                    last = tr(g.bank(4, cols=P, at=h * P), head(end, h), g.ident[:])
                last.then_inc(ke_ps, 1)
                before(9, 12)
                pe.wait_ge(att_ready, n + 1)
                pe.wait_ge(zgv_in, n * 16 + 16)
                pe.wait_ge(gs_ready, n + 1)
                for h in range(GH):
                    v, o = zgv[:, 2, h * GV:(h + 1) * GV], g.ps[:, 6 * 512 + h * GV:6 * 512 + (h + 1) * GV]
                    mm(o, head(att, h), v, start=True, stop=False)
                    last = mm(o, head(qi, h), head(GS, h), start=False, stop=True)
                last.then_inc(o_ps, 1)
                pe.wait_ge(ke_kept, n + 1)
                for h in range(GH):
                    last = mm(g.ps[:, 2 * 512 + h * GV:2 * 512 + (h + 1) * GV], head(keT, h),
                              zgv[:, 2, h * GV:(h + 1) * GV], start=True, stop=True)
                last.then_inc(gs_ps, 1)
                before(12, 2 * KD)
                out.turn(pe, n)

            for n in range(3):
                tile(n, n)
            with pe.Fori(3, NT) as n:
                tile(n, 3)
            out.product(pe, NT - 1, range(0, 2 * KD), False)

        @block.scalar
        def _(act):
            A = nc.scalar.activation

            def tile(n, stage):
                ch = Chain(act, ach, n * ASTEPS)
                act.wait_ge(xs_ps, n + 1)
                A(xs[:].rearrange("p h c -> p (h c)"), g.ps[:, 2 * 512:4 * 512], ACT.Copy)
                A(b_rows[:].rearrange("p c n -> p (c n)"), g.bank(4, cols=2 * P), ACT.Copy).then_inc(xs_kept, 1)
                for half in range(2):
                    act.wait_ge(seg_ps, n * 2 + half + 1)
                    A(dec[:, half * R:(half + 1) * R, :].rearrange("p h t -> p (h t)"),
                      g.ps[:, (6, 2)[half] * 512:((6, 2)[half] + 2) * 512], ACT.Exp).then_inc(dec_ready, 1)
                act.wait_ge(gdiff, n * 4 + 4)
                A(qd[:], d1[:], ACT.Exp)
                A(kd[:], d1[:], ACT.Exp, scale=-1.0)
                A(ref2[:], ref2[:], ACT.Exp)
                A(end[:], end[:], ACT.Exp)
                A(ecg[:], cum[:], ACT.Exp).then_inc(gexp, 1)
                if stage >= 2:
                    out.norm2(act, n - 2)
                act.wait_ge(y_sum, n + 1)
                for c in range(2):
                    ins = A(yt[:, c * R:(c + 1) * R, :], yb[:, c * R:(c + 1) * R, :], ACT.Square,
                            accum_out=msy[:, c:c + 1])
                ch.step(ins)
                ch.step(A(msy[:, 2:4], msy[:, 0:2], ACT.Ln, scale=2.0 / D, bias=g.eps[:]))
                A(ry[:], msy[:, 2:4], ACT.Exp, scale=-0.5).then_inc(ry_ready, 1)
                act.wait_ge(ry_ready, n + 1)
                act.wait_ge(ke_ps, n + 1)
                A(keT[:].rearrange("p h d -> p (h d)"), g.bank(4), ACT.Copy).then_inc(ke_kept, 1)
                act.wait_ge(o_ps, n + 1)
                for h in range(GH):
                    ins = A(yt[:, h * 4:(h + 1) * 4, :].rearrange("p h c -> p (h c)"), g.ps[:, 6 * 512 + h * GV:6 * 512 + (h + 1) * GV],
                            ACT.Square, accum_out=mso[:, h:h + 1])
                ch.step(ins)
                ch.step(A(mso[:, 4:8], mso[:, 0:4], ACT.Ln, scale=1.0 / GV, bias=g.eps[:]))
                A(ro[:], mso[:, 4:8], ACT.Exp, scale=-0.5).then_inc(ro_ready, 1)
                act.wait_ge(ro_ready, n + 1)
                assert ch.n == ASTEPS
                out.keep_turned(act, n)

            for n in range(3):
                tile(n, n)
            with act.Fori(3, NT) as n:
                tile(n, 3)
            for n in (NT - 2, NT - 1):
                out.norm2(act, n)

        @block.vector
        def _(dve):
            V, stt = nc.vector, nc.vector.scalar_tensor_tensor
            V.memset(S[:], 0.0).then_inc(s_ready, 1)
            V.memset(GS[:], 0.0).then_inc(gs_ready, 1)
            dve.wait_ge(s_ready, 1)
            dve.wait_ge(gs_ready, 1)

            def tile(n, stage):
                ch = Chain(dve, vch, n * VSTEPS)
                dta = g.dta[:, bass.ds(n, 1), :].squeeze(1)
                V.tensor_tensor(dec[:], bcast(dta.unsqueeze(2), [P, HS, P]), bcast(g.tri[:].unsqueeze(1), [P, HS, P]),
                                ALU.mult).then_inc(seg_in, 1)
                dve.wait_ge(xs_kept, n + 1)
                V.tensor_tensor(xdt[:], xs[:], per_head(g.dt, n), ALU.mult)
                V.tensor_tensor(cb[:], g.bank(4, cols=2 * P, at=2 * P).rearrange("p (c t) -> p c t", c=2),
                                bcast(g.tri[:].unsqueeze(1), [P, 2, P]), ALU.mult).then_inc(xdt_ready, 1)
                dve.wait_ge(xdt_ready, n + 1)
                V.tensor_tensor(xend[:], xdt[:], per_head(g.etoend, n), ALU.mult).then_inc(xend_ready, 1)
                dve.wait_ge(gla_in, n * 32 + 32)
                by_half = lambda t: t[:].rearrange("p h (c t) -> p (h c) t", c=2)
                V.tensor_tensor(by_half(d1), by_half(cum), bcast(by_half(cum)[:, :, HALF // 2:HALF // 2 + 1],
                                                                 [P, 2 * GH, HALF]), ALU.subtract).then_inc(gdiff, 1)
                seam = bcast(cum[:, :, HALF - 1:HALF], [P, GH, HALF])
                V.tensor_tensor(ref2[:, :, 0:HALF], seam, cum[:, :, 0:HALF], ALU.subtract).then_inc(gdiff, 1)
                V.tensor_tensor(ref2[:, :, HALF:P], cum[:, :, HALF:P], seam, ALU.subtract).then_inc(gdiff, 1)
                V.tensor_tensor(end[:], bcast(cum[:, :, P - 1:P], [P, GH, P]), cum[:], ALU.subtract).then_inc(gdiff, 1)
                for c in range(2):
                    dve.wait_ge(dec_ready, n * 2 + c + 1)
                    m = dec[:, c * R:(c + 1) * R, :]
                    V.tensor_tensor(m, m, bcast(cb[:, c:c + 1, :], [P, R, P]), ALU.mult).then_inc(m_ready, 1)
                dve.wait_ge(gexp, n + 1)
                q, k = qk[:, 0:GH, :], qk[:, GH:NQK, :]
                stt(out=qd[:], in0=q, scalar=QS, in1=qd[:], op0=ALU.mult, op1=ALU.mult)
                V.tensor_tensor(kd[:], k, kd[:], ALU.mult)
                stt(out=ref2[:, :, HALF:P], in0=q[:, :, HALF:P], scalar=QS, in1=ref2[:, :, HALF:P],
                    op0=ALU.mult, op1=ALU.mult)
                V.tensor_tensor(ref2[:, :, 0:HALF], k[:, :, 0:HALF], ref2[:, :, 0:HALF], ALU.mult)
                stt(out=qi[:], in0=q, scalar=QS, in1=ecg[:], op0=ALU.mult, op1=ALU.mult)
                V.tensor_tensor(end[:], k, end[:], ALU.mult).then_inc(gprod, 1)
                if stage >= 2:
                    out.modulate(dve, n - 2, stage == 2)
                dve.wait_ge(y_ps, n + 1)
                if stage == 0:
                    dve.wait_ge(consts_in, 48)
                V.tensor_tensor(yt[:], xs[:], bcast(dskip[:].unsqueeze(2), [P, HS, HP]), ALU.mult)
                ch.step(V.tensor_tensor(yb[:], g.ps[:, 2 * 512:4 * 512].rearrange("p (h c) -> p h c", c=HP),
                                        per_head(g.ecum, n), ALU.mult))
                V.tensor_tensor(yb[:], yb[:], g.ps[:, 6 * 512:8 * 512].rearrange("p (h c) -> p h c", c=HP), ALU.add).then_inc(y_used, 1)
                dve.wait_ge(y_used, n + 1)
                ch.mark(V.tensor_tensor(S[:], S[:], per_head(g.etot, n), ALU.mult))
                ch.step(V.tensor_tensor(yb[:], yb[:], yt[:], ALU.add))
                dve.wait_ge(zgv_in, n * 16 + 16)
                V.tensor_tensor(yb[:].rearrange("p h c -> p (h c)"), yb[:].rearrange("p h c -> p (h c)"), zgv[:, 0, :],
                                ALU.mult).then_inc(y_sum, 1)
                dve.wait_ge(su_ps, n + 1)
                V.tensor_tensor(S[:], S[:], g.ps[:, 4 * 512:6 * 512].rearrange("p (h c) -> p h c", c=HP),
                                ALU.add).then_inc(s_ready, 1)
                dve.wait_ge(att_ps, n + 1)
                ch.step(V.tensor_tensor(att[:], g.bank(2).rearrange("p (h t) -> p h t", h=GH),
                                        bcast(g.blk[:].unsqueeze(1), [P, GH, P]), ALU.mult))
                V.tensor_copy(att[0:HALF, :, HALF:P], g.bank(3, rows=HALF, cols=GH * HALF).rearrange(
                    "p (h t) -> p h t", h=GH)).then_inc(att_ready, 1)
                dve.wait_ge(ry_ready, n + 1)
                for c in range(2):
                    ins = stt(out=out.cat[:, c * 512:(c + 1) * 512], in0=yb[:, c * R:(c + 1) * R, :].rearrange(
                        "p h c -> p (h c)"), scalar=ry[:, c:c + 1], in1=ssdn[:, c * 512:(c + 1) * 512],
                        op0=ALU.mult, op1=ALU.mult)
                ch.mark(ins)
                dve.wait_ge(ro_ready, n + 1)
                for h in range(GH):
                    ins = stt(out=out.cat[:, D + h * GV:D + (h + 1) * GV], in0=g.ps[:, 6 * 512 + h * GV:6 * 512 + (h + 1) * GV],
                              scalar=ro[:, h:h + 1], in1=glan[:], op0=ALU.mult, op1=ALU.mult)
                ch.step(ins)
                V.tensor_tensor(out.cat[:, D:2 * D], out.cat[:, D:2 * D], zgv[:, 1, :], ALU.mult).then_inc(out.cat_ready, 1)
                dve.wait_ge(gs_ps, n + 1)
                for h in range(GH):
                    ins = stt(out=head(GS, h), in0=head(GS, h), scalar=ecg[:, h, P - 1:P],
                              in1=g.ps[:, 2 * 512 + h * GV:2 * 512 + (h + 1) * GV], op0=ALU.mult, op1=ALU.add)
                ins.then_inc(gs_ready, 1)
                dve.wait_ge(gs_ready, n + 2)
                ch.join()
                assert ch.n == VSTEPS
                if stage:
                    out.residual(dve, n - 1, stage == 1)

            for n in range(3):
                tile(n, n)
                if n == 0:
                    out.prepare(dve)
            with dve.Fori(3, NT) as n:
                tile(n, 3)
            out.modulate(dve, NT - 2, False)
            out.residual(dve, NT - 1, False)
            out.modulate(dve, NT - 1, False)


def mix_sample(g):
    nc, io = g.nc, g.io
    HC = HS // 2
    QS = float(P) ** -0.5
    with ExitStack() as st:
        sb = lambda n, s: st.enter_context(nc.sbuf_tensor("s_" + n, s, F32))
        sem = lambda n: g.sem("s_" + n)
        out = Output(g, st, "so_", NS)
        xbc, qk, cum, zgv = sb("xbc", [P, NXBC, NS]), sb("qk", [P, NQK, NS]), sb("cum", [P, GH, NS]), sb("zgv", [NS, 3, D])
        S = sb("S", [P, NS, HC, P])
        xr, bc, dtx, da = sb("xr", [NS, D]), sb("bc", [NS, 4 * P]), sb("dtx", [NS, D]), sb("da", [NS, D])
        turned = sb("turned", [P, 2, HC, NS])
        ts, yT = [sb("t0", [P, HC, P]), sb("t1", [P, HC, P])], sb("yT", [P, HC, NS])
        ela, qpad = sb("ela", [P, GH, NS]), sb("qpad", [P, GH, NS, NS])
        dskip, ssdn, glan = sb("dskip", [NS, HS]), sb("ssdn", [NS, D]), sb("glan", [NS, GV])
        y, junk = sb("y", [NS, D]), out.x1[0:NS, :]
        v = [st.enter_context(nc.sbuf_tensor(f"s_v_{part}", [NS, D], F32R)) for part in ("high", "low")]
        sel8 = st.enter_context(nc.sbuf_tensor("s_sel8", [NS, NS, P], F32R))
        ms, r = sb("ms", [NS, 12]), sb("r", [NS, 6])
        b_spread, b_kept = [out.catT[:, 2 * i:2 * i + 2, :] for i in range(2)], sem("b_kept")
        zero, zero_ready = sb("zero", [P, NS]), sem("zero_ready")
        none, none_ready, none_stored = out.h2[0:TILED - ROWS, :], sem("none_ready"), sem("none_stored")
        small_in, xbc_in = sem("small_in"), sem("xbc_in")
        S_in = [sem(f"S_in{b}") for b in range(NS)]
        GS_in = [sem(f"GS_in{b}") for b in range(NS)]
        v_high, v_split = sem("v_high"), sem("v_split")
        s_decayed, g_decayed, s_input = sem("s_decayed"), sem("g_decayed"), sem("s_input")
        rows_ps, rows_kept, pre, turn_ps, turn_kept = (sem("rows_ps"), sem("rows_kept"), sem("pre"), sem("turn_ps"),
                                                       sem("turn_kept"))
        bc_ps, s_new, yT_ps, y_done, yr = sem("bc_ps"), sem("s_new"), sem("yT_ps"), sem("y_done"), sem("yr")
        e_ready, v_ps, g_new, o_ps, o_r = sem("e_ready"), sem("v_ps"), sem("g_new"), sem("o_ps"), sem("o_r")
        vch, ach, s_out, g_out = sem("vch"), sem("ach"), sem("s_out"), sem("g_out")
        block = st.enter_context(nc.Block())

        GS = S[:].rearrange("p b c n -> p b (c n)").rearrange("p b (h v) -> p b h v", h=GH)

        by_group = lambda ap: ap.rearrange("p (g r) n -> p g r n", g=2)

        def c_spread(b):
            return bcast(g.bank(4 + b % 2, cols=2 * P, at=2 * P).rearrange("p (g n) -> p g n", g=2).unsqueeze(2),
                         [P, 2, HC // 2, P])

        @block.sync
        def _(sp):
            sp.dma_start(xbc[:], g.xbc_d[:, :, SEQ:ROWS].rearrange("c p t -> p c t")).then_inc(xbc_in, 16)
            sp.dma_start(qk[:], g.qk_d[:, :, SEQ:ROWS].rearrange("c p t -> p c t")).then_inc(small_in, 16)
            sp.dma_start(cum[:], g.cum_d[:, :, SEQ:ROWS].rearrange("c p t -> p c t")).then_inc(small_in, 16)
            sp.dma_start(zgv[:], g.proj_d[SEQ:ROWS, :, :]).then_inc(small_in, 16)
            sp.dma_start(dskip[:], io["d_skip"].partition_broadcast(NS)).then_inc(small_in, 16)
            sp.dma_start(ssdn[:], io["ssd_norm"].partition_broadcast(NS)).then_inc(small_in, 16)
            sp.dma_start(glan[:], io["gla_norm"].partition_broadcast(NS)).then_inc(small_in, 16)
            sp.dma_start(out.x[0:NS, :], io["x_sample"]).then_inc(out.x_in, 16)
            for b in range(NS):
                sp.dma_start(S[:, b], io["state_ssm"][:, b]).then_inc(S_in[b], 16)
            out.load_constants(sp)
            for b in range(NS):
                sp.wait_ge(s_new, b + 1)
                sp.dma_start(io["ssm_s"][:, b], S[:, b]).then_inc(s_out, 16)
                sp.wait_ge(s_out, 16 * (b + 1))
                sp.dma_start(GS[:, b], io["state_gla"][:, b]).then_inc(GS_in[b], 16)
            out.load_weights(sp)
            for b in range(NS):
                sp.wait_ge(g_new, b + 1)
                sp.dma_start(io["gla_s"][:, b], GS[:, b]).then_inc(g_out, 16)
            out.store(sp, 0, SEQ)
            sp.wait_ge(g_out, 16 * NS)
            sp.wait_ge(out.x1_stored, 16)
            sp.wait_ge(out.h2_stored, 16)

        @block.gpsimd
        def _(pool):
            nc.gpsimd.memset(zero[:], 0.0).then_inc(zero_ready, 1)
            nc.gpsimd.memset(none, 0.0).then_inc(none_ready, 1)
            pool.wait_ge(none_ready, 1)
            pool.dma_start(g.h2_d[ROWS:TILED, :], none).then_inc(none_stored, 16)
            T = nc.gpsimd.tensor_tensor
            pool.wait_ge(turn_kept, 1)
            for b in range(NS):
                pool.wait_ge(S_in[b], 16)
                T(S[:, b], S[:, b], bcast(turned[:, 1, :, b:b + 1], [P, HC, P]), ALU.mult).then_inc(s_decayed, 1)
                pool.wait_ge(b_kept, b + 1)
                if b >= 2:
                    pool.wait_ge(s_new, b - 1)
                T(by_group(ts[b % 2][:]), bcast(b_spread[b % 2].unsqueeze(2), [P, 2, HC // 2, P]), by_group(bcast(turned[:, 0, :, b:b + 1], [P, HC, P])),
                  ALU.mult).then_inc(s_input, 1)
            pool.wait_ge(e_ready, 1)
            for b in range(NS):
                pool.wait_ge(GS_in[b], 16)
                T(GS[:, b], GS[:, b], bcast(ela[:, :, b:b + 1], [P, GH, GV]), ALU.mult).then_inc(g_decayed, 1)
            pool.wait_ge(none_stored, 16)

        @block.tensor
        def _(pe):
            mm, tr = nc.tensor.matmul, nc.tensor.transpose
            pe.wait_ge(xbc_in, 16)
            for c in range(NXBC):
                last = tr(g.ps[0:NS, c * P:(c + 1) * P], xbc[:, c, :], g.ident[:])
            last.then_inc(rows_ps, 1)
            pe.wait_ge(pre, 2)
            for n, src in enumerate((dtx, da)):
                for c in range(HC):
                    last = tr(g.bank(3, cols=NS, at=(n * HC + c) * NS), src[:, c * P:(c + 1) * P], g.ident[0:NS, 0:NS])
            last.then_inc(turn_ps, 1)
            for b in range(NS):
                if b >= 2:
                    pe.wait_ge(s_new, b - 1)
                mm(g.bank(4 + b % 2), g.sel8[:, b, :], bc[:], start=True, stop=True).then_inc(bc_ps, 1)
            pe.wait_ge(s_new, NS)
            for c in range(HC):
                last = tr(g.ps[0:NS, c * P:(c + 1) * P], yT[:, c, :], g.ident[:])
            last.then_inc(yT_ps, 1)
            pe.wait_ge(zero_ready, 1)
            for n in (2, 3):
                mm(g.bank(n, rows=NS), zero[:], bcast(g.ones[:].unsqueeze(1), [P, 4, P]), start=True, stop=False)

            def spread_v(b):
                if b >= 2:
                    pe.wait_ge(g_new, b - 1)
                for half in range(2):
                    for part in range(2):
                        last = mm(g.bank(4 + 2 * (b % 2) + half), sel8[:, b, :],
                                  v[part][:, half * 512:(half + 1) * 512], start=(part == 0), stop=(part == 1))
                last.then_inc(v_ps, 1)

            pe.wait_ge(v_split, 1)
            spread_v(0)
            for b in range(NS):
                if b + 1 < NS:
                    spread_v(b + 1)
                pe.wait_ge(g_new, b + 1)
                for h in range(GH):
                    last = mm(g.ps[0:NS, 2 * 512 + h * GV:2 * 512 + (h + 1) * GV], qpad[:, h, b, :], GS[:, b, h, :],
                              start=False, stop=(b == NS - 1 and h % 2 == 1))
            last.then_inc(o_ps, 1)
            out.turn(pe, 0)
            out.product(pe, 0, range(0, 2 * KD), True)

        @block.scalar
        def _(act):
            A = nc.scalar.activation
            ch = Chain(act, ach)
            act.wait_ge(rows_ps, 1)
            A(xr[:], g.ps[0:NS, 0:D], ACT.Copy)
            A(bc[:], g.bank(2, rows=NS), ACT.Copy).then_inc(rows_kept, 1)
            act.wait_ge(turn_ps, 1)
            A(turned[:].rearrange("p a c b -> p (a c b)"), g.bank(3, cols=2 * HC * NS), ACT.Copy).then_inc(turn_kept, 1)
            act.wait_ge(small_in, 96)
            A(ela[:], cum[:], ACT.Exp).then_inc(e_ready, 1)
            for b in range(NS):
                act.wait_ge(bc_ps, b + 1)
                if b >= 2:
                    act.wait_ge(s_input, b - 1)
                A(b_spread[b % 2].rearrange("p g n -> p (g n)"), g.bank(4 + b % 2, cols=2 * P),
                  ACT.Copy).then_inc(b_kept, 1)
            act.wait_ge(y_done, 1)
            for c in range(2):
                ins = A(junk[:, c * 512:(c + 1) * 512], y[:, c * 512:(c + 1) * 512], ACT.Square, accum_out=ms[:, c:c + 1])
            ch.step(ins)
            ch.step(A(ms[:, 2:4], ms[:, 0:2], ACT.Ln, scale=2.0 / D, bias=g.eps[0:NS, :]))
            A(r[:, 0:2], ms[:, 2:4], ACT.Exp, scale=-0.5).then_inc(yr, 1)
            act.wait_ge(o_ps, 1)
            for h in range(GH):
                ins = A(junk[:, h * GV:(h + 1) * GV], g.ps[0:NS, 2 * 512 + h * GV:2 * 512 + (h + 1) * GV], ACT.Square,
                        accum_out=ms[:, 4 + h:5 + h])
            ch.step(ins)
            ch.step(A(ms[:, 8:12], ms[:, 4:8], ACT.Ln, scale=1.0 / GV, bias=g.eps[0:NS, :]))
            A(r[:, 2:6], ms[:, 8:12], ACT.Exp, scale=-0.5).then_inc(o_r, 1)
            out.keep_turned(act, 0)
            out.norm2(act, 0)

        @block.vector
        def _(dve):
            V, stt = nc.vector, nc.vector.scalar_tensor_tensor
            ch = Chain(dve, vch)
            heads = lambda ap: ap.rearrange("p (h c) -> p h c", c=HP)
            per_head = lambda ap: bcast(ap.unsqueeze(2), [NS, HS, HP])
            V.tensor_copy(heads(da[:]), per_head(g.edta[:])).then_inc(pre, 1)
            dve.wait_ge(rows_kept, 1)
            V.tensor_tensor(heads(dtx[:]), heads(xr[:]), per_head(g.dt[0:NS, NT, :]), ALU.mult).then_inc(pre, 1)
            dve.wait_ge(small_in, 96)
            split_high(nc, v[0][:], zgv[:, 2, :]).then_inc(v_high, 1)
            V.tensor_copy(sel8[:], g.sel8[:]).then_inc(v_high, 1)
            dve.wait_ge(v_high, 2)
            split_low(nc, v[1][:], v[0][:], zgv[:, 2, :]).then_inc(v_split, 1)
            dve.wait_ge(turn_kept, 1)
            for b in range(NS):
                s_b = S[:, b]
                t = ts[b % 2]
                dve.wait_ge(s_decayed, b + 1)
                dve.wait_ge(s_input, b + 1)
                ch.step(V.tensor_tensor(s_b, s_b, t[:], ALU.add))
                ch.step(V.tensor_tensor(by_group(t[:]), by_group(s_b), c_spread(b), ALU.mult))
                V.tensor_reduce(yT[:, :, b:b + 1].squeeze(2), t[:], AXX, ALU.add).then_inc(s_new, 1)
                dve.wait_ge(s_new, b + 1)
            dve.wait_ge(small_in, 96)
            dve.wait_ge(yT_ps, 1)
            ch.step(V.tensor_tensor(heads(xr[:]), heads(xr[:]), per_head(dskip[:]), ALU.mult))
            ch.step(V.tensor_tensor(y[:], g.ps[0:NS, 0:D], xr[:], ALU.add))
            V.tensor_tensor(y[:], y[:], zgv[:, 0, :], ALU.mult).then_inc(y_done, 1)
            ch.step(V.tensor_scalar(qk[:, 0:GH, :], qk[:, 0:GH, :], QS, None, ALU.mult))
            ch.mark(V.tensor_tensor(qpad[:], bcast(qk[:, 0:GH, :].unsqueeze(3), [P, GH, NS, NS]),
                                    bcast(g.eye8[:].unsqueeze(1), [P, GH, NS, NS]), ALU.mult))
            tv = ts[0][:].rearrange("p c n -> p (c n)").rearrange("p (h v) -> p h v", h=GH)
            for b in range(NS):
                gs_b = GS[:, b]
                dve.wait_ge(v_ps, b + 1)
                ch.step(V.tensor_tensor(tv, g.ps[:, (4 + 2 * (b % 2)) * 512:(6 + 2 * (b % 2)) * 512].rearrange("p (h v) -> p h v", h=GH),
                                        bcast(qk[:, GH:NQK, b:b + 1], [P, GH, GV]), ALU.mult))
                dve.wait_ge(g_decayed, b + 1)
                V.tensor_tensor(gs_b, gs_b, tv, ALU.add).then_inc(g_new, 1)
                dve.wait_ge(g_new, b + 1)
            out.prepare(dve)
            dve.wait_ge(yr, 1)
            for c in range(2):
                cols = slice(c * 512, (c + 1) * 512)
                stt(out=out.cat[0:NS, cols], in0=y[:, cols], scalar=r[:, c:c + 1], in1=ssdn[:, cols],
                    op0=ALU.mult, op1=ALU.mult)
            dve.wait_ge(o_r, 1)
            for h in range(GH):
                ins = stt(out=out.cat[0:NS, D + h * GV:D + (h + 1) * GV],
                          in0=g.ps[0:NS, 2 * 512 + h * GV:2 * 512 + (h + 1) * GV], scalar=r[:, 2 + h:3 + h],
                          in1=glan[:], op0=ALU.mult, op1=ALU.mult)
            ch.step(ins)
            V.tensor_tensor(out.cat[0:NS, D:2 * D], out.cat[0:NS, D:2 * D], zgv[:, 1, :], ALU.mult).then_inc(out.cat_ready, 1)
            out.residual(dve, 0, True)
            dve.wait_ge(none_stored, 16)
            out.modulate(dve, 0, True)



class Router:

    VSTEPS = 52

    def __init__(self, g, st):
        nc = g.nc
        self.g = g
        sb = lambda n, s, dt=F32: st.enter_context(nc.sbuf_tensor("r_" + n, s, dt))
        sem = lambda n: g.sem("r_" + n)
        self.wq, self.keys = sb("wq", [P, 4, KD, 512]), sb("keys", [P, 2 * PH, P])
        self.h2 = sb("h2", [P, D])
        self.h2T, self.qT = sb("h2T", [P, KD, P]), sb("qT", [P, 2 * PH, P])
        self.work = sb("work", [P, 2 * PH, P])
        self.v, self.iu, self.inum = (sb("v", [P, 2 * PH, TOPK]), sb("iu", [P, 2 * PH, TOPK], U32),
                                      sb("inum", [P, 2 * PH, TOPK]))
        self.top, self.pos = sb("top", [P, PH, TOPK]), sb("pos", [P, PH, TOPK], U32)
        self.part = sb("part", [P, 2, PH, TOPK], U32)
        self.row = sb("row", [P, 2, PH, TOPK])
        self.total, self.e = sb("total", [P, PH]), sb("e", [P, PH, TOPK])
        self.gate, self.num = sb("gate", [P, SLOTS]), sb("num", [P, SLOTS])
        self.idx = sb("idx", [P, SLOTS], U32)
        self.wq_in, self.keys_in, self.h2_in = [sem(f"wq_in{b}") for b in range(4)], sem("keys_in"), sem("h2_in")
        self.h2T_ps, self.h2T_kept, self.q_ps, self.q_kept = sem("h2T_ps"), sem("h2T_kept"), sem("q_ps"), sem("q_kept")
        self.s_ps, self.s_kept, self.vch = sem("s_ps"), sem("s_kept"), sem("vch")
        self.shifted, self.e_ready, self.chosen, self.numbered, self.gated = (
            sem("shifted"), sem("e_ready"), sem("chosen"), sem("numbered"), sem("gated"))

    def load_constants(self, sp):
        for b in range(4):
            sp.dma_start(self.wq[:, b], self.g.io["w_query"][b]).then_inc(self.wq_in[b], 16)
            if b == 0:
                sp.dma_start(self.keys[:], self.g.io["sub_keys"]).then_inc(self.keys_in, 16)

    def tensor(self, pe, n):
        g, nc = self.g, self.g.nc
        pe.wait_ge(self.h2_in, n * 16 + 16)
        for k in range(KD):
            last = nc.tensor.transpose(g.ps[:, 2 * 512 + k * P:2 * 512 + (k + 1) * P], self.h2[:, k * P:(k + 1) * P],
                                       g.ident[:])
        last.then_inc(self.h2T_ps, 1)
        yield
        pe.wait_ge(self.h2T_kept, n + 1)

        def scores(b):
            pe.wait_ge(self.keys_in, 16)
            pe.wait_ge(self.q_kept, n * 4 + b + 1)
            for m in range(4):
                u = b * 4 + m
                last = nc.tensor.matmul(g.bank(4 + b, cols=P, at=m * P), self.qT[:, u, :],
                                        self.keys[:, u, :], start=True, stop=True)
            last.then_inc(self.s_ps, 1)

        for b in range(4):
            pe.wait_ge(self.wq_in[b], 16)
            for m in range(4):
                for k in range(KD):
                    last = nc.tensor.matmul(g.bank(4 + b, cols=P, at=m * P), self.wq[:, b, k, m * P:(m + 1) * P],
                                            self.h2T[:, k, :], start=(k == 0), stop=(k == KD - 1))
                if m == 3:
                    last.then_inc(self.q_ps, 1)
                if m % 2:
                    yield
            if b:
                scores(b - 1)
                yield
        scores(3)
        yield

    def scalar(self, act, n):
        g, A = self.g, self.g.nc.scalar.activation
        act.wait_ge(self.h2T_ps, n + 1)
        A(self.h2T[:].rearrange("p k r -> p (k r)"), g.ps[:, 2 * 512:4 * 512], ACT.Copy).then_inc(self.h2T_kept, 1)
        yield

        def scores(b):
            act.wait_ge(self.s_ps, n * 4 + b + 1)
            A(self.work[:, b * 4:(b + 1) * 4, :].rearrange("p k r -> p (k r)"), g.bank(4 + b),
              ACT.Copy).then_inc(self.s_kept, 1)

        for b in range(4):
            act.wait_ge(self.q_ps, n * 4 + b + 1)
            A(self.qT[:, b * 4:(b + 1) * 4, :].rearrange("p k r -> p (k r)"), g.bank(4 + b), ACT.Copy).then_inc(self.q_kept, 1)
            yield
            if b:
                scores(b - 1)
                yield
        scores(3)
        yield
        for half in range(2):
            hs = slice(half * (PH // 2), (half + 1) * (PH // 2))
            act.wait_ge(self.shifted, n * 2 + half + 1)
            A(self.e[:, hs], self.e[:, hs], ACT.Exp).then_inc(self.e_ready, 1)
            yield

    def top16(self, ch, vals, idxs, src, us):
        V = self.g.nc.vector
        for first in (0, 8):
            for u in us:
                last = V.max(vals[:, u, first:first + 8], src(u))
            ch.step_apart(last)
            yield
            for u in us:
                last = V.max_index(idxs[:, u, first:first + 8], vals[:, u, first:first + 8], src(u))
            ch.step_apart(last)
            yield
            if first == 0:
                for u in us:
                    last = V.match_replace(src(u), vals[:, u, 0:8], src(u), LOWEST)
                ch.step_apart(last)
                yield

    def vector(self, dve, n):
        V = self.g.nc.vector
        ch = Chain(dve, self.vch, n * self.VSTEPS)
        sides = self.v[:].rearrange("p (h s) k -> p h s k", s=2)
        numbers = self.inum[:].rearrange("p (h s) k -> p h s k", s=2)
        cand = self.work[:].rearrange("p (h s) k -> p h (s k)", s=2)
        H = PH // 2
        pair = [P, H, TOPK, TOPK]
        for half in range(2):
            for b in (2 * half, 2 * half + 1):
                wait_apart(dve, self.s_kept, n * 4 + b + 1)
                yield from self.top16(ch, self.v, self.iu, lambda u: self.work[:, u, :], range(b * 4, b * 4 + 4))
            hs, us = slice(half * H, half * H + H), slice(half * PH, half * PH + PH)
            ch.mark(V.tensor_copy(self.inum[:, us, :], self.iu[:, us, :]))
            square = cand[:, hs, :].rearrange("p h (a b) -> p h a b", b=TOPK)
            ch.step_apart(V.tensor_tensor(square, bcast(sides[:, hs, 0, :].unsqueeze(3), pair),
                                          bcast(sides[:, hs, 1, :].unsqueeze(2), pair), ALU.add))
            yield
            yield from self.top16(ch, self.top, self.pos, lambda h: cand[:, h, :], range(hs.start, hs.stop))
            ch.mark(V.tensor_single_scalar(self.part[:, 0, hs], self.pos[:, hs], 4, ALU.logical_shift_right))
            ch.step(V.tensor_single_scalar(self.part[:, 1, hs], self.pos[:, hs], TOPK - 1, ALU.bitwise_and))
            yield
            for side in range(2):
                hit = square
                ch.step(V.tensor_tensor(hit, bcast(self.g.iota16[:].unsqueeze(1).unsqueeze(1), pair),
                                        bcast(self.part[:, side, hs].unsqueeze(3), pair), ALU.is_equal))
                yield
                ch.step(V.tensor_tensor(hit, hit, bcast(numbers[:, hs, side, :].unsqueeze(2), pair), ALU.mult))
                summed = V.tensor_reduce(self.row[:, side, hs], hit, AXX, ALU.add)
                if side == 0:
                    ch.step(summed)
                    yield
            summed.then_inc(self.chosen, 1)
            dve.wait_ge(self.chosen, n * 4 + 2 * half + 1)
            ks = slice(half * (SLOTS // 2), (half + 1) * (SLOTS // 2))
            V.scalar_tensor_tensor(out=self.num[:, ks], in0=self.row[:, 0, hs].rearrange("p h k -> p (h k)"),
                                   scalar=float(P), in1=self.row[:, 1, hs].rearrange("p h k -> p (h k)"),
                                   op0=ALU.mult, op1=ALU.add).then_inc(self.chosen, 1)
            dve.wait_ge(self.chosen, n * 4 + 2 * half + 2)
            V.tensor_copy(self.idx[:, ks], self.num[:, ks]).then_inc(self.numbered, 1)
            yield
            V.tensor_tensor(self.e[:, hs], self.top[:, hs], bcast(self.top[:, hs, 0:1], [P, H, TOPK]),
                            ALU.subtract).then_inc(self.shifted, 1)
            yield
            dve.wait_ge(self.e_ready, n * 2 + half + 1)
            ch.step(V.tensor_reduce(self.total[:, hs], self.e[:, hs], AXX, ALU.add))
            ch.step(V.reciprocal(self.total[:, hs], self.total[:, hs]))
            V.tensor_tensor(self.gate[:, ks].rearrange("p (h k) -> p h k", k=TOPK), self.e[:, hs],
                            bcast(self.total[:, hs].unsqueeze(2), [P, H, TOPK]), ALU.mult).then_inc(self.gated, 1)
            yield
        assert ch.n == self.VSTEPS, ch.n


class Finish:

    def __init__(self, g, st):
        self.g = g
        sb = lambda n, s: st.enter_context(g.nc.sbuf_tensor("f_" + n, s, F32))
        sem = lambda n: g.sem("f_" + n)
        self.x1, self.gate2, self.final, self.y = sb("x1", [P, D]), sb("gate2", [P, D]), sb("final", [P, D]), sb("y", [P, D])
        self.ms, self.r = sb("ms", [P, 2]), sb("r", [P, 1])
        self.consts_in, self.x1_in, self.ach = sem("consts_in"), sem("x1_in"), sem("ach")
        self.sum_read, self.x2_ready, self.r_ready, self.y_ready = (sem("sum_read"), sem("x2_ready"), sem("r_ready"),
                                                                    sem("y_ready"))
        self.stored = sem("stored")

    def add(self, dve, n, rs):
        g, V = self.g, self.g.nc.vector
        dve.wait_ge(self.x1_in, n * 16 + 16)
        dve.wait_ge(self.stored, n * 16 + 16)
        V.tensor_tensor(self.y[0:rs, :], g.ps[0:rs, 0:D], self.gate2[0:rs, :], ALU.mult).then_inc(self.sum_read, 1)
        dve.wait_ge(self.sum_read, n + 1)
        V.tensor_tensor(self.x1[0:rs, :], self.y[0:rs, :], self.x1[0:rs, :], ALU.add).then_inc(self.x2_ready, 1)

    def scale(self, dve, n, rs):
        dve.wait_ge(self.r_ready, n + 1)
        self.g.nc.vector.scalar_tensor_tensor(out=self.y[0:rs, :], in0=self.x1[0:rs, :], scalar=self.r[0:rs, :],
                                              in1=self.final[0:rs, :], op0=ALU.mult, op1=ALU.mult).then_inc(self.y_ready, 1)

    def scalar(self, act, n, rs):
        g, A = self.g, self.g.nc.scalar.activation
        act.wait_ge(self.x2_ready, n + 1)
        ch = Chain(act, self.ach, n * 2)
        ch.step(A(self.y[0:rs, :], self.x1[0:rs, :], ACT.Square, accum_out=self.ms[0:rs, 0:1]))
        ch.step(A(self.ms[0:rs, 1:2], self.ms[0:rs, 0:1], ACT.Ln, scale=1.0 / D, bias=g.eps[0:rs, :]))
        A(self.r[0:rs, :], self.ms[0:rs, 1:2], ACT.Exp, scale=-0.5).then_inc(self.r_ready, 1)
        act.wait_ge(self.r_ready, n + 1)


PE_PIECES = {q: 1 for q in range(1, 14)}
ACT_PIECES = {q: 1 for q in (2, 4, 6, 7, 9, 10, 12, 13, 14, 18, 26)}
DVE_PIECES = {8: 2, 9: 3, 11: 2, 12: 3, 13: 2, 14: 2, 15: 2, 16: 2, 17: 4, 19: 4, 20: 4, 21: 3, 22: 3, 23: 3,
              24: 3, 25: 3, 27: 1}
FIRST_ACT_PIECES = {6: 1}
FIRST_DVE_PIECES = {0: 4, 1: 4, 2: 4, 3: 4, 4: 3, 5: 3, 7: 1}


def drive(pieces, count):
    for _ in range(count):
        next(pieces, None)


def experts(g):
    nc, io = g.nc, g.io
    NG = SLOTS // GROUP
    with ExitStack() as st:
        sb = lambda n, s, dt=F32: st.enter_context(nc.sbuf_tensor("e_" + n, s, dt))
        sem = lambda n: g.sem("e_" + n)
        rt, fin = Router(g, st), Finish(g, st)
        buf = [sb(f"buf{s}", [P, 2 * D]) for s in range(RING)]
        idx, gate, h2 = sb("idx", [P, SLOTS], U32), sb("gate", [P, SLOTS]), sb("h2", [P, D])
        dots, acts, wts = sb("dots", [P, SLOTS]), sb("acts", [P, SLOTS]), sb("wts", [P, SLOTS])
        diag = sb("diag", [P, RING, P])
        h2_kept, idx_kept, generated = sem("h2_kept"), sem("idx_kept"), sem("generated")
        landed = [sem(f"landed{s}") for s in range(RING)]
        dotted, wch, weighed, summed = sem("dotted"), sem("wch"), sem("weighed"), sem("summed")
        idxT, turned = sb("idxT", [P, NS], U32), sb("turned", [P, 2, NS])
        wpad = sb("wpad", [P, NS, NS])
        turn_ps, turn_kept, idxT_ready, spread_in, gates_in = (sem("turn_ps"), sem("turn_kept"), sem("idxT_ready"),
                                                               sem("spread_in"), sem("gates_in"))
        s_dotted, s_acted, s_weighed, s_summed = sem("s_dotted"), sem("s_acted"), sem("s_weighed"), sem("s_summed")
        wide = rt.wq[:].rearrange("p n k c -> p (n k c)")
        spread = lambda b: wide[:, b * D:(b + 1) * D]
        block = st.enter_context(nc.Block())
        HALF_SLOTS = SLOTS // 2
        PER = 16 * (SLOTS // RING)

        @block.sync
        def _(sp):
            sp.sem_inc(fin.stored, 16)
            sp.dma_start(rt.h2[:], g.h2_d[0:P, :]).then_inc(rt.h2_in, 16)
            rt.load_constants(sp)
            sp.dma_start(fin.gate2[:], g.mod_d[NS, 5 * D:6 * D].partition_broadcast(P)).then_inc(fin.consts_in, 16)
            sp.dma_start(fin.final[:], io["norm_final"].partition_broadcast(P)).then_inc(fin.consts_in, 16)

            def store_y(n):
                sp.wait_ge(fin.y_ready, n + 1)
                sp.dma_start(io["y_p"][bass.ds(n * P, P), :], fin.y[:]).then_inc(fin.stored, 16)

            def tile(n, first):
                sp.wait_ge(h2_kept, n + 1)
                sp.dma_start(rt.h2[:], g.h2_d[bass.ds(n * P + P, P), :]).then_inc(rt.h2_in, 16)
                if not first:
                    store_y(n - 1)
                sp.dma_start(fin.x1[:], g.x1_d[bass.ds(n * P, P), :]).then_inc(fin.x1_in, 16)

            tile(0, True)
            with sp.Fori(1, NT) as n:
                tile(n, False)
            sp.wait_ge(rt.q_ps, 4 * (NT + 1))
            for b in range(NS):
                sp.dma_start(spread(b), g.h2_d[SEQ + b, :].partition_broadcast(P)).then_inc(spread_in, 16)
            sp.wait_ge(fin.sum_read, NT)
            sp.dma_start(fin.gate2[0:NS, :], g.mod_d[0:NS, 5 * D:6 * D]).then_inc(gates_in, 16)
            store_y(NT - 1)
            sp.dma_start(fin.x1[0:NS, :], g.x1_d[SEQ:ROWS, :]).then_inc(fin.x1_in, 16)
            sp.wait_ge(fin.y_ready, NT + 1)
            sp.dma_start(io["y_s"], fin.y[0:NS, :]).then_inc(fin.stored, 16)
            sp.wait_ge(fin.stored, 16 * (NT + 2))

        @block.gpsimd
        def _(pool):
            def gather(s, numbers, **kw):
                return pool.indirect_dma_start(out=buf[s][:], out_offset=None, in_=io["experts"],
                                               in_offset=bass.IndirectOffsetOnAxis(ap=numbers, axis=0), **kw)

            def tile(n):
                for k in range(SLOTS):
                    wait_apart(pool, summed, n * SLOTS + k + 1)
                    if k in (0, HALF_SLOTS - RING):
                        half = 0 if k == 0 else 1
                        ks = slice(half * HALF_SLOTS, (half + 1) * HALF_SLOTS)
                        wait_apart(pool, rt.numbered, n * 2 + half + 1)
                        nc.gpsimd.tensor_copy(idx[:, ks], rt.idx[:, ks]).then_inc(idx_kept, 1)
                        wait_apart(pool, idx_kept, n * 2 + half + 1)
                    gather(k % RING, idx[:, k:k + 1]).then_inc(landed[k % RING], 16)

            with pool.Fori(0, NT) as n:
                tile(n)
            pool.wait_ge(idxT_ready, 1)
            for b in range(NS):
                wait_apart(pool, summed, NT * SLOTS + b + 1)
                gather(b % RING, idxT[:, b:b + 1]).then_inc(landed[b % RING], 16)

        @block.tensor
        def _(pe):
            pe.sem_inc(summed, RING)
            drive(rt.tensor(pe, 0), 99)
            def tile(n, first):
                route = rt.tensor(pe, n + 1)
                for k in range(SLOTS):
                    if k == 0 and not first:
                        pe.wait_ge(fin.sum_read, n)
                    pe.wait_ge(weighed, n * SLOTS + k + 1)
                    for cols in range(2):
                        last = nc.tensor.matmul(g.bank(cols), diag[:, k % RING, :],
                                                buf[k % RING][:, D + cols * 512:D + (cols + 1) * 512],
                                                start=(k == 0), stop=(k == SLOTS - 1))
                    last.then_inc(summed, 1)
                    if k % GROUP == GROUP - 1:
                        drive(route, PE_PIECES.get(k // GROUP, 0))

            tile(0, True)
            with pe.Fori(1, NT) as n:
                tile(n, False)
            pe.wait_ge(rt.gated, 2 * (NT + 1))
            for m, src in enumerate((rt.num, rt.gate)):
                last = nc.tensor.transpose(g.bank(2, cols=NS, at=m * NS), src[0:NS, :], g.ident[0:NS, 0:NS])
            last.then_inc(turn_ps, 1)
            pe.wait_ge(fin.sum_read, NT)
            for b in range(NS):
                pe.wait_ge(s_weighed, b + 1)
                for cols in range(2):
                    last = nc.tensor.matmul(g.bank(cols, rows=NS), wpad[:, b, :],
                                            buf[b % RING][:, D + cols * 512:D + (cols + 1) * 512],
                                            start=(b == 0), stop=(b == NS - 1))
                last.then_inc(s_summed, 1)

        @block.scalar
        def _(act):
            A = nc.scalar.activation
            own = rt.scalar(act, 0)
            drive(own, 10)
            def tile(n, first):
                ch = Chain(act, wch, n * (2 + 2 * NG))
                route = rt.scalar(act, n + 1)
                for q in range(NG):
                    if q in (0, NG // 2):
                        half = 0 if q == 0 else 1
                        gs = slice(half * HALF_SLOTS, (half + 1) * HALF_SLOTS)
                        act.wait_ge(rt.gated, n * 2 + half + 1)
                        ch.step(A(gate[:, gs], rt.gate[:, gs], ACT.Copy))
                    ks = slice(q * GROUP, (q + 1) * GROUP)
                    act.wait_ge(dotted, n * SLOTS + (q + 1) * GROUP)
                    ch.step(A(acts[:, ks], dots[:, ks], ACT.Gelu))
                    for k in range(q * GROUP, (q + 1) * GROUP):
                        last = A(wts[:, k:k + 1], acts[:, k:k + 1], ACT.Copy, scale=gate[:, k:k + 1])
                    ch.step(last)
                    for k in range(q * GROUP, (q + 1) * GROUP):
                        act.wait_ge(summed, n * SLOTS + k + 1)
                        A(diag[:, k % RING, :], g.ident[:], ACT.Copy, scale=wts[:, k:k + 1]).then_inc(weighed, 1)
                    if first:
                        drive(own, FIRST_ACT_PIECES.get(q, 0))
                    drive(route, ACT_PIECES.get(q, 0))
                    if q == 0 and not first:
                        fin.scalar(act, n - 1, P)

            tile(0, True)
            with act.Fori(1, NT) as n:
                tile(n, False)
            act.wait_ge(turn_ps, 1)
            A(turned[:].rearrange("p a b -> p (a b)"), g.bank(2, cols=2 * NS), ACT.Copy).then_inc(turn_kept, 1)
            fin.scalar(act, NT - 1, P)
            for b in range(NS):
                act.wait_ge(s_dotted, b + 1)
                A(wts[:, b:b + 1], dots[:, b:b + 1], ACT.Gelu).then_inc(s_acted, 1)
            fin.scalar(act, NT, NS)

        @block.vector
        def _(dve):
            V = nc.vector

            def dot(s, row, out, sem):
                down = buf[s][:, 0:D]
                V.scalar_tensor_tensor(out=down, in0=down, scalar=1.0, in1=row, op0=ALU.mult, op1=ALU.mult,
                                       accum_out=out).then_inc(sem, 1)

            own = rt.vector(dve, 0)
            drive(own, 23)
            dve.wait_ge(fin.consts_in, 32)
            def tile(n, first):
                route = rt.vector(dve, n + 1)
                if not first:
                    dve.wait_ge(dotted, n * SLOTS)
                V.tensor_copy(h2[:], rt.h2[:]).then_inc(h2_kept, 1)
                dve.wait_ge(h2_kept, n + 1)
                for k in range(SLOTS):
                    dve.wait_ge(landed[k % RING], n * PER + 16 * (k // RING) + 16)
                    dot(k % RING, h2[:], dots[:, k:k + 1], dotted)
                    if k % GROUP == GROUP - 1:
                        if first:
                            drive(own, FIRST_DVE_PIECES.get(k // GROUP, 0))
                        drive(route, DVE_PIECES.get(k // GROUP, 0))
                    if k == GROUP - 1 and not first:
                        dve.wait_ge(summed, n * SLOTS + RING)
                        fin.add(dve, n - 1, P)
                    if k == 2 * GROUP - 1 and not first:
                        fin.scale(dve, n - 1, P)

            tile(0, True)
            with dve.Fori(1, NT) as n:
                tile(n, False)
            dve.wait_ge(turn_kept, 1)
            V.tensor_copy(idxT[:], turned[:, 0, :]).then_inc(idxT_ready, 1)
            dve.wait_ge(summed, NT * SLOTS + RING)
            fin.add(dve, NT - 1, P)
            fin.scale(dve, NT - 1, P)
            dve.wait_ge(spread_in, 16 * NS)
            dve.wait_ge(gates_in, 16)

            def weigh(b):
                dve.wait_ge(s_acted, b + 1)
                V.scalar_tensor_tensor(out=wpad[:, b, :], in0=g.eye8[:, b, :], scalar=wts[:, b:b + 1],
                                       in1=bcast(turned[:, 1, b:b + 1], [P, NS]), op0=ALU.mult,
                                       op1=ALU.mult).then_inc(s_weighed, 1)

            for b in range(NS):
                dve.wait_ge(landed[b % RING], NT * PER + 16 * (b // RING + 1))
                dot(b % RING, spread(b), dots[:, b:b + 1], s_dotted)
                if b:
                    weigh(b - 1)
            weigh(NS - 1)
            dve.wait_ge(s_summed, NS)
            fin.add(dve, NT, NS)
            fin.scale(dve, NT, NS)


def build(nc, io):
    with ExitStack() as stack:
        g = Prog(nc, stack, io)
        with ExitStack() as st:
            hT = [st.enter_context(nc.sbuf_tensor(f"hT_{part}", [P, KD, ROWS], F32R)) for part in ("high", "low")]
            with ExitStack() as rows:
                x = rows.enter_context(nc.sbuf_tensor("x_rows", [P, NT + 1, D], F32))
                r = rows.enter_context(nc.sbuf_tensor("x_rms", [P, NT + 1], F32))
                g.phase(modulation, x, r)
                g.phase(norm_in, x, r, hT)
            g.phase(projections, hT)
        g.phase(mix_sample)
        g.phase(mix_prompt)
        g.phase(experts)


def laid_out(np, x):
    f = {k: np.asarray(v) for k, v in x.items()}
    chunks = lambda w, n: w.reshape(KD, P, w.shape[1] // n, n).transpose(2, 1, 0, 3)
    wide = lambda w: w.reshape(w.shape[0] // P, P, w.shape[1]).transpose(1, 0, 2)
    w_in = f["w_in"][0]
    cuts = np.cumsum([0, D, NXBC * P, HS, GH * P, GH * P, D, D, 16])
    z, xbc, dt, q, k, v, go, gate = (w_in[:, a:b] for a, b in zip(cuts[:-1], cuts[1:]))
    per_chunk = lambda a: a.reshape(-1, NXBC, P).transpose(1, 2, 0)
    heads = lambda s: s.transpose(3, 0, 1, 2)
    return {
        "c_all": np.concatenate([f["c_sample"], f["c_prompt"]]),
        "w_mod": chunks(f["w_mod"][0], 512), "b_mod": f["b_mod"][0],
        "norm_mix": f["norm_mix"][0], "norm_ffn": f["norm_ffn"][0], "norm_final": f["norm_final"],
        "x_prompt": f["x_prompt"][0], "x_sample": f["x_sample"][:, 0],
        "w_chan": chunks(np.concatenate([xbc, q, k], axis=1), P),
        "w_rows": chunks(np.concatenate([z, go, v], axis=1), 512),
        "w_small": wide(np.concatenate([gate, np.zeros_like(gate), dt], axis=1)),
        "conv_par": np.concatenate([per_chunk(f["w_conv"][0]), per_chunk(f["b_conv"][0]),
                                    per_chunk(f["state_conv"][0].transpose(1, 0, 2))], axis=2),
        "dt_bias": f["dt_bias"][0], "a_log": f["a_log"][0],
        "w_gate_up": f["w_gate_up"][0], "b_gate": f["b_gate"][0].reshape(GH, P).T,
        "state_ssm": f["state_ssm"][0].reshape(NS, HS // 2, P, P).transpose(2, 0, 1, 3),
        "state_gla": f["state_gla"][0].transpose(2, 0, 1, 3),
        "d_skip": f["d_skip"][0], "ssd_norm": f["ssd_norm"][0], "gla_norm": f["gla_norm"][0],
        "w_out": wide(f["w_out"][0]),
        "w_query": chunks(f["w_query"][0], 512),
        "sub_keys": np.stack([f["sub_keys1"][0], f["sub_keys2"][0]], axis=1).reshape(2 * PH, P, P).transpose(2, 0, 1),
        "experts": np.concatenate([f["expert_down"][0], f["expert_up"][0]], axis=1),
    }


OUTS = {"y_p": (SEQ, D), "y_s": (NS, D), "conv_p": (NXBC, P, 3), "ssm_p": (P, HS * HP), "gla_p": (P, GH * GV),
        "conv_s": (NXBC, P, 3 * NS), "ssm_s": (P, NS, HS // 2, P), "gla_s": (P, NS, GH, GV)}


def program(nc, arrays):
    io = {}
    for n, a in arrays.items():
        io[n] = nc.dram_tensor(f"in_{n}", a.shape, mybir.dt.from_np(a.dtype), kind="ExternalInput").ap()
    for n, shape in OUTS.items():
        io[n] = nc.dram_tensor(f"out_{n}", shape, F32, kind="ExternalOutput").ap()
    build(nc, io)


def kernel(**inputs):
    import numpy as np
    import concourse.bacc as bacc
    from concourse.bass_utils import run_bass_kernel_spmd

    nc = bacc.Bacc("TRN2", target_bir_lowering=False, num_devices=1)
    arrays = {n: np.ascontiguousarray(a) for n, a in laid_out(np, inputs).items()}
    program(nc, arrays)
    r = run_bass_kernel_spmd(nc, [{f"in_{n}": a for n, a in arrays.items()}], core_ids=[0]).results[0]
    o = {n: np.asarray(r[f"out_{n}"]) for n in OUTS}
    state = lambda a: a.reshape(NXBC * P, 3, -1).transpose(2, 1, 0)[None]
    return (o["y_p"][None], o["y_s"][:, None], state(o["conv_p"]),
            o["ssm_p"].T.reshape(1, 1, HS, HP, P), o["gla_p"].reshape(P, GH, GV).transpose(1, 0, 2)[None, None],
            state(o["conv_s"]), o["ssm_s"].transpose(1, 2, 0, 3).reshape(1, NS, HS, HP, P),
            o["gla_s"].transpose(1, 2, 0, 3)[None])
```
